# Optimizing a Trainium2 kernel written in Bass

```python
import math
import jax, jax.numpy as jnp
from jax import lax
import numpy as np

D_MODEL = 2048
BATCH = 1
SEQ = 256
DEPTH = 1

D_SSD = 2048
SSD_HEAD_DIM = 64
SSD_HEADS = D_SSD // SSD_HEAD_DIM
SSD_GROUPS = 4
SSD_STATE = 128
CONV_K = 5
CONV_CH = D_SSD + 2 * SSD_GROUPS * SSD_STATE
CHUNK = 128
ATT_HEADS = 16
ATT_HEAD_DIM = 64
ATT_V_DIM = 2 * ATT_HEAD_DIM
Q_COLS = 2 * ATT_HEADS * ATT_HEAD_DIM
V_COLS = ATT_HEADS * ATT_V_DIM
Q_BLOCK = 128
ROPE_THETA = 10000.0
N_BRANCHES = 2
IN_SPLITS = (D_SSD, CONV_CH, 2 * SSD_HEADS, Q_COLS, Q_COLS, V_COLS, N_BRANCHES * D_MODEL)
IN_COLS = sum(IN_SPLITS)
SPLIT_POINTS = [int(s) for s in np.cumsum(IN_SPLITS)[:-1]]
PEER_HEADS = 8
PEER_NKEYS = 128
PEER_EXPERTS = PEER_NKEYS * PEER_NKEYS
PEER_KEY_DIM = 256
PEER_HALF = PEER_KEY_DIM // 2
PEER_TOPK = 16
TOK_BLOCK = 128
PLE_DIM = 256
EPS = 1e-6

kernel_name = 'hybrid_ssd_diffattn_peer_block'

def rms_norm(x, g):
    xf = x.astype(jnp.float32)
    y = xf * lax.rsqrt(jnp.mean(xf * xf, axis=-1, keepdims=True) + EPS)
    return (y * g.astype(jnp.float32)).astype(x.dtype)

def rope(t, pos):
    d = t.shape[-1]
    inv = ROPE_THETA ** (-jnp.arange(0, d, 2, dtype=jnp.float32) / d)
    ang = pos.astype(jnp.float32)[..., None] * inv
    cos = jnp.cos(ang)[:, :, None, :]
    sin = jnp.sin(ang)[:, :, None, :]
    tf = t.astype(jnp.float32)
    t1, t2 = tf[..., : d // 2], tf[..., d // 2:]
    return jnp.concatenate([t1 * cos - t2 * sin, t2 * cos + t1 * sin], axis=-1).astype(t.dtype)

def centred_depthwise_conv(u, w, b):
    y = lax.conv_general_dilated(
        u, w[:, None, :].astype(u.dtype), window_strides=(1,),
        padding=[(CONV_K // 2, CONV_K // 2)],
        dimension_numbers=('NWC', 'WIO', 'NWC'),
        feature_group_count=u.shape[-1])
    return y + b.astype(u.dtype)

def ssd_scan(x, dt, A, Bm, Cm):
    b, S, H, P = x.shape
    G, N = Bm.shape[-2], Bm.shape[-1]
    R = H // G
    nc = S // CHUNK
    a = (dt * A).reshape(b, nc, CHUNK, G, R)
    xdt = (x.astype(jnp.float32) * dt[..., None]).reshape(b, nc, CHUNK, G, R, P)
    Bc = Bm.astype(jnp.float32).reshape(b, nc, CHUNK, G, N)
    Cc = Cm.astype(jnp.float32).reshape(b, nc, CHUNK, G, N)
    a_cs = jnp.cumsum(a, axis=2)
    seg = a_cs[:, :, :, None] - a_cs[:, :, None]
    tri = jnp.tril(jnp.ones((CHUNK, CHUNK), dtype=bool))[:, :, None, None]
    Lm = jnp.exp(jnp.where(tri, seg, -jnp.inf))
    cb = jnp.einsum('bclgn,bcsgn->bclsg', Cc, Bc)
    y_diag = jnp.einsum('bclsgr,bcsgrp->bclgrp', Lm * cb[..., None], xdt)
    decay_in = jnp.exp(a_cs[:, :, -1:] - a_cs)
    states = jnp.einsum('bclgn,bclgrp->bcgrpn', Bc, xdt * decay_in[..., None])
    chunk_decay = jnp.exp(a_cs[:, :, -1])

    def step(h, inp):
        st, dec = inp
        return h * dec[..., None, None] + st, h

    h0 = jnp.zeros((b, G, R, P, N), jnp.float32)
    _, h_in = lax.scan(step, h0, (jnp.moveaxis(states, 1, 0), jnp.moveaxis(chunk_decay, 1, 0)))
    h_in = jnp.moveaxis(h_in, 0, 1)
    y_off = jnp.einsum('bclgn,bcgrpn->bclgrp', Cc, h_in) * jnp.exp(a_cs)[..., None]
    return (y_diag + y_off).reshape(b, S, H, P)

def diff_attention(q, k, v, lam):
    b, S, H2, d = q.shape
    H = H2 // 2
    nb = S // Q_BLOCK
    scale = d ** -0.5
    qb = jnp.moveaxis(q.reshape(b, nb, Q_BLOCK, H2, d), 1, 0)

    def block(qi):
        s = jnp.einsum('bqhd,bkhd->bhqk', qi, k).astype(jnp.float32) * scale
        pr = jax.nn.softmax(s, axis=-1).reshape(b, H, 2, Q_BLOCK, S)
        att = pr[:, :, 0] - lam * pr[:, :, 1]
        return jnp.einsum('bhqk,bkhe->bqhe', att.astype(v.dtype), v)

    o = lax.map(block, qb)
    return jnp.moveaxis(o, 0, 1).reshape(b, S, H, v.shape[-1])

def peer(h, wq, keys, u, v):
    b, S, D = h.shape
    T = b * S
    ht = h.reshape(T, D)
    q = (ht @ wq.astype(ht.dtype)).reshape(T, PEER_HEADS, 2, PEER_HALF)
    s = jnp.einsum('thid,hind->thin', q, keys.astype(q.dtype)).astype(jnp.float32)
    v_top, i_top = lax.top_k(s, PEER_TOPK)
    cand = (v_top[:, :, 0, :, None] + v_top[:, :, 1, None, :]).reshape(T, PEER_HEADS, PEER_TOPK * PEER_TOPK)
    cidx = (i_top[:, :, 0, :, None] * PEER_NKEYS + i_top[:, :, 1, None, :]).reshape(T, PEER_HEADS, PEER_TOPK * PEER_TOPK)
    sc, pos = lax.top_k(cand, PEER_TOPK)
    eidx = jnp.take_along_axis(cidx, pos, axis=-1)
    gate = jax.nn.softmax(sc, axis=-1)
    nb = T // TOK_BLOCK

    def block(args):
        hb, ib, gb = args
        ub = jnp.take(u, ib, axis=0).astype(hb.dtype)
        a = jnp.einsum('td,thkd->thk', hb, ub).astype(jnp.float32)
        w = jax.nn.gelu(a, approximate=False) * gb
        vb = jnp.take(v, ib, axis=0).astype(hb.dtype)
        return jnp.einsum('thk,thkd->td', w.astype(hb.dtype), vb)

    out = lax.map(block, (ht.reshape(nb, TOK_BLOCK, D),
                          eidx.reshape(nb, TOK_BLOCK, PEER_HEADS, PEER_TOPK),
                          gate.reshape(nb, TOK_BLOCK, PEER_HEADS, PEER_TOPK)))
    return out.reshape(b, S, D)

def _normal(k, shape, scale):
    return jax.random.normal(k, shape, jnp.float32) * scale

def setup_inputs(seed: int = 0) -> dict:
    key = jax.random.key(seed)
    k = jax.random.split(key, 32)
    L = DEPTH
    x = _normal(k[0], (BATCH, SEQ, D_MODEL), 1.0)
    p = _normal(k[1], (DEPTH, BATCH, SEQ, PLE_DIM), 1.0)
    positions = jnp.broadcast_to(jnp.arange(SEQ, dtype=jnp.int32), (BATCH, SEQ))
    norm1_g = 1.0 + _normal(k[2], (L, D_MODEL), 0.02)
    w_in = _normal(k[3], (L, D_MODEL, IN_COLS), D_MODEL ** -0.5)
    conv_w = _normal(k[4], (L, CONV_K, CONV_CH), CONV_K ** -0.5)
    conv_b = _normal(k[5], (L, CONV_CH), 0.02)
    a_log_f = jnp.log(jax.random.uniform(k[6], (L, SSD_HEADS), jnp.float32, 1.0, 16.0))
    a_log_b = jnp.log(jax.random.uniform(k[7], (L, SSD_HEADS), jnp.float32, 1.0, 16.0))
    dt0_f = jnp.exp(jax.random.uniform(k[8], (L, SSD_HEADS), jnp.float32, math.log(1e-3), math.log(1e-1)))
    dt0_b = jnp.exp(jax.random.uniform(k[9], (L, SSD_HEADS), jnp.float32, math.log(1e-3), math.log(1e-1)))
    dt_bias_f = dt0_f + jnp.log(-jnp.expm1(-dt0_f))
    dt_bias_b = dt0_b + jnp.log(-jnp.expm1(-dt0_b))
    d_skip = 1.0 + _normal(k[10], (L, SSD_HEADS), 0.02)
    ssd_norm_g = 1.0 + _normal(k[11], (L, D_SSD), 0.02)
    q_norm_g = 1.0 + _normal(k[12], (L, ATT_HEAD_DIM), 0.02)
    k_norm_g = 1.0 + _normal(k[13], (L, ATT_HEAD_DIM), 0.02)
    lam_q1 = _normal(k[14], (L, ATT_HEAD_DIM), 0.1)
    lam_k1 = _normal(k[15], (L, ATT_HEAD_DIM), 0.1)
    lam_q2 = _normal(k[16], (L, ATT_HEAD_DIM), 0.1)
    lam_k2 = _normal(k[17], (L, ATT_HEAD_DIM), 0.1)
    subln_g = 1.0 + _normal(k[18], (L, ATT_V_DIM), 0.02)
    w_ssd_br = _normal(k[19], (L, D_SSD, D_MODEL), D_SSD ** -0.5)
    w_att_br = _normal(k[20], (L, V_COLS, D_MODEL), V_COLS ** -0.5)
    w_out = _normal(k[21], (L, D_MODEL, D_MODEL), D_MODEL ** -0.5)
    norm2_g = 1.0 + _normal(k[22], (L, D_MODEL), 0.02)
    peer_wq = _normal(k[23], (L, D_MODEL, PEER_HEADS * PEER_KEY_DIM), D_MODEL ** -0.5)
    peer_keys = _normal(k[24], (L, PEER_HEADS, 2, PEER_NKEYS, PEER_HALF), PEER_HALF ** -0.5)
    peer_u = _normal(k[25], (L, PEER_EXPERTS, D_MODEL), D_MODEL ** -0.5)
    peer_v = _normal(k[26], (L, PEER_EXPERTS, D_MODEL), PEER_HEADS ** -0.5)
    norm3_g = 1.0 + _normal(k[27], (L, D_MODEL), 0.02)
    ple_gate_w = _normal(k[28], (L, D_MODEL, D_MODEL), D_MODEL ** -0.5)
    ple_up_w = _normal(k[29], (L, PLE_DIM, D_MODEL), PLE_DIM ** -0.5)
    return {'x': x, 'p': p, 'positions': positions, 'norm1_g': norm1_g, 'w_in': w_in,
            'conv_w': conv_w, 'conv_b': conv_b, 'a_log_f': a_log_f, 'a_log_b': a_log_b,
            'dt_bias_f': dt_bias_f, 'dt_bias_b': dt_bias_b, 'd_skip': d_skip,
            'ssd_norm_g': ssd_norm_g, 'q_norm_g': q_norm_g, 'k_norm_g': k_norm_g,
            'lam_q1': lam_q1, 'lam_k1': lam_k1, 'lam_q2': lam_q2, 'lam_k2': lam_k2,
            'subln_g': subln_g, 'w_ssd_br': w_ssd_br, 'w_att_br': w_att_br, 'w_out': w_out,
            'norm2_g': norm2_g, 'peer_wq': peer_wq, 'peer_keys': peer_keys, 'peer_u': peer_u,
            'peer_v': peer_v, 'norm3_g': norm3_g, 'ple_gate_w': ple_gate_w, 'ple_up_w': ple_up_w}

def reference(x, p, positions, norm1_g, w_in, conv_w, conv_b, a_log_f, a_log_b,
              dt_bias_f, dt_bias_b, d_skip, ssd_norm_g, q_norm_g, k_norm_g,
              lam_q1, lam_k1, lam_q2, lam_k2, subln_g, w_ssd_br, w_att_br, w_out,
              norm2_g, peer_wq, peer_keys, peer_u, peer_v, norm3_g, ple_gate_w, ple_up_w):
    f32 = jnp.float32
    b, S, _ = x.shape

    def flip(t):
        return jnp.flip(t, axis=1)

    for i in range(DEPTH):
        h = rms_norm(x, norm1_g[i])
        proj = h @ w_in[i].astype(h.dtype)
        z, xbc, dt_raw, q, k, v, gates = jnp.split(proj, SPLIT_POINTS, axis=-1)

        xbc = jax.nn.silu(centred_depthwise_conv(xbc, conv_w[i], conv_b[i]))
        xs, bm, cm = jnp.split(xbc, [D_SSD, D_SSD + SSD_GROUPS * SSD_STATE], axis=-1)
        xs = xs.reshape(b, S, SSD_HEADS, SSD_HEAD_DIM)
        bm = bm.reshape(b, S, SSD_GROUPS, SSD_STATE)
        cm = cm.reshape(b, S, SSD_GROUPS, SSD_STATE)
        dt_raw = dt_raw.astype(f32)
        dt_f = jax.nn.softplus(dt_raw[..., :SSD_HEADS] + dt_bias_f[i].astype(f32))
        dt_b = jax.nn.softplus(dt_raw[..., SSD_HEADS:] + dt_bias_b[i].astype(f32))
        y_f = ssd_scan(xs, dt_f, -jnp.exp(a_log_f[i].astype(f32)), bm, cm)
        y_b = flip(ssd_scan(flip(xs), flip(dt_b), -jnp.exp(a_log_b[i].astype(f32)), flip(bm), flip(cm)))
        y_ssd = y_f + y_b + d_skip[i].astype(f32)[:, None] * xs.astype(f32)
        y_ssd = y_ssd.reshape(b, S, D_SSD) * jax.nn.silu(z.astype(f32))
        y_ssd = rms_norm(y_ssd.astype(x.dtype), ssd_norm_g[i])

        q = rope(rms_norm(q.reshape(b, S, 2 * ATT_HEADS, ATT_HEAD_DIM), q_norm_g[i]), positions)
        k = rope(rms_norm(k.reshape(b, S, 2 * ATT_HEADS, ATT_HEAD_DIM), k_norm_g[i]), positions)
        v = v.reshape(b, S, ATT_HEADS, ATT_V_DIM)
        lam_init = 0.8 - 0.6 * math.exp(-0.3 * i)
        lam = (jnp.exp(jnp.sum(lam_q1[i].astype(f32) * lam_k1[i].astype(f32)))
               - jnp.exp(jnp.sum(lam_q2[i].astype(f32) * lam_k2[i].astype(f32))) + lam_init)
        o = diff_attention(q, k, v, lam)
        o = rms_norm(o, subln_g[i]) * (1.0 - lam_init)
        y_att = o.reshape(b, S, V_COLS)

        g_ssd, g_att = jnp.split(jax.nn.sigmoid(gates.astype(f32)), N_BRANCHES, axis=-1)
        mixed = (g_ssd * (y_ssd @ w_ssd_br[i].astype(y_ssd.dtype)).astype(f32)
                 + g_att * (y_att @ w_att_br[i].astype(y_att.dtype)).astype(f32))
        x = x + (mixed.astype(x.dtype) @ w_out[i].astype(x.dtype))

        x = x + peer(rms_norm(x, norm2_g[i]), peer_wq[i], peer_keys[i], peer_u[i], peer_v[i])

        ple_gate = jax.nn.sigmoid((rms_norm(x, norm3_g[i]) @ ple_gate_w[i].astype(x.dtype)).astype(f32))
        ple = (p[i] @ ple_up_w[i].astype(p.dtype)).astype(f32)
        x = x + (ple_gate * ple).astype(x.dtype)
    return x


_drawn_inputs = setup_inputs


def setup_inputs(seed=0):
    import zlib

    import numpy as np

    out = dict(_drawn_inputs(seed))
    spreads = {}
    factors = {'d_skip': 13.908,
     'ssd_norm_g': 10.05,
     'q_norm_g': 4.189,
     'k_norm_g': 3.7,
     'lam_q1': 6.051,
     'subln_g': 12.711,
     'norm2_g': 7.695,
     'norm3_g': 64.0}
    for name, (base, spread) in spreads.items():
        noise = np.random.default_rng([zlib.crc32(name.encode()), seed]).standard_normal(out[name].shape)
        drawn = base * np.exp(spread * noise) if base else spread * noise
        out[name] = __import__('jax').numpy.asarray(drawn.astype(out[name].dtype))
    for name, factor in factors.items():
        out[name] = (out[name] * factor).astype(out[name].dtype)
    return out
```

```python
from contextlib import ExitStack, contextmanager

import concourse.bass as bass
import numpy as np
from concourse import mybir

F32 = mybir.dt.float32
F32R = mybir.dt.float32r
I32 = mybir.dt.int32
U32 = mybir.dt.uint32
ALU = mybir.AluOpType
ACT = mybir.ActivationFunctionType
AX = mybir.AxisListType

P = 128
D = 2048
TT = 2
S = TT * P
KC = D // P
SSD_HEADS, SSD_DIM, GROUPS, STATE = 32, 64, 4, 128
HPG = SSD_HEADS // GROUPS
CONV_K = 5
XBC = (D + 2 * GROUPS * STATE) // P
ATT_HEADS, ATT_DIM = 16, 64
EXPERT_HEADS, NKEYS, TOPK = 8, 128, 16
PICKS = EXPERT_HEADS * TOPK
PLE = 256
EPS = 1e-6
LAM_INIT = 0.2
SCALE = ATT_DIM ** -0.5
LOWEST = -3.0e38
SLOTS = 8

NB = 512
HALF = 2 * NB
RAW, SPLIT = 4, 4
AHEAD = 2
STAGES = [("xbc", 6), ("z", 4), ("q", 4), ("k", 4), ("v", 4), ("gates", 8),
          ("ssd_out", 4), ("att_out", 4), ("w_out", 4), ("peer_q", 4), ("ple_gate", 4)]
FIRST = {}
_n = 0
for _name, _k in STAGES:
    FIRST[_name] = _n
    _n += _k
BLOCKS = _n
HALVES = 8 * BLOCKS
BLOCKS_OF = dict(STAGES)

G1, GS, G3, GA, CW, CB = 0, 16, 32, 48, 49, 49 + XBC * CONV_K
COLS = CB + XBC
R_DTB, R_ALOG, R_DSKIP, R_QG, R_KG, R_LAM, R_INV = 0, 64, 128, 160, 224, 288, 544
ROWS = 576


class Steps:

    def __init__(self, eng, sem):
        self.eng, self.sem, self.n = eng, sem, 0

    def mark(self, ins):
        ins.then_inc(self.sem, 1)
        self.n = self.n + 1

    def wait(self):
        self.eng.wait_ge(self.sem, self.n)


@contextmanager
def looped(eng, times, *counts):
    start = [s.n for s, _ in counts]
    with eng.Fori(0, times) as i:
        for (s, per), n in zip(counts, start):
            s.n = n + i * per
        yield i
    for (s, per), n in zip(counts, start):
        s.n = n + times * per


def build(nc, x, wall, wdt, cols, rows, pos, g2, keys_t, peer_u, peer_v, p_t, ple_up, out):
    ctx = ExitStack()
    with ctx:
        def sb(name, shape, dt=F32):
            return ctx.enter_context(nc.sbuf_tensor(name, shape, dt))

        def sem(name):
            return ctx.enter_context(nc.semaphore(name))

        act_hi = sb("act_hi", [P, KC, S], F32R)
        act_lo = sb("act_lo", [P, KC, S], F32R)
        w_hi = sb("w_hi", [P, SPLIT, HALF], F32R)
        w_lo = sb("w_lo", [P, SPLIT, HALF], F32R)
        w_raw = sb("w_raw", [P, RAW, 2 * HALF])
        work = sb("work", [P, 12 * D])
        ident = sb("ident", [P, P])
        upper = sb("upper", [P, P])
        lower = sb("lower", [P, P])
        below = sb("below", [P, P])
        above = sb("above", [P, P])
        colc = sb("colc", [P, COLS])
        rowc = sb("rowc", [P, ROWS])
        pos_i = sb("pos_i", [P, TT], I32)
        stat = sb("stat", [P, 8])
        small = sb("small", [P, 1664])

        def carve(*shapes):
            at, views = 0, []
            for shape in shapes:
                n = int(np.prod(shape))
                v = small[:, at:at + n]
                if len(shape) > 1:
                    names = "abcd"[:len(shape)]
                    v = v.rearrange("p (" + " ".join(names) + ") -> p " + " ".join(names),
                                    **dict(zip(names, shape)))
                views.append(v)
                at += n
            return views

        dtv, av, aexp, dtt, ex, dd, cbm = carve(
            (TT, 64), (TT, 64), (64,), (5, TT * 64), (4, SSD_HEADS), (TT, SSD_HEADS), (2, 2, P))
        trig, posf, ang, hstat, lamp, lam, mx, nmx, rs, ri = carve(
            (2, TT, 2, ATT_DIM), (TT,), (5, TT, 32), (4, ATT_HEADS), (2, ATT_DIM), (4,),
            (2, 4), (2, 4), (2, 4), (2, 4))
        v16, i16, i16f, sc16, ps16, psf, ef, esum = carve(
            (KC, TOPK), (KC, TOPK), (KC, TOPK), (EXPERT_HEADS, TOPK), (EXPERT_HEADS, TOPK), (2, PICKS),
            (2, PICKS), (2, EXPERT_HEADS))
        i16, ps16 = i16.bitcast(U32), ps16.bitcast(U32)
        iota_i = sb("iota_i", [P, TOPK], I32)
        iota_f = sb("iota_f", [P, TOPK])
        picks = sb("picks", [P, TT, PICKS], I32)
        gate = sb("gate", [P, TT, PICKS])
        dots = sb("dots", [P, TT, PICKS])
        staged = sb("staged", [P, 2 * SLOTS], I32)

        PS = ctx.enter_context(nc.psum_tensor("PS", [P, 8 * NB], F32))

        def blk(first, n=1):
            return work[:, first * D:(first + n) * D]

        def bank(b, n=1):
            return PS[:, b * NB:(b + n) * NB]

        def tiles(v):
            return v.rearrange("p (t d) -> p t d", t=TT)

        small_in = sem("small_in")
        x_in = sem("x_in")
        masks = sem("masks")
        raw_in = [sem(f"raw_in{k}") for k in range(RAW)]
        hi_split = sem("hi_split")
        lo_split = sem("lo_split")
        half_free = sem("half_free")
        banks_free = sem("banks_free")
        own_act = sem("own_act")
        own_dve = sem("own_dve")
        own_pool = sem("own_pool")
        squares = sem("squares")
        means = sem("means")
        roots = sem("roots")
        rows_ready = sem("rows_ready")
        turned = sem("turned")
        turned_hi = sem("turned_hi")
        turned_lo = sem("turned_lo")
        dt_sum = sem("dt_sum")
        dt_abs = sem("dt_abs")
        dt_exp = sem("dt_exp")
        pad_free = sem("pad_free")
        conved = sem("conved")
        silued = sem("silued")
        xt_turned = sem("xt_turned")
        xt_out = sem("xt_out")
        a_ready = sem("a_ready")
        dec_sum = sem("dec_sum")
        dec_exp = sem("dec_exp")
        decayed = sem("decayed")
        xd_ready = sem("xd_ready")
        state_sum = sem("state_sum")
        state_out = sem("state_out")
        rh_ready = sem("rh_ready")
        seg_sum = sem("seg_sum")
        seg_exp = sem("seg_exp")
        cb_sum = sem("cb_sum")
        em_ready = sem("em_ready")
        skip_ready = sem("skip_ready")
        y_sum = sem("y_sum")
        y_done = sem("y_done")
        head_sq = sem("head_sq")
        head_ms = sem("head_ms")
        head_rt = sem("head_rt")
        angles = sem("angles")
        sines = sem("sines")
        lam_sum = sem("lam_sum")
        lam_exp = sem("lam_exp")
        roped = sem("roped")
        qk_turned = sem("qk_turned")
        qk_out = sem("qk_out")
        scored = sem("scored")
        maxed = sem("maxed")
        expd = sem("expd")
        att_ready = sem("att_ready")
        att_turned = sem("att_turned")
        att_out = sem("att_out")
        o_sum = sem("o_sum")
        o_done = sem("o_done")
        x_again = sem("x_again")
        g2_in = sem("g2_in")
        keys_in = sem("keys_in")
        key_sum = sem("key_sum")
        key_out = sem("key_out")
        top_sub = sem("top_sub")
        top_exp = sem("top_exp")
        picked = sem("picked")
        indices_staged = sem("indices_staged")
        gathers_due = sem("gathers_due")
        row_in = [sem(f"row_in{k}") for k in range(SLOTS)]
        row_free = sem("row_free")
        gelued = sem("gelued")
        ple_in = sem("ple_in")
        ple_sum = sem("ple_sum")
        ple_out = sem("ple_out")
        out_ready = sem("out_ready")
        stored = sem("stored")

        x_sb = tiles(blk(0, 2))
        wdt_sb = blk(11)[:, 0:KC * 64].rearrange("p (c n) -> p c n", c=KC)
        xbc = blk(2, 3).rearrange("p (c s) -> p c s", c=XBC)
        pad = blk(8, 2)[:, 0:8 * (S + 4)].rearrange("p (m s) -> p m s", m=8)
        conv = blk(10).rearrange("p (m s) -> p m s", m=8)
        z_sb = tiles(blk(6, 2))
        xt = tiles(blk(0, 2))
        bt = tiles(blk(5)[:, 0:TT * NB])
        hs = tiles(blk(5)[:, TT * NB:2 * TT * NB])
        rh = blk(2, 2).rearrange("p (b r h l) -> p b r h l", b=2, r=2, h=HPG)
        em = blk(8, 2).rearrange("p (b r h l) -> p b r h l", b=2, r=2, h=HPG)
        xf = blk(10).rearrange("p (b r d) -> p b r d", b=2, r=2)
        xd = tiles(blk(11)[:, 0:2 * NB])
        xsk = blk(11)[:, 2 * NB:3 * NB]
        ytmp = blk(11)[:, 3 * NB:4 * NB]
        q_sb, k_sb, v_sb = (tiles(blk(n, 2)) for n in (0, 2, 4))
        sq = blk(8)[:, 0:NB]
        rot = blk(9)[:, 0:2 * NB].rearrange("p (k d) -> p k d", k=2)
        qkt = blk(8)[:, 0:2 * NB].rearrange("p (b s) -> p b s", b=2)
        att = blk(8)[:, 2 * NB:4 * NB].rearrange("p (b t s) -> p b t s", b=2, t=TT)
        prob = blk(9).rearrange("p (b j s) -> p b j s", b=2, j=4)
        att_t = blk(10)[:, 0:2 * NB].rearrange("p (b s) -> p b s", b=2)
        att_x = tiles(blk(10)[:, 2 * NB:3 * NB])
        o_sq = blk(11)
        gates = tiles(blk(2, 4))
        mixed = tiles(blk(8, 2))
        mtmp = tiles(blk(0)[:, 0:2 * NB])
        x1 = tiles(blk(10, 2))
        h2 = tiles(blk(8, 2))
        g2_sb = blk(0)
        keys_sb = blk(1).rearrange("p (n k) -> p n k", n=KC)
        pq = blk(2, 2).rearrange("p (n s) -> p n s", n=KC)
        cand = blk(5).rearrange("p (h c) -> p h c", h=EXPERT_HEADS)
        onehot = blk(6).rearrange("p (k c) -> p k c", c=TOPK)
        slot = blk(0, SLOTS).rearrange("p (n d) -> p n d", n=SLOTS)
        h3 = tiles(blk(8, 2))
        pt_sb = blk(3)[:, 0:2 * S].rearrange("p (c s) -> p c s", c=2)
        up_sb = blk(1, 2).rearrange("p (c n) -> p c n", c=2)
        ple_sb = tiles(blk(4, 2))
        gsig = blk(6).rearrange("p (b t n) -> p b t n", b=2, t=TT)

        JUNK = [10, 8, 4, 0]

        def key_scores(t):
            return blk((4, 7)[t]).rearrange("p (n k) -> p n k", n=KC)

        def head_src(n):
            src, b, t = (q_sb, k_sb)[n // 8], (n % 8) // 2, n % 2
            return src[:, t, b * NB:(b + 1) * NB]

        block = ctx.enter_context(nc.Block())

        @block.sync
        def _(sp):
            for t in range(TT):
                sp.dma_start(x_sb[:, t, :], x[t]).then_inc(x_in, 16)
            for u in range(RAW):
                sp.dma_start(w_raw[:, u, :], wall[u]).then_inc(raw_in[u], 16)
            with sp.Fori(1, BLOCKS) as b:
                for u in range(RAW):
                    sp.wait_ge(lo_split, 8 * b - 8 + 2 * u + 2)
                    sp.dma_start(w_raw[:, u, :], wall[bass.ds(4 * b + u, 1)]
                                 .rearrange("o p n -> (o p) n")).then_inc(raw_in[u], 16)
            with sp.Fori(0, D // NB) as b:
                sp.wait_ge(out_ready, b + 1)
                sp.dma_start(out[:, :, bass.ds(b * NB, NB)].rearrange("t p n -> p t n"),
                             x1[:, :, bass.ds(b * NB, NB)]).then_inc(stored, 16)
            sp.wait_ge(stored, 16 * (D // NB))

        @block.gpsimd
        def _(pool):
            own = Steps(pool, own_pool)
            for m in (upper, lower, below, above):
                own.mark(pool.memset(m[:, :], 1.0))
            own.mark(pool.memset(ident[:, :], 0.0))
            own.wait()
            for m, op, sign in ((upper, ALU.is_ge, -1), (lower, ALU.is_ge, 1),
                                (below, ALU.is_gt, 1), (above, ALU.is_gt, -1)):
                pool.affine_select(out=m[:, :], in_=m[:, :], compare_op=op, fill=0.0, base=0,
                                   pattern=[[-sign, P]], channel_multiplier=sign).then_inc(masks, 1)
            pool.affine_select(out=ident[:, :], in_=ident[:, :], compare_op=ALU.not_equal, fill=1.0,
                               base=0, pattern=[[-1, P]], channel_multiplier=1).then_inc(masks, 1)
            pool.iota(iota_i[:, :], pattern=[[1, TOPK]], base=0, channel_multiplier=0).then_inc(masks, 1)

            pool.wait_ge(masks, 6)
            pool.wait_ge(small_in, 64)
            pool.wait_ge(xt_out, 10)
            pool.wait_ge(decayed, 1)

            def heads(v):
                return v.rearrange("p (h d) -> p h d", h=HPG)

            def per_head(v, n):
                return v.unsqueeze(2).to_broadcast([P, HPG, n])

            for g in range(GROUPS):
                if g:
                    pool.wait_ge(state_sum, g)
                for t in range(TT):
                    pool.tensor_tensor(heads(xd[:, t, :]), heads(xt[:, t, g * NB:(g + 1) * NB]),
                                       per_head(dd[:, t, g * HPG:(g + 1) * HPG], SSD_DIM),
                                       ALU.mult).then_inc(xd_ready, 1)
                for c in range(TT):
                    n = TT * g + c
                    if n >= 2:
                        pool.wait_ge(seg_sum, n - 1)
                    for r, m in ((0, upper), (1, lower)):
                        a_h = av[:, c, 32 * r + g * HPG:32 * r + (g + 1) * HPG]
                        pool.tensor_tensor(rh[:, n % 2, r], m[:, :].unsqueeze(1).to_broadcast([P, HPG, P]),
                                           per_head(a_h, P), ALU.mult).then_inc(rh_ready, 1)
                    if n:
                        pool.wait_ge(y_done, n)
                    pool.tensor_tensor(heads(xsk), heads(xt[:, c, g * NB:(g + 1) * NB]),
                                       per_head(rowc[:, R_DSKIP + g * HPG:R_DSKIP + (g + 1) * HPG], SSD_DIM),
                                       ALU.mult).then_inc(skip_ready, 1)

            pool.wait_ge(rows_ready, 3)
            for t in range(TT):
                pool.dma_start(x1[:, t, :], x[t]).then_inc(x_again, 16)
            pool.wait_ge(rows_ready, 4)
            pool.dma_start(g2_sb, g2[0:1, :].to_broadcast([P, D])).then_inc(g2_in, 16)
            pool.dma_start(blk(1), keys_t).then_inc(keys_in, 16)

            pool.wait_ge(picked, TT)
            done = 0
            for t in range(TT):
                for table in (peer_u, peer_v):
                    with pool.Fori(0, PICKS // (2 * SLOTS)) as i:
                        for half in range(2):
                            first = done + half * SLOTS + 2 * SLOTS * i
                            pool.wait_ge(row_free, first + 1)
                            pool.tensor_copy(staged[:, half * SLOTS:(half + 1) * SLOTS],
                                             picks[:, t, bass.ds(i * 2 * SLOTS + half * SLOTS, SLOTS)])\
                                .then_inc(indices_staged, 1)
                            pool.wait_ge(indices_staged, done // SLOTS + 2 * i + half + 1)
                            for s in range(SLOTS):
                                pool.wait_ge(row_free, first + s + 1)
                                pool.sem_inc(gathers_due, 1)
                                k = half * SLOTS + s
                                pool.indirect_dma_start(
                                    slot[:, s, :], None, table[:, :],
                                    bass.IndirectOffsetOnAxis(ap=staged[:, k:k + 1], axis=0),
                                ).then_inc(row_in[s], 16)
                    done += PICKS
            pool.wait_ge(row_free, 4 * PICKS + SLOTS)
            pool.dma_start(blk(1, 2), ple_up).then_inc(ple_in, 16)
            pool.dma_start(blk(3)[:, 0:2 * S], p_t).then_inc(ple_in, 16)

        @block.scalar
        def _(act):
            act.sem_inc(half_free, SPLIT)
            act.sem_inc(banks_free, 4)
            act.dma_start(colc[:, :], cols).then_inc(small_in, 16)
            act.dma_start(rowc[:, :], rows[0:1, :].to_broadcast([P, ROWS])).then_inc(small_in, 16)
            act.dma_start(pos_i[:, :], pos).then_inc(small_in, 16)
            act.dma_start(blk(11)[:, 0:KC * 64], wdt).then_inc(small_in, 16)

            def hi(n, first, block_no):
                act.wait_ge(raw_in[(n // 2) % RAW], 16 * block_no + 16 * (n // 8 + 1))
                act.wait_ge(half_free, first + n + 1)
                act.activation(w_hi[:, n % SPLIT, :],
                               w_raw[:, (n // 2) % RAW, (n % 2) * HALF:(n % 2 + 1) * HALF],
                               ACT.Copy).then_inc(hi_split, 1)

            def stage(name, after):
                with act.Fori(0, BLOCKS_OF[name] // 2) as i:
                    for b in range(2):
                        block_no = FIRST[name] + b + 2 * i
                        for j in range(8):
                            hi(AHEAD + j, 8 * block_no, block_no)
                        act.wait_ge(half_free, 8 * block_no + 8 + SPLIT)
                        after(b + 2 * i, b)

            def stage_with(name, during, straight_after=None):
                last = name == STAGES[-1][0]
                for b in range(BLOCKS_OF[name]):
                    block_no = FIRST[name] + b
                    for j in range(8):
                        if 8 * block_no + AHEAD + j < HALVES:
                            hi(AHEAD + j, 8 * block_no, block_no)
                        during(b, j)
                    if straight_after:
                        act.wait_ge(half_free, 8 * block_no + 8 + SPLIT)
                        straight_after(b, b % 2)

            def squares_of(k, src):
                for t in range(TT):
                    ins = act.activation(blk(JUNK[k]), src[:, t, :], ACT.Square,
                                         accum_out=stat[:, t:t + 1])
                    if t == 0:
                        ins.then_inc(own_act, 1)
                        act.wait_ge(own_act, k + 1)
                    else:
                        ins.then_inc(squares, 1)
                act.wait_ge(means, k + 1)
                act.activation(stat[:, 4:6], stat[:, 2:4], ACT.Sqrt).then_inc(roots, 1)

            def turn(k, gain=None):
                for m in range(8):
                    act.wait_ge(turned, 8 * k + m + 1)
                    for c in range(2):
                        ins = act.activation(act_hi[:, 2 * m + c, :],
                                             bank(4 + m % 4)[:, c * S:(c + 1) * S], ACT.Copy,
                                             scale=gain(2 * m + c) if gain else 1.0)
                    ins.then_inc(turned_hi, 1)

            def col(base):
                return lambda c: colc[:, base + c:base + c + 1]

            for n in range(AHEAD):
                hi(n, 0, 0)
            act.wait_ge(x_in, 32)
            squares_of(0, x_sb)
            act.wait_ge(small_in, 64)
            turn(0, col(G1))

            def xbc_rows(b):
                act.wait_ge(half_free, 8 * b + 8 + SPLIT)
                act.wait_ge(pad_free, b + 1)
                for m in range(2):
                    act.activation(pad[:, 4 * (b % 2) + 2 * m:4 * (b % 2) + 2 * m + 2, 2:2 + S],
                                   bank(2 * (b % 2) + m).rearrange("p (m s) -> p m s", m=2),
                                   ACT.Copy).then_inc(banks_free, 1)

            def xbc_silu(b):
                act.wait_ge(conved, b + 1)
                act.activation(xbc[:, 4 * b:4 * b + 4, :], conv[:, 4 * (b % 2):4 * (b % 2) + 4, :],
                               ACT.Silu).then_inc(silued, 1)

            def xbc_during(b, j):
                if b and j == 2:
                    xbc_rows(b - 1)
                if b and j == 7:
                    xbc_silu(b - 1)

            stage_with("xbc", xbc_during)
            xbc_rows(5)

            def z_after(b, parity):
                for t in range(TT):
                    act.activation(z_sb[:, t, bass.ds(b * NB, NB)], bank(2 * parity + t), ACT.Silu)\
                        .then_inc(banks_free, 1)

            stage("z", z_after)
            xbc_silu(5)

            act.wait_ge(dt_abs, 1)
            act.activation(dtt[:, 1, :], dtt[:, 1, :], ACT.Exp, scale=-1.0).then_inc(dt_exp, 1)
            act.activation(aexp[:, :], rowc[:, R_ALOG:R_ALOG + 64], ACT.Exp).then_inc(dt_exp, 1)
            for m in range(10):
                act.wait_ge(xt_turned, m + 1)
                t, q = m % 2, m // 2
                act.activation(xt[:, t, q * NB:(q + 1) * NB] if q < 4 else bt[:, t, :],
                               bank(4 + m % 4), ACT.Copy).then_inc(xt_out, 1)
            act.wait_ge(dec_sum, 1)
            act.activation(ex[:, :, :], bank(0)[:, 0:4 * SSD_HEADS].rearrange("p (k h) -> p k h", k=4),
                           ACT.Exp).then_inc(dec_exp, 1)
            for g in range(GROUPS):
                for c in range(TT):
                    n = TT * g + c
                    act.wait_ge(seg_sum, n + 1)
                    if n >= 2:
                        act.wait_ge(y_sum, n - 1)
                    for r in range(2):
                        for q in range(2):
                            ins = act.activation(em[:, n % 2, r, 4 * q:4 * q + 4, :],
                                                 bank(4 + 2 * r + q).rearrange("p (h l) -> p h l", h=4),
                                                 ACT.Exp)
                    ins.then_inc(seg_exp, 1)
                    if c == 0:
                        act.wait_ge(state_sum, g + 1)
                        if g:
                            act.wait_ge(y_sum, 2 * g)
                        act.activation(hs[:, :, :], tiles(bank(2, 2)), ACT.Copy).then_inc(state_out, 1)
            act.wait_ge(y_done, 8)
            squares_of(1, z_sb)

            def copy_out(dst):
                def f(b, parity):
                    for t in range(TT):
                        act.activation(dst[:, t, bass.ds(b * NB, NB)], bank(2 * parity + t), ACT.Copy)\
                            .then_inc(banks_free, 1)
                return f

            def head_norms(first):
                def f(b, j):
                    n = first + 2 * b + j // 4
                    if j % 4 == 0:
                        if n:
                            act.wait_ge(head_ms, n)
                        act.activation(sq, head_src(n), ACT.Square).then_inc(head_sq, 1)
                    if j % 4 == 2:
                        act.wait_ge(head_ms, n + 1)
                        act.activation(hstat[:, 2, 0:8], hstat[:, 1, 0:8], ACT.Sqrt).then_inc(head_rt, 1)
                return f

            stage("q", copy_out(q_sb))
            act.wait_ge(angles, 1)
            act.activation(ang[:, 0:2], ang[:, 0:2], ACT.Sin).then_inc(sines, 1)
            act.wait_ge(lam_sum, 1)
            act.activation(lam[:, 0:2], lam[:, 0:2], ACT.Exp).then_inc(lam_exp, 1)
            stage_with("k", head_norms(0), copy_out(k_sb))
            stage_with("v", head_norms(8), copy_out(v_sb))

            for h in range(ATT_HEADS + 1):
                if h < ATT_HEADS:
                    act.wait_ge(qk_turned, h + 1)
                    if h >= 2:
                        act.wait_ge(scored, h - 1)
                    act.activation(qkt[:, h % 2, :], bank(h % 2), ACT.Copy).then_inc(qk_out, 1)
                if h:
                    n = h - 1
                    act.wait_ge(maxed, n + 1)
                    if n >= 2:
                        act.wait_ge(att_ready, n - 1)
                    for k in range(4):
                        j, t = k // 2, k % 2
                        ins = act.activation(prob[:, n % 2, k, :],
                                             bank(2 + 2 * (n % 2) + j)[:, t * S:(t + 1) * S], ACT.Exp,
                                             bias=nmx[:, n % 2, k:k + 1], scale=SCALE,
                                             accum_out=rs[:, n % 2, k:k + 1])
                    ins.then_inc(expd, 1)
            act.wait_ge(o_done, ATT_HEADS)
            for t in range(TT):
                if t:
                    act.wait_ge(head_ms, 17)
                act.activation(o_sq, q_sb[:, t, :], ACT.Square).then_inc(head_sq, 1)
                act.wait_ge(head_ms, 17 + t)
                act.activation(hstat[:, 2, :], hstat[:, 1, :], ACT.Sqrt).then_inc(head_rt, 1)

            def gates_after(b, parity):
                for t in range(TT):
                    act.activation(gates[:, t, bass.ds(b * NB, NB)], bank(2 * parity + t), ACT.Sigmoid)\
                        .then_inc(banks_free, 1)

            def nothing(b, parity):
                pass

            stage("gates", gates_after)
            turn(1, col(GS))
            stage("ssd_out", nothing)
            turn(2, lambda c: colc[:, GA:GA + 1])
            stage("att_out", nothing)
            turn(3)
            stage("w_out", nothing)
            act.wait_ge(banks_free, 4 + 2 * FIRST["peer_q"])
            squares_of(2, x1)
            turn(4)

            def pq_after(b, parity):
                for m in range(2):
                    act.activation(pq[:, bass.ds(4 * b + 2 * m, 2), :],
                                   bank(2 * parity + m).rearrange("p (m s) -> p m s", m=2), ACT.Copy)\
                        .then_inc(banks_free, 1)

            stage("peer_q", pq_after)
            for t in range(TT):
                act.wait_ge(key_sum, t + 1)
                act.activation(key_scores(t), bank(4 * t, 4).rearrange("p (n k) -> p n k", n=KC), ACT.Copy)\
                    .then_inc(key_out, 1)
            for t in range(TT):
                act.wait_ge(top_sub, t + 1)
                act.activation(gate[:, t, :], gate[:, t, :], ACT.Exp).then_inc(top_exp, 1)
            for t in range(TT):
                act.wait_ge(row_free, SLOTS + (2 * t + 1) * PICKS)
                act.activation(dots[:, t, :], dots[:, t, :], ACT.Gelu).then_inc(gelued, 1)

            act.wait_ge(row_free, SLOTS + 4 * PICKS)
            squares_of(3, x1)
            for b in range(D // NB):
                act.wait_ge(ple_sum, b + 1)
                act.activation(ple_sb[:, :, b * NB:(b + 1) * NB], tiles(bank(2 * (b % 2), 2)), ACT.Copy)\
                    .then_inc(ple_out, 1)
            turn(5, col(G3))

            def sig_after(b, parity):
                if b >= 2:
                    act.wait_ge(out_ready, b - 1)
                for t in range(TT):
                    act.activation(gsig[:, parity, t, :], bank(2 * parity + t), ACT.Sigmoid)\
                        .then_inc(banks_free, 1)

            stage_with("ple_gate", lambda b, j: None, sig_after)

        @block.vector
        def _(dve):
            own = Steps(dve, own_dve)
            dve.sem_inc(row_free, SLOTS)

            def lo(n, first):
                dve.wait_ge(hi_split, first + n + 1)
                dve.tensor_tensor(w_lo[:, n % SPLIT, :],
                                  w_raw[:, (n // 2) % RAW, (n % 2) * HALF:(n % 2 + 1) * HALF],
                                  w_hi[:, n % SPLIT, :].bitcast(F32), ALU.subtract).then_inc(lo_split, 1)

            def stage(name, after=None, signals=0):
                with looped(dve, BLOCKS_OF[name] // 2, (own, 2 * signals)) as i:
                    for b in range(2):
                        block_no = FIRST[name] + b + 2 * i
                        for j in range(8):
                            lo(AHEAD + j, 8 * block_no)
                        if after:
                            dve.wait_ge(half_free, 8 * block_no + 8 + SPLIT)
                            after(b + 2 * i, b)

            def stage_with(name, during=None, straight_after=None):
                for b in range(BLOCKS_OF[name]):
                    block_no = FIRST[name] + b
                    for j in range(8):
                        if 8 * block_no + AHEAD + j < HALVES:
                            lo(AHEAD + j, 8 * block_no)
                        if during:
                            during(b, j)
                    if straight_after:
                        straight_after(b, b % 2)

            def norm(k):
                dve.wait_ge(squares, k + 1)
                dve.tensor_scalar(stat[:, 2:4], stat[:, 0:2], 1.0 / D, EPS, ALU.mult, ALU.add)\
                    .then_inc(means, 1)
                dve.wait_ge(roots, k + 1)
                own.mark(dve.reciprocal(stat[:, 6:8], stat[:, 4:6]))
                own.wait()

            def scaled(dst, src):
                for t in range(TT):
                    ins = dve.tensor_scalar(dst[:, t, :], src[:, t, :], stat[:, 6 + t:7 + t], None, ALU.mult)
                ins.then_inc(rows_ready, 1)

            def turn(k, gain=None):
                for m in range(8):
                    dve.wait_ge(turned_hi, 8 * k + m + 1)
                    for c in range(2):
                        ins = dve.scalar_tensor_tensor(
                            out=act_lo[:, 2 * m + c, :], in0=bank(4 + m % 4)[:, c * S:(c + 1) * S],
                            scalar=gain(2 * m + c) if gain else 1.0,
                            in1=act_hi[:, 2 * m + c, :].bitcast(F32), op0=ALU.mult, op1=ALU.subtract)
                    ins.then_inc(turned_lo, 1)

            def col(base):
                return lambda c: colc[:, base + c:base + c + 1]

            for b in range(2):
                dve.memset(pad[:, 4 * b:4 * b + 4, :], 0.0).then_inc(pad_free, 1)
            for n in range(AHEAD):
                lo(n, 0)
            norm(0)
            scaled(x_sb, x_sb)
            dve.wait_ge(small_in, 64)
            turn(0, col(G1))

            dve.wait_ge(dt_sum, 1)
            own.mark(dve.tensor_tensor(dtt[:, 0, :].rearrange("p (t h) -> p t h", t=TT),
                                       bank(4)[:, 0:TT * 64].rearrange("p (t h) -> p t h", t=TT),
                                       rowc[:, R_DTB:R_DTB + 64].unsqueeze(1).to_broadcast([P, TT, 64]),
                                       ALU.add))
            own.wait()
            dve.scalar_tensor_tensor(out=dtt[:, 1, :], in0=dtt[:, 0, :], scalar=-1.0, in1=dtt[:, 0, :],
                                     op0=ALU.mult, op1=ALU.max).then_inc(dt_abs, 1)

            def conv_chunk(b, m):
                dve.wait_ge(banks_free, 4 + 2 * b + 2)
                if b >= 2:
                    dve.wait_ge(silued, b - 1)
                k, ch = 4 * (b % 2) + m, 4 * b + m
                for tap in range(CONV_K):
                    w = colc[:, CW + CONV_K * ch + tap:CW + CONV_K * ch + tap + 1]
                    if tap == 0:
                        ins = dve.tensor_scalar(conv[:, k, :], pad[:, k, 0:S], w,
                                                colc[:, CB + ch:CB + ch + 1], ALU.mult, ALU.add)
                    else:
                        own.wait()
                        ins = dve.scalar_tensor_tensor(out=conv[:, k, :], in0=pad[:, k, tap:tap + S],
                                                       scalar=w, in1=conv[:, k, :],
                                                       op0=ALU.mult, op1=ALU.add)
                    if tap < CONV_K - 1:
                        own.mark(ins)
                    else:
                        ins.then_inc(conved if m == 3 else pad_free if m == 2 else own_dve, 1)
                        if m < 2:
                            own.n += 1

            def xbc_during(b, j):
                if b and 3 <= j <= 6:
                    conv_chunk(b - 1, (1, 0, 2, 3)[j - 3])

            stage_with("xbc", xbc_during)
            for m in range(4):
                conv_chunk(5, (1, 0, 2, 3)[m])
            stage("z")

            dve.wait_ge(dt_exp, 2)
            s_, s2, p_ = dtt[:, 2, :], dtt[:, 3, :], dtt[:, 4, :]

            def step(ins):
                own.mark(ins)
                own.wait()

            step(dve.tensor_scalar(s2, dtt[:, 1, :], 2.0, None, ALU.add))
            step(dve.reciprocal(p_, s2))
            step(dve.tensor_tensor(s_, dtt[:, 1, :], p_, ALU.mult))
            step(dve.tensor_tensor(s2, s_, s_, ALU.mult))
            step(dve.tensor_scalar(p_, s2, 1.0 / 17, None, ALU.mult))
            for k in range(7, 0, -1):
                step(dve.scalar_tensor_tensor(out=p_, in0=p_, scalar=1.0 / (2 * k + 1), in1=s2,
                                              op0=ALU.add, op1=ALU.mult))
            step(dve.scalar_tensor_tensor(out=p_, in0=p_, scalar=1.0, in1=s_, op0=ALU.add, op1=ALU.mult))
            step(dve.tensor_scalar(s2, dtt[:, 0, :], 0.0, None, ALU.max))
            step(dve.scalar_tensor_tensor(out=dtv.rearrange("p t h -> p (t h)"), in0=p_, scalar=2.0,
                                          in1=s2, op0=ALU.mult, op1=ALU.add))
            for t in range(TT):
                ins = dve.scalar_tensor_tensor(out=av[:, t, :], in0=dtv[:, t, :], scalar=-1.0,
                                               in1=aexp[:, :], op0=ALU.mult, op1=ALU.mult)
            ins.then_inc(a_ready, 1)
            dve.wait_ge(dec_exp, 1)
            for t in range(TT):
                ins = dve.tensor_tensor(dd[:, t, :], dtv[:, t, 32 * t:32 * t + 32], ex[:, 2 + t, :], ALU.mult)
            ins.then_inc(decayed, 1)

            def heads(v):
                return v.rearrange("p (h d) -> p h d", h=HPG)

            def per_head(v):
                return v.unsqueeze(2).to_broadcast([P, HPG, SSD_DIM])

            def matrices(n):
                g, c = n // TT, n % TT
                if n == 0:
                    dve.wait_ge(xt_out, 10)
                if n >= 2:
                    dve.wait_ge(y_sum, n - 1)
                for r in range(2):
                    d_h = dtv[:, c, 32 * r + g * HPG:32 * r + (g + 1) * HPG]
                    dve.tensor_tensor(heads(xf[:, n % 2, r, :]), heads(xt[:, c, g * NB:(g + 1) * NB]),
                                      per_head(d_h), ALU.mult).then_inc(own_dve, 1)
                own.n += 2
                dve.wait_ge(cb_sum, n + 1)
                for r, m in ((0, upper), (1, lower)):
                    own.mark(dve.tensor_tensor(cbm[:, n % 2, r, :], bank(0)[:, (n % 2) * P:(n % 2 + 1) * P],
                                               m[:, :], ALU.mult))
                own.wait()
                dve.wait_ge(seg_exp, n + 1)
                for r in range(2):
                    e = em[:, n % 2, r]
                    ins = dve.tensor_tensor(e, e, cbm[:, n % 2, r, :].unsqueeze(1).to_broadcast([P, HPG, P]),
                                            ALU.mult)
                ins.then_inc(em_ready, 1)

            def outputs(n):
                g, c = n // TT, n % TT
                dve.wait_ge(y_sum, n + 1)
                step(dve.tensor_tensor(heads(ytmp), heads(bank(2)), per_head(ex[:, c, g * HPG:(g + 1) * HPG]),
                                       ALU.mult))
                step(dve.tensor_tensor(ytmp, ytmp, bank(1), ALU.add))
                dve.wait_ge(skip_ready, n + 1)
                step(dve.tensor_tensor(ytmp, ytmp, xsk, ALU.add))
                zg = z_sb[:, c, g * NB:(g + 1) * NB]
                dve.tensor_tensor(zg, zg, ytmp, ALU.mult).then_inc(y_done, 1)

            for n in range(8):
                matrices(n)
                if n:
                    outputs(n - 1)
            outputs(7)
            norm(1)
            scaled(z_sb, z_sb)

            stage("q")

            C1, C2 = 6.28125, 0.0019350051879882812
            C3 = 6.283185307179586 - C1 - C2
            MAGIC, PI = 1.5 * 2.0 ** 23, 3.1415925
            step(dve.tensor_copy(posf[:, :], pos_i[:, :]))
            inv = rowc[:, R_INV:R_INV + 32]
            for t in range(TT):
                own.mark(dve.tensor_scalar(ang[:, 4, t, :], inv, posf[:, t:t + 1], None, ALU.mult))
            own.wait()
            whole = ang[:, 4]
            for k, shift in ((0, 0.0), (1, 0.25)):
                r, turns = ang[:, k], ang[:, 2 + k]
                step(dve.tensor_scalar(turns, whole, 1.0 / 6.283185307179586, shift, ALU.mult, ALU.add))
                step(dve.tensor_scalar(turns, turns, MAGIC, None, ALU.add))
                step(dve.tensor_scalar(turns, turns, -MAGIC, None, ALU.add))
                step(dve.scalar_tensor_tensor(out=r, in0=turns, scalar=-C1, in1=whole, op0=ALU.mult, op1=ALU.add))
                step(dve.scalar_tensor_tensor(out=r, in0=turns, scalar=-C2, in1=r, op0=ALU.mult, op1=ALU.add))
                step(dve.scalar_tensor_tensor(out=r, in0=turns, scalar=-C3, in1=r, op0=ALU.mult, op1=ALU.add))
                if k:
                    step(dve.tensor_scalar(r, r, 1.5707963267948966, None, ALU.add))
                ins = dve.tensor_scalar(r, r, PI, -PI, ALU.min, ALU.max)
                if k:
                    ins.then_inc(angles, 1)
                else:
                    step(ins)
            step(dve.tensor_tensor(lamp[:, :, :], rowc[:, R_LAM:R_LAM + 128].rearrange("p (k d) -> p k d", k=2),
                                   rowc[:, R_LAM + 128:R_LAM + 256].rearrange("p (k d) -> p k d", k=2), ALU.mult))
            dve.tensor_reduce(lam[:, 0:2], lamp[:, :, :], AX.X, ALU.add).then_inc(lam_sum, 1)
            dve.wait_ge(sines, 1)
            for w, base in ((0, R_QG), (1, R_KG)):
                for t in range(TT):
                    for half in range(2):
                        g_ = rowc[:, base + 32 * half:base + 32 * half + 32]
                        own.mark(dve.tensor_tensor(trig[:, w, t, 0, 32 * half:32 * half + 32],
                                                   ang[:, 1, t, :], g_, ALU.mult))
                        own.mark(dve.tensor_tensor(trig[:, w, t, 1, 32 * half:32 * half + 32],
                                                   ang[:, 0, t, :], g_, ALU.mult))
            dve.wait_ge(lam_exp, 1)
            step(dve.tensor_tensor(lam[:, 2:3], lam[:, 1:2], lam[:, 0:1], ALU.subtract))
            step(dve.tensor_scalar(lam[:, 3:4], lam[:, 2:3], -LAM_INIT, None, ALU.add))

            def eight(v):
                return v.rearrange("p (h d) -> p h d", h=8)

            def head_norms(first):
                def f(b, j):
                    n = first + 2 * b + j // 4
                    if j % 4 == 1:
                        dve.wait_ge(head_sq, n + 1)
                        step(dve.tensor_reduce(hstat[:, 0, 0:8], eight(sq), AX.X, ALU.add))
                        dve.tensor_scalar(hstat[:, 1, 0:8], hstat[:, 0, 0:8], 1.0 / ATT_DIM, EPS,
                                          ALU.mult, ALU.add).then_inc(head_ms, 1)
                    if j % 4 == 3:
                        v = head_src(n)
                        dve.wait_ge(head_rt, n + 1)
                        step(dve.reciprocal(hstat[:, 3, 0:8], hstat[:, 2, 0:8]))
                        step(dve.tensor_tensor(eight(v), eight(v),
                                               hstat[:, 3, 0:8].unsqueeze(2).to_broadcast([P, 8, ATT_DIM]),
                                               ALU.mult))
                        for k in range(2):
                            tr = trig[:, n // 8, n % 2, k, :]
                            own.mark(dve.tensor_tensor(eight(rot[:, k, :]), eight(v),
                                                       tr.unsqueeze(1).to_broadcast([P, 8, ATT_DIM]), ALU.mult))
                        own.wait()
                        rc, rsn = eight(rot[:, 0, :]), eight(rot[:, 1, :])
                        step(dve.tensor_tensor(eight(v)[:, :, 0:32], rc[:, :, 0:32], rsn[:, :, 32:64],
                                               ALU.subtract))
                        dve.tensor_tensor(eight(v)[:, :, 32:64], rc[:, :, 32:64], rsn[:, :, 0:32],
                                          ALU.add).then_inc(roped, 1)
                        dve.wait_ge(roped, n + 1)
                return f

            stage_with("k", head_norms(0))
            stage_with("v", head_norms(8))

            def maxima(h):
                dve.wait_ge(scored, h + 1)
                for j in range(2):
                    own.mark(dve.tensor_reduce(mx[:, h % 2, 2 * j:2 * j + 2],
                                               tiles(bank(2 + 2 * (h % 2) + j)), AX.X, ALU.max))
                own.wait()
                if h >= 2:
                    dve.wait_ge(expd, h - 1)
                dve.tensor_scalar(nmx[:, h % 2, :], mx[:, h % 2, :], -SCALE, None, ALU.mult).then_inc(maxed, 1)

            def combine(h):
                dve.wait_ge(expd, h + 1)
                step(dve.reciprocal(ri[:, h % 2, :], rs[:, h % 2, :]))
                step(dve.tensor_scalar(ri[:, h % 2, 2:4], ri[:, h % 2, 2:4], lam[:, 3:4], None, ALU.mult))
                for t in range(TT):
                    own.mark(dve.tensor_scalar(att_x[:, t, :], prob[:, h % 2, 2 + t, :],
                                               ri[:, h % 2, 2 + t:3 + t], None, ALU.mult))
                own.wait()
                if h >= 2:
                    dve.wait_ge(att_turned, h - 1)
                for t in range(TT):
                    ins = dve.scalar_tensor_tensor(out=att[:, h % 2, t, :], in0=prob[:, h % 2, t, :],
                                                   scalar=ri[:, h % 2, t:t + 1], in1=att_x[:, t, :],
                                                   op0=ALU.mult, op1=ALU.add)
                ins.then_inc(att_ready, 1)

            def read_out(h):
                dve.wait_ge(att_turned, h + 1)
                if h >= 2:
                    dve.wait_ge(o_sum, h - 1)
                dve.tensor_copy(att_t[:, h % 2, :], bank(6)).then_inc(att_out, 1)

            def values(h):
                dve.wait_ge(o_sum, h + 1)
                dve.tensor_copy(q_sb[:, :, h * P:(h + 1) * P], tiles(bank(7)[:, (h % 2) * S:(h % 2 + 1) * S]))\
                    .then_inc(o_done, 1)

            for h in range(ATT_HEADS + 2):
                if h < ATT_HEADS:
                    maxima(h)
                if h >= 2:
                    values(h - 2)
                if 1 <= h <= ATT_HEADS:
                    combine(h - 1)
                    read_out(h - 1)
            for t in range(TT):
                v16h = q_sb[:, t, :].rearrange("p (h d) -> p h d", h=ATT_HEADS)
                dve.wait_ge(head_sq, 17 + t)
                step(dve.tensor_reduce(hstat[:, 0, :], o_sq.rearrange("p (h d) -> p h d", h=ATT_HEADS),
                                       AX.X, ALU.add))
                dve.tensor_scalar(hstat[:, 1, :], hstat[:, 0, :], 1.0 / P, EPS, ALU.mult, ALU.add)\
                    .then_inc(head_ms, 1)
                dve.wait_ge(head_rt, 17 + t)
                step(dve.reciprocal(hstat[:, 3, :], hstat[:, 2, :]))
                step(dve.tensor_scalar(hstat[:, 3, :], hstat[:, 3, :], 1.0 - LAM_INIT, None, ALU.mult))
                ins = dve.tensor_tensor(v16h, v16h, hstat[:, 3, :].unsqueeze(2).to_broadcast([P, ATT_HEADS, P]),
                                        ALU.mult)
                if t == 0:
                    step(ins)
                else:
                    ins.then_inc(rows_ready, 1)

            stage("gates")
            turn(1, col(GS))

            def ssd_after(b, parity):
                for t in range(TT):
                    dve.tensor_tensor(mixed[:, t, bass.ds(b * NB, NB)], gates[:, t, bass.ds(b * NB, NB)],
                                      bank(2 * parity + t), ALU.mult).then_inc(banks_free, 1)

            stage("ssd_out", ssd_after)
            turn(2, lambda c: colc[:, GA:GA + 1])

            def att_after(b, parity):
                for t in range(TT):
                    dve.tensor_tensor(mtmp[:, t, :], gates[:, t, bass.ds(D + b * NB, NB)],
                                      bank(2 * parity + t), ALU.mult).then_inc(banks_free, 1)
                dve.wait_ge(banks_free, 4 + 2 * FIRST["att_out"] + 2 * b + 2)
                own.mark(dve.tensor_tensor(mixed[:, :, bass.ds(b * NB, NB)], mixed[:, :, bass.ds(b * NB, NB)],
                                           mtmp, ALU.add))
                own.wait()

            stage("att_out", att_after, 1)
            dve.engine_nop().then_inc(rows_ready, 1)
            turn(3)

            def x_after(b, parity):
                for t in range(TT):
                    dve.tensor_tensor(x1[:, t, bass.ds(b * NB, NB)], x1[:, t, bass.ds(b * NB, NB)],
                                      bank(2 * parity + t), ALU.add).then_inc(banks_free, 1)

            dve.wait_ge(x_again, 32)
            stage("w_out", x_after)
            norm(2)
            dve.wait_ge(g2_in, 16)
            for t in range(TT):
                ins = dve.scalar_tensor_tensor(out=h2[:, t, :], in0=x1[:, t, :], scalar=stat[:, 6 + t:7 + t],
                                               in1=g2_sb, op0=ALU.mult, op1=ALU.mult)
            ins.then_inc(rows_ready, 1)
            turn(4)
            stage("peer_q")

            step(dve.tensor_copy(iota_f[:, :], iota_i[:, :]))

            def top16(n, src, vals, idx):
                for r in range(2):
                    for k in range(n):
                        own.mark(dve.max(vals[:, k, 8 * r:8 * r + 8], src[:, k, :]))
                    own.wait()
                    for k in range(n):
                        own.mark(dve.max_index(idx[:, k, 8 * r:8 * r + 8], vals[:, k, 8 * r:8 * r + 8],
                                               src[:, k, :]))
                    own.wait()
                    if r == 0:
                        for k in range(n):
                            own.mark(dve.match_replace(src[:, k, :], vals[:, k, 0:8], src[:, k, :], LOWEST))
                        own.wait()

            for t in range(TT):
                dve.wait_ge(key_out, t + 1)
                top16(KC, key_scores(t), v16, i16)
                step(dve.tensor_copy(i16f[:, :, :], i16[:, :, :]))
                vv = v16[:, :, :].rearrange("p (h k) c -> p h k c", k=2)
                c4 = cand.rearrange("p h (a b) -> p h a b", a=TOPK)
                step(dve.tensor_tensor(c4, vv[:, :, 0, :].unsqueeze(3).to_broadcast([P, EXPERT_HEADS, TOPK, TOPK]),
                                       vv[:, :, 1, :].unsqueeze(2).to_broadcast([P, EXPERT_HEADS, TOPK, TOPK]),
                                       ALU.add))
                top16(EXPERT_HEADS, cand, sc16, ps16)
                dve.tensor_tensor(gate[:, t, :].rearrange("p (h k) -> p h k", h=EXPERT_HEADS), sc16[:, :, :],
                                  sc16[:, :, 0:1].to_broadcast([P, EXPERT_HEADS, TOPK]), ALU.subtract)\
                    .then_inc(top_sub, 1)
                pos16 = ps16.rearrange("p h k -> p (h k)").bitcast(I32)
                pk = picks[:, t, :]
                for k in range(2):
                    if k == 0:
                        step(dve.tensor_scalar(pk, pos16, 4, None, ALU.logical_shift_right))
                    else:
                        step(dve.tensor_scalar(pk, pos16, TOPK - 1, None, ALU.bitwise_and))
                    step(dve.tensor_copy(psf[:, k, :], pk))
                    step(dve.tensor_tensor(onehot, psf[:, k, :].unsqueeze(2).to_broadcast([P, PICKS, TOPK]),
                                           iota_f[:, :].unsqueeze(1).to_broadcast([P, PICKS, TOPK]),
                                           ALU.is_equal))
                    oh = onehot.rearrange("p (h k) c -> p h k c", h=EXPERT_HEADS)
                    ii = i16f[:, :, :].rearrange("p (h k) c -> p h k c", k=2)[:, :, k, :]
                    step(dve.tensor_tensor(oh, oh, ii.unsqueeze(2).to_broadcast([P, EXPERT_HEADS, TOPK, TOPK]),
                                           ALU.mult))
                    step(dve.tensor_reduce(ef[:, k, :], onehot, AX.X, ALU.add))
                step(dve.scalar_tensor_tensor(out=psf[:, 0, :], in0=ef[:, 0, :], scalar=float(NKEYS),
                                              in1=ef[:, 1, :], op0=ALU.mult, op1=ALU.add))
                dve.tensor_copy(pk, psf[:, 0, :]).then_inc(picked, 1)
                dve.wait_ge(picked, t + 1)
                dve.wait_ge(top_exp, t + 1)
                g3 = gate[:, t, :].rearrange("p (h k) -> p h k", h=EXPERT_HEADS)
                step(dve.tensor_reduce(esum[:, 0, :], g3, AX.X, ALU.add))
                step(dve.reciprocal(esum[:, 1, :], esum[:, 0, :]))
                step(dve.tensor_tensor(g3, g3, esum[:, 1, :].unsqueeze(2).to_broadcast([P, EXPERT_HEADS, TOPK]),
                                       ALU.mult))

            used = 0
            for t in range(TT):
                with dve.Fori(0, PICKS // SLOTS) as i:
                    for s in range(SLOTS):
                        dve.wait_ge(row_in[s], 16 * (used // SLOTS) + 16 * i + 16)
                        dve.scalar_tensor_tensor(out=slot[:, s, :], in0=slot[:, s, :], scalar=1.0,
                                                 in1=h2[:, t, :], op0=ALU.mult, op1=ALU.mult,
                                                 accum_out=dots[:, t, bass.ds(i * SLOTS + s, 1)])\
                            .then_inc(row_free, 1)
                used += PICKS
                dve.wait_ge(gelued, t + 1)
                step(dve.tensor_tensor(dots[:, t, :], dots[:, t, :], gate[:, t, :], ALU.mult))
                with dve.Fori(0, PICKS // SLOTS) as i:
                    for s in range(SLOTS):
                        dve.wait_ge(row_free, SLOTS + used + SLOTS * i + s)
                        dve.wait_ge(row_in[s], 16 * (used // SLOTS) + 16 * i + 16)
                        dve.scalar_tensor_tensor(out=x1[:, t, :], in0=slot[:, s, :],
                                                 scalar=dots[:, t, bass.ds(i * SLOTS + s, 1)],
                                                 in1=x1[:, t, :], op0=ALU.mult, op1=ALU.add)\
                            .then_inc(row_free, 1)
                used += PICKS

            norm(3)
            scaled(h3, x1)
            turn(5, col(G3))

            def out_after(b, parity):
                dve.wait_ge(banks_free, 4 + 2 * FIRST["ple_gate"] + 2 * b + 2)
                step(dve.tensor_tensor(gsig[:, parity], gsig[:, parity], ple_sb[:, :, b * NB:(b + 1) * NB],
                                       ALU.mult))
                xs = x1[:, :, b * NB:(b + 1) * NB]
                dve.tensor_tensor(xs, xs, gsig[:, parity], ALU.add).then_inc(out_ready, 1)

            dve.wait_ge(ple_out, 4)
            stage_with("ple_gate", None, out_after)

        @block.tensor
        def _(pe):
            def mm(out_, lhs, rhs, start, stop, shared=False):
                return nc.tensor.matmul(out_, lhs, rhs, start=start, stop=stop, skip_group_check=shared)

            def turn(k, src):
                pe.wait_ge(rows_ready, k + 1)
                for m in range(8):
                    if 8 * k + m >= 4:
                        pe.wait_ge(turned_lo, 8 * k + m - 3)
                    for c in range(2):
                        for t in range(TT):
                            ins = pe.transpose(bank(4 + m % 4)[:, c * S + t * P:c * S + (t + 1) * P],
                                               src[:, t, (2 * m + c) * P:(2 * m + c + 1) * P], ident[:, :])
                    ins.then_inc(turned, 1)

            def stage(name, k, by_feature=False):
                pe.wait_ge(turned_lo, 8 * k + 8)
                with pe.Fori(0, BLOCKS_OF[name] // 2) as i:
                    for b in range(2):
                        block_no = FIRST[name] + b + 2 * i
                        pe.wait_ge(banks_free, 2 * block_no + 2)
                        for j in range(8):
                            pe.wait_ge(lo_split, 8 * block_no + j + 1)
                            for cc in range(2):
                                c = 2 * j + cc
                                wh = w_hi[:, j % SPLIT, cc * NB:(cc + 1) * NB]
                                wl = w_lo[:, j % SPLIT, cc * NB:(cc + 1) * NB]
                                if by_feature:
                                    for m in range(4):
                                        o = bank(2 * b + m // 2)[:, (m % 2) * S:(m % 2 + 1) * S]
                                        cut = slice(m * P, (m + 1) * P)
                                        mm(o, wh[:, cut], act_hi[:, c, :], c == 0 and m % 2 == 0, False, True)
                                        mm(o, wh[:, cut], act_lo[:, c, :], False, False, True)
                                        ins = mm(o, wl[:, cut], act_hi[:, c, :], False, c == KC - 1, True)
                                else:
                                    for t in range(TT):
                                        o, cut = bank(2 * b + t), slice(t * P, (t + 1) * P)
                                        mm(o, act_hi[:, c, cut], wh, c == 0, False)
                                        mm(o, act_hi[:, c, cut], wl, False, False)
                                        ins = mm(o, act_lo[:, c, cut], wh, False, c == KC - 1)
                            ins.then_inc(half_free, 1)

            pe.wait_ge(masks, 6)
            turn(0, x_sb)
            pe.wait_ge(turned_lo, 8)
            pe.wait_ge(small_in, 64)
            for t in range(TT):
                for c in range(KC):
                    for part, a in enumerate((act_hi, act_lo)):
                        ins = mm(bank(4)[:, t * 64:(t + 1) * 64], a[:, c, t * P:(t + 1) * P].bitcast(F32),
                                 wdt_sb[:, c, :], c == 0 and part == 0, c == KC - 1 and part == 1)
            ins.then_inc(dt_sum, 1)
            stage("xbc", 0, by_feature=True)
            stage("z", 0)

            pe.wait_ge(silued, 6)
            pe.wait_ge(dt_abs, 1)
            for m in range(10):
                if m >= 4:
                    pe.wait_ge(xt_out, m - 3)
                t, q = m % 2, m // 2
                for c in range(4):
                    ins = pe.transpose(bank(4 + m % 4)[:, c * P:(c + 1) * P],
                                       xbc[:, 4 * q + c, t * P:(t + 1) * P], ident[:, :])
                ins.then_inc(xt_turned, 1)
            pe.wait_ge(a_ready, 1)
            pe.wait_ge(banks_free, 4 + 2 * FIRST["q"])
            for k, (m, t, r) in enumerate(((lower, 0, 1), (upper, 1, 0), (below, 0, 0), (above, 1, 1))):
                ins = mm(bank(0)[:, 32 * k:32 * k + 32], m[:, :], av[:, t, 32 * r:32 * r + 32], True, True)
            ins.then_inc(dec_sum, 1)

            def states(g):
                pe.wait_ge(xd_ready, 2 * g + 2)
                if g:
                    pe.wait_ge(y_done, 2 * g)
                for t in range(TT):
                    ins = mm(bank(2 + t), bt[:, t, g * P:(g + 1) * P], xd[:, t, :], True, True)
                ins.then_inc(state_sum, 1)

            def segments(n):
                g, c = n // TT, n % TT
                pe.wait_ge(rh_ready, 2 * n + 2)
                if n:
                    pe.wait_ge(seg_exp, n)
                else:
                    pe.wait_ge(xt_out, 10)
                for r, m in ((0, below), (1, above)):
                    for q in range(2):
                        ins = mm(bank(4 + 2 * r + q), m[:, :],
                                 rh[:, n % 2, r, 4 * q:4 * q + 4, :].rearrange("p h l -> p (h l)"), True, True)
                ins.then_inc(seg_sum, 1)
                if n == 0:
                    pe.wait_ge(dec_exp, 1)
                if n:
                    pe.wait_ge(em_ready, n)
                mm(bank(0)[:, (n % 2) * P:(n % 2 + 1) * P], xbc[:, 16 + g, c * P:(c + 1) * P],
                   xbc[:, 20 + g, c * P:(c + 1) * P], True, True).then_inc(cb_sum, 1)

            def products(n):
                g, c = n // TT, n % TT
                pe.wait_ge(em_ready, n + 1)
                if n:
                    pe.wait_ge(y_done, n)
                for h in range(HPG):
                    for r in range(2):
                        mm(bank(1)[:, h * SSD_DIM:(h + 1) * SSD_DIM], em[:, n % 2, r, h, :],
                           xf[:, n % 2, r, h * SSD_DIM:(h + 1) * SSD_DIM], r == 0, r == 1)
                pe.wait_ge(state_out, g + 1)
                mm(bank(2), xbc[:, 20 + g, c * P:(c + 1) * P], hs[:, 1 - c, :], True, True).then_inc(y_sum, 1)

            states(0)
            segments(0)
            for n in range(8):
                if n < 7:
                    segments(n + 1)
                products(n)
                if n % 2 and n < 7:
                    states(n // 2 + 1)

            pe.wait_ge(y_done, 8)
            for name in ("q", "k", "v"):
                stage(name, 0)

            def turn_qk(h):
                if h >= 2:
                    pe.wait_ge(qk_out, h - 1)
                for w, src in enumerate((q_sb, k_sb)):
                    for t in range(TT):
                        ins = pe.transpose(bank(h % 2)[:, w * S + t * P:w * S + (t + 1) * P],
                                           src[:, t, h * P:(h + 1) * P], ident[:, :])
                ins.then_inc(qk_turned, 1)

            def scores(h):
                pe.wait_ge(qk_out, h + 1)
                if h >= 2:
                    pe.wait_ge(expd, h - 1)
                for j in range(2):
                    rows_j = slice(ATT_DIM * j, ATT_DIM * (j + 1))
                    for t in range(TT):
                        ins = mm(bank(2 + 2 * (h % 2) + j)[:, t * S:(t + 1) * S],
                                 qkt[rows_j, h % 2, t * P:(t + 1) * P], qkt[rows_j, h % 2, S:2 * S], True, True)
                ins.then_inc(scored, 1)

            def turn_att(h):
                pe.wait_ge(att_ready, h + 1)
                if h:
                    pe.wait_ge(att_out, h)
                for t in range(TT):
                    for kc in range(2):
                        ins = pe.transpose(bank(6)[:, kc * S + t * P:kc * S + (t + 1) * P],
                                           att[:, h % 2, t, kc * P:(kc + 1) * P], ident[:, :])
                ins.then_inc(att_turned, 1)

            def times_v(h):
                pe.wait_ge(att_out, h + 1)
                if h:
                    pe.wait_ge(o_done, h)
                for t in range(TT):
                    for kc in range(2):
                        ins = mm(bank(7)[:, (h % 2) * S + t * P:(h % 2) * S + (t + 1) * P],
                                 att_t[:, h % 2, kc * S + t * P:kc * S + (t + 1) * P],
                                 v_sb[:, kc, h * P:(h + 1) * P], kc == 0, kc == 1)
                ins.then_inc(o_sum, 1)

            pe.wait_ge(roped, 16)
            pe.wait_ge(banks_free, 4 + 2 * FIRST["gates"])
            turn_qk(0)
            for h in range(ATT_HEADS + 1):
                if h + 1 < ATT_HEADS:
                    turn_qk(h + 1)
                if h < ATT_HEADS:
                    scores(h)
                if h:
                    turn_att(h - 1)
                    times_v(h - 1)

            pe.wait_ge(expd, ATT_HEADS)
            stage("gates", 0)
            turn(1, z_sb)
            stage("ssd_out", 1)
            turn(2, q_sb)
            stage("att_out", 2)
            turn(3, mixed)
            stage("w_out", 3)
            turn(4, h2)
            stage("peer_q", 4, by_feature=True)

            pe.wait_ge(keys_in, 16)
            pe.wait_ge(banks_free, 4 + 2 * FIRST["ple_gate"])
            for t in range(TT):
                for n in range(KC):
                    ins = mm(bank(4 * t + n // 4)[:, (n % 4) * NKEYS:(n % 4 + 1) * NKEYS],
                             pq[:, n, t * P:(t + 1) * P], keys_sb[:, n, :], True, True)
                ins.then_inc(key_sum, 1)

            pe.wait_ge(ple_in, 32)
            pe.wait_ge(key_out, 2)
            for b in range(D // NB):
                if b >= 2:
                    pe.wait_ge(ple_out, b - 1)
                for t in range(TT):
                    for c in range(2):
                        ins = mm(bank(2 * (b % 2) + t), pt_sb[:, c, t * P:(t + 1) * P],
                                 up_sb[:, c, b * NB:(b + 1) * NB], c == 0, c == 1)
                ins.then_inc(ple_sum, 1)
            turn(5, h3)
            pe.wait_ge(ple_out, 4)
            stage("ple_gate", 5)


def _columns(m, nblocks):
    return m.reshape(4, 4, P, nblocks, NB).transpose(3, 0, 2, 1, 4).reshape(nblocks * 4, P, 4 * NB)


def kernel(**inputs):
    import numpy as np
    import concourse.bacc as bacc
    from concourse.bass_utils import run_bass_kernel_spmd

    a = {k: np.asarray(v) for k, v in inputs.items()}
    w_in = a["w_in"][0]
    at = np.cumsum([0, D, XBC * P, 2 * SSD_HEADS, D, D, D, 2 * D])
    z, xbc, dt, q, k, v, gates = (w_in[:, at[n]:at[n + 1]] for n in range(7))
    parts = {"xbc": xbc, "z": z, "q": q, "k": k, "v": v, "gates": gates,
             "ssd_out": a["w_ssd_br"][0], "att_out": a["w_att_br"][0], "w_out": a["w_out"][0],
             "peer_q": a["peer_wq"][0], "ple_gate": a["ple_gate_w"][0]}
    wall = np.concatenate([_columns(parts[name], n) for name, n in STAGES])

    def chunks(g):
        return g.reshape(-1, P).T

    cols = np.concatenate([
        chunks(a["norm1_g"][0]), chunks(a["ssd_norm_g"][0]), chunks(a["norm3_g"][0]),
        a["subln_g"][0].reshape(P, 1),
        a["conv_w"][0].reshape(CONV_K, XBC, P).transpose(2, 1, 0).reshape(P, XBC * CONV_K),
        chunks(a["conv_b"][0])], axis=1)
    inv = (10000.0 ** (-np.arange(0, ATT_DIM, 2, dtype=np.float64) / ATT_DIM)).astype(np.float32)
    rows = np.concatenate([
        a["dt_bias_f"][0], a["dt_bias_b"][0], a["a_log_f"][0], a["a_log_b"][0], a["d_skip"][0],
        a["q_norm_g"][0], a["k_norm_g"][0], a["lam_q1"][0], a["lam_q2"][0], a["lam_k1"][0],
        a["lam_k2"][0], inv]).reshape(1, ROWS)
    arrays = {
        "x": a["x"].reshape(TT, P, D),
        "wall": wall,
        "wdt": dt.reshape(KC, P, 64).transpose(1, 0, 2).reshape(P, KC * 64),
        "cols": cols,
        "rows": rows,
        "pos": a["positions"].reshape(TT, P).T.astype(np.int32),
        "g2": a["norm2_g"].reshape(1, D),
        "keys_t": a["peer_keys"][0].transpose(3, 0, 1, 2).reshape(P, KC * NKEYS),
        "peer_u": a["peer_u"][0],
        "peer_v": a["peer_v"][0],
        "p_t": a["p"][0, 0].reshape(S, 2, P).transpose(2, 1, 0).reshape(P, 2 * S),
        "ple_up": a["ple_up_w"][0].reshape(2, P, D).transpose(1, 0, 2).reshape(P, 2 * D),
    }
    arrays = {n: np.ascontiguousarray(v) for n, v in arrays.items()}
    nc = bacc.Bacc("TRN2", target_bir_lowering=False, num_devices=1)
    args = [nc.dram_tensor(n, v.shape, mybir.dt.from_np(v.dtype), kind="ExternalInput").ap()
            for n, v in arrays.items()]
    out = nc.dram_tensor("out", (TT, P, D), F32, kind="ExternalOutput").ap()
    build(nc, *args, out)
    r = run_bass_kernel_spmd(nc, [arrays], core_ids=[0])
    return r.results[0]["out"].reshape(1, S, D)
```

```python
from contextlib import ExitStack

import concourse.bass as bass
import numpy as np
from concourse import mybir

F32 = mybir.dt.float32
F32R = mybir.dt.float32r
I32 = mybir.dt.int32
U32 = mybir.dt.uint32
ALU = mybir.AluOpType
ACT = mybir.ActivationFunctionType
AX = mybir.AxisListType

P = 128
D = 2048
TT = 2
S = TT * P
KC = D // P
SSD_HEADS, SSD_DIM, GROUPS, STATE = 32, 64, 4, 128
HPG = SSD_HEADS // GROUPS
CONV_K = 5
XBC = (D + 2 * GROUPS * STATE) // P
ATT_HEADS, ATT_DIM = 16, 64
EXPERT_HEADS, NKEYS, TOPK = 8, 128, 16
PICKS = EXPERT_HEADS * TOPK
PLE = 256
EPS = 1e-6
LAM_INIT = 0.2
SCALE = ATT_DIM ** -0.5
LOWEST = -3.0e38
SLOTS = 8

NB = 512
PIECE = 2 * NB
RING = 4
AHEAD = 2
STAGES = [("xbc", 6), ("q", 4), ("k", 4), ("v", 4), ("z", 4), ("gates", 8),
          ("ssd_out", 4), ("att_out", 4), ("w_out", 4), ("peer_q", 4), ("ple_gate", 4)]
FIRST = {}
_n = 0
for _name, _k in STAGES:
    FIRST[_name] = _n
    _n += _k
BLOCKS = _n
PIECES = 8 * BLOCKS

XT_0 = 57
SSD_0, SSD_STEP = 62, 10
NORM_0, NORM_STEP = 82, 4
ATT_0, ATT_STEP = 150, 4
O_NORM = 219
Y_NORM = 179
X_NORM = 339
TURNS = {1: FIRST["ssd_out"], 2: FIRST["att_out"], 3: FIRST["w_out"], 4: FIRST["peer_q"]}

G1, GS, G2, G3, GA, CW = 0, 16, 32, 48, 64, 65
CB = CW + XBC * CONV_K
COLS = CB + XBC
R_DTB, R_ALOG, R_DSKIP, R_QG, R_KG, R_LAM, R_INV = 0, 64, 128, 160, 224, 288, 544
ROWS = 576


class Steps:

    def __init__(self, eng, sem):
        self.eng, self.sem, self.n = eng, sem, 0

    def mark(self, ins):
        ins.then_inc(self.sem, 1)
        self.n = self.n + 1

    def wait(self):
        self.eng.wait_ge(self.sem, self.n)


def turn_step(s, late):
    for k, first in TURNS.items():
        m = s - late - 8 * first
        if -8 <= m < -2:
            return k, m + 8
        if 2 <= m < 4:
            return k, m + 4
    return None


def build(nc, x, wall, wdt, cols, rows, pos, g2, keys_t, peer_u, peer_v, p_t, ple_up, out):
    ctx = ExitStack()
    with ctx:
        def sb(name, shape, dt=F32):
            return ctx.enter_context(nc.sbuf_tensor(name, shape, dt))

        def sem(name):
            return ctx.enter_context(nc.semaphore(name))

        act_hi = sb("act_hi", [P, KC, S], F32R)
        act_lo = sb("act_lo", [P, KC, S], F32R)
        w_hi = sb("w_hi", [P, RING, PIECE], F32R)
        w_lo = sb("w_lo", [P, RING, PIECE], F32R)
        w_raw = sb("w_raw", [P, RING, PIECE])
        work = sb("work", [P, 14 * D])
        ident = sb("ident", [P, P])
        upper = sb("upper", [P, P])
        lower = sb("lower", [P, P])
        below = sb("below", [P, P])
        above = sb("above", [P, P])
        colc = sb("colc", [P, COLS])
        rowc = sb("rowc", [P, ROWS])
        pos_i = sb("pos_i", [P, TT], I32)
        stat = sb("stat", [P, 4, 4, TT])
        iota_i = sb("iota_i", [P, TOPK], I32)
        iota_f = sb("iota_f", [P, TOPK])
        staged = sb("staged", [P, 2 * SLOTS], I32)
        small = sb("small", [P, 2320])

        def carve(at, *shapes):
            views = []
            for shape in shapes:
                n = int(np.prod(shape))
                v = small[:, at:at + n]
                if len(shape) > 1:
                    names = "abcd"[:len(shape)]
                    v = v.rearrange("p (" + " ".join(names) + ") -> p " + " ".join(names),
                                    **dict(zip(names, shape)))
                views.append(v)
                at += n
            return views

        dtv, av, aexp, ex, dd, dtt = carve(
            0, (TT, 64), (TT, 64), (64,), (4, SSD_HEADS), (TT, SSD_HEADS), (5, TT * 64))
        cbm, = carve(512, (2, P))
        trig, hstat, lam, mx, nmx, rs, ri, posf, ang, lamp = carve(
            1152, (2, TT, 2, ATT_DIM), (4, ATT_HEADS), (4,), (2, 4), (2, 4), (2, 4), (2, 4), (TT,),
            (5, TT, 32), (2, ATT_DIM))
        v16, i16, i16f, sc16, ps16, psf, ef, esum, picks, gate, dots = carve(
            0, (KC, TOPK), (KC, TOPK), (KC, TOPK), (EXPERT_HEADS, TOPK), (EXPERT_HEADS, TOPK),
            (2, PICKS), (2, PICKS), (2, EXPERT_HEADS), (TT, PICKS), (TT, PICKS), (TT, PICKS))
        i16, ps16, picks = i16.bitcast(U32), ps16.bitcast(U32), picks.bitcast(I32)

        PS = ctx.enter_context(nc.psum_tensor("PS", [P, 8 * NB], F32))

        def blk(first, n=1):
            return work[:, first * D:(first + n) * D]

        def bank(b, n=1):
            return PS[:, b * NB:(b + n) * NB]

        def tiles(v):
            return v.rearrange("p (t d) -> p t d", t=TT)

        def by_block(v):
            return v.rearrange("p (b t n) -> p b t n", t=TT, n=NB)

        small_in = sem("small_in")
        x_in = sem("x_in")
        masks = sem("masks")
        raw_in = [sem(f"raw_in{k}") for k in range(RING)]
        hi_split = sem("hi_split")
        lo_split = sem("lo_split")
        used = sem("used")
        banks_free = sem("banks_free")
        own_act = sem("own_act")
        own_dve = sem("own_dve")
        own_pool = sem("own_pool")
        squares = sem("squares")
        means = sem("means")
        roots = sem("roots")
        h_ready = sem("h_ready")
        turned = sem("turned")
        turned_hi = sem("turned_hi")
        turned_lo = sem("turned_lo")
        dt_sum = sem("dt_sum")
        dt_abs = sem("dt_abs")
        dt_exp = sem("dt_exp")
        pad_zero = sem("pad_zero")
        rows_in = sem("rows_in")
        conved = sem("conved")
        silued = sem("silued")
        xt_turned = sem("xt_turned")
        xt_out = sem("xt_out")
        a_ready = sem("a_ready")
        dec_sum = sem("dec_sum")
        dec_exp = sem("dec_exp")
        decayed = sem("decayed")
        xd_ready = sem("xd_ready")
        xf_ready = sem("xf_ready")
        state_sum = sem("state_sum")
        state_out = sem("state_out")
        rh_ready = sem("rh_ready")
        seg_sum = sem("seg_sum")
        seg_exp = sem("seg_exp")
        cb_sum = sem("cb_sum")
        cb_out = sem("cb_out")
        em_ready = sem("em_ready")
        skip_ready = sem("skip_ready")
        y_sum = sem("y_sum")
        y_done = sem("y_done")
        z_ready = sem("z_ready")
        y_gated = sem("y_gated")
        head_sq = sem("head_sq")
        head_ms = sem("head_ms")
        head_rt = sem("head_rt")
        angles = sem("angles")
        sines = sem("sines")
        lam_sum = sem("lam_sum")
        lam_exp = sem("lam_exp")
        roped = sem("roped")
        qk_turned = sem("qk_turned")
        qk_out = sem("qk_out")
        scored = sem("scored")
        maxed = sem("maxed")
        expd = sem("expd")
        att_ready = sem("att_ready")
        att_turned = sem("att_turned")
        att_out = sem("att_out")
        o_sum = sem("o_sum")
        o_done = sem("o_done")
        o_ready = sem("o_ready")
        mixed_ready = sem("mixed_ready")
        x_again = sem("x_again")
        g2_in = sem("g2_in")
        keys_in = sem("keys_in")
        h2_ready = sem("h2_ready")
        key_sum = sem("key_sum")
        key_out = sem("key_out")
        top_sub = sem("top_sub")
        top_exp = sem("top_exp")
        picked = sem("picked")
        indices_staged = sem("indices_staged")
        gathers_due = sem("gathers_due")
        row_in = [sem(f"row_in{k}") for k in range(SLOTS)]
        row_free = sem("row_free")
        gelued = sem("gelued")
        ple_in = sem("ple_in")
        ple_sum = sem("ple_sum")
        ple_out = sem("ple_out")
        out_ready = sem("out_ready")
        stored = sem("stored")

        x_sb = tiles(blk(0, 2))
        wdt_sb = blk(10)[:, 0:KC * 64].rearrange("p (c n) -> p c n", c=KC)
        xbc = blk(2, 3).rearrange("p (c s) -> p c s", c=XBC)
        conv = blk(11).rearrange("p (m s) -> p m s", m=8)
        pad = blk(12, 2)[:, 0:8 * (S + 4)].rearrange("p (m s) -> p m s", m=8)
        qkv = by_block(blk(8, 6))
        xt = tiles(blk(0, 2))
        rh = blk(2).rearrange("p (r h l) -> p r h l", r=2, h=HPG)
        em = blk(3).rearrange("p (r h l) -> p r h l", r=2, h=HPG)
        bt = tiles(blk(5)[:, 0:TT * NB])
        hs = blk(5)[:, TT * NB:TT * NB + NB]
        sq = blk(5)[:, 3 * NB:4 * NB]
        xf = blk(6)[:, 0:2 * NB].rearrange("p (r d) -> p r d", r=2)
        xd = tiles(blk(6)[:, 2 * NB:4 * NB])
        xsk = blk(7)[:, 0:NB]
        ytmp = blk(7)[:, NB:2 * NB]
        rot = blk(7)[:, 2 * NB:4 * NB].rearrange("p (k d) -> p k d", k=2)
        qkt = blk(4)[:, 0:2 * NB].rearrange("p (b s) -> p b s", b=2)
        att_t = blk(4)[:, 2 * NB:4 * NB].rearrange("p (b s) -> p b s", b=2)
        prob = blk(5).rearrange("p (b j s) -> p b j s", b=2, j=4)
        att = blk(6)[:, 0:2 * NB].rearrange("p (b t s) -> p b t s", b=2, t=TT)
        att_x = tiles(blk(6)[:, 2 * NB:3 * NB])
        z_tmp = by_block(blk(7))
        o_sq = blk(7)
        mixed, g_att = by_block(blk(2, 2)), by_block(blk(10, 2))
        x1 = tiles(blk(12, 2))
        h2 = tiles(blk(8, 2))
        g2_sb = blk(4)
        keys_sb = blk(5).rearrange("p (n k) -> p n k", n=KC)
        pq = blk(6, 2).rearrange("p (n s) -> p n s", n=KC)
        key_scores = [blk(10 + t).rearrange("p (n k) -> p n k", n=KC) for t in range(TT)]
        cand = blk(0).rearrange("p (h c) -> p h c", h=EXPERT_HEADS)
        onehot = blk(1).rearrange("p (k c) -> p k c", c=TOPK)
        slot = blk(0, SLOTS).rearrange("p (n d) -> p n d", n=SLOTS)
        pt_sb, = carve(0, (2, S))
        up_sb = by_block(blk(10, 2))
        g_ple = by_block(blk(6))

        JUNK = [7, 3, 0, 0]

        def head_src(n):
            return qkv[:, 4 * (n // 8) + (n % 8) // 2, n % 2, :]

        def head_cols(w, t, h):
            return qkv[:, 4 * w + h // 4, t, (h % 4) * P:(h % 4 + 1) * P]

        def gates_of(b):
            return mixed[:, b] if b < 4 else g_att[:, b - 4]

        def ssd_step(s):
            return (s - SSD_0) // SSD_STEP, (s - SSD_0) % SSD_STEP

        def att_step(s):
            return (s - ATT_0) // ATT_STEP, (s - ATT_0) % ATT_STEP

        def norm_step(s):
            return (s - NORM_0) // NORM_STEP, (s - NORM_0) % NORM_STEP

        def read_out(s, j=1):
            if s % 8 != j or s < 8:
                return None, 0, 0
            n = s // 8 - 1
            name = [m for m, k in STAGES if FIRST[m] <= n][-1]
            return name, n - FIRST[name], n % 2

        block = ctx.enter_context(nc.Block())

        @block.sync
        def _(sp):
            for t in range(TT):
                sp.dma_start(x_sb[:, t, :], x[t]).then_inc(x_in, 16)
            for k in range(RING):
                sp.dma_start(w_raw[:, k, :], wall[k]).then_inc(raw_in[k], 16)
            with sp.Fori(1, PIECES // RING) as g:
                for k in range(RING):
                    sp.wait_ge(lo_split, RING * g - RING + k + 1)
                    sp.dma_start(w_raw[:, k, :], wall[bass.ds(RING * g + k, 1)]
                                 .rearrange("o p n -> (o p) n")).then_inc(raw_in[k], 16)
            with sp.Fori(0, D // NB) as b:
                sp.wait_ge(out_ready, b + 1)
                sp.dma_start(out[:, :, bass.ds(b * NB, NB)].rearrange("t p n -> p t n"),
                             x1[:, :, bass.ds(b * NB, NB)]).then_inc(stored, 16)
            sp.wait_ge(stored, 16 * (D // NB))

        @block.gpsimd
        def _(pool):
            own = Steps(pool, own_pool)
            for m in (upper, lower, below, above):
                own.mark(pool.memset(m[:, :], 1.0))
            own.mark(pool.memset(ident[:, :], 0.0))
            own.wait()
            for m, op, sign in ((upper, ALU.is_ge, -1), (lower, ALU.is_ge, 1),
                                (below, ALU.is_gt, 1), (above, ALU.is_gt, -1)):
                pool.affine_select(out=m[:, :], in_=m[:, :], compare_op=op, fill=0.0, base=0,
                                   pattern=[[-sign, P]], channel_multiplier=sign).then_inc(masks, 1)
            pool.affine_select(out=ident[:, :], in_=ident[:, :], compare_op=ALU.not_equal, fill=1.0,
                               base=0, pattern=[[-1, P]], channel_multiplier=1).then_inc(masks, 1)
            pool.iota(iota_i[:, :], pattern=[[1, TOPK]], base=0, channel_multiplier=0).then_inc(masks, 1)

            pool.wait_ge(masks, 6)
            pool.wait_ge(small_in, 64)
            pool.wait_ge(xt_out, 10)
            pool.wait_ge(decayed, 1)

            def heads(v):
                return v.rearrange("p (h d) -> p h d", h=HPG)

            def per_head(v, n):
                return v.unsqueeze(2).to_broadcast([P, HPG, n])

            for n in range(TT * GROUPS):
                g, c = n // TT, n % TT
                hg = slice(g * HPG, (g + 1) * HPG)
                xg = [heads(xt[:, t, g * NB:(g + 1) * NB]) for t in range(TT)]

                def steps_of_a(r, m):
                    if n:
                        pool.wait_ge(seg_sum, 2 * n - 1 + r)
                    pool.tensor_tensor(rh[:, r], m[:, :].unsqueeze(1).to_broadcast([P, HPG, P]),
                                       per_head(av[:, c, 32 * r + g * HPG:32 * r + (g + 1) * HPG], P),
                                       ALU.mult).then_inc(rh_ready, 1)

                steps_of_a(0, upper)
                if c == 0:
                    if g:
                        pool.wait_ge(state_sum, n)
                    for t in (1, 0):
                        pool.tensor_tensor(heads(xd[:, t, :]), xg[t], per_head(dd[:, t, hg], SSD_DIM),
                                           ALU.mult).then_inc(xd_ready, 1)
                steps_of_a(1, lower)
                if n:
                    pool.wait_ge(y_sum, n)
                for r in range(2):
                    pool.tensor_tensor(heads(xf[:, r, :]), xg[c],
                                       per_head(dtv[:, c, 32 * r + g * HPG:32 * r + (g + 1) * HPG], SSD_DIM),
                                       ALU.mult).then_inc(xf_ready, 1)
                if n:
                    pool.wait_ge(y_done, n)
                pool.tensor_tensor(heads(xsk), xg[c],
                                   per_head(rowc[:, R_DSKIP + g * HPG:R_DSKIP + (g + 1) * HPG], SSD_DIM),
                                   ALU.mult).then_inc(skip_ready, 1)

            pool.wait_ge(o_done, ATT_HEADS)
            for t in range(TT):
                pool.dma_start(x1[:, t, :], x[t]).then_inc(x_again, 16)
            pool.dma_start(g2_sb, g2[0:1, :].to_broadcast([P, D])).then_inc(g2_in, 16)
            pool.dma_start(blk(5), keys_t).then_inc(keys_in, 16)

            pool.wait_ge(picked, TT)
            pool.dma_start(blk(10, 2), ple_up).then_inc(ple_in, 16)
            pool.dma_start(small[:, 0:2 * S], p_t).then_inc(ple_in, 16)
            done = 0
            for t in range(TT):
                for table in (peer_u, peer_v):
                    with pool.Fori(0, PICKS // (2 * SLOTS)) as i:
                        for half in range(2):
                            first = done + half * SLOTS + 2 * SLOTS * i
                            pool.wait_ge(row_free, first + 1)
                            pool.tensor_copy(staged[:, half * SLOTS:(half + 1) * SLOTS],
                                             picks[:, t, bass.ds(i * 2 * SLOTS + half * SLOTS, SLOTS)])\
                                .then_inc(indices_staged, 1)
                            pool.wait_ge(indices_staged, done // SLOTS + 2 * i + half + 1)
                            for s in range(SLOTS):
                                pool.wait_ge(row_free, first + s + 1)
                                pool.sem_inc(gathers_due, 1)
                                k = half * SLOTS + s
                                pool.indirect_dma_start(
                                    slot[:, s, :], None, table[:, :],
                                    bass.IndirectOffsetOnAxis(ap=staged[:, k:k + 1], axis=0),
                                ).then_inc(row_in[s], 16)
                    done += PICKS

        @block.scalar
        def _(act):
            act.sem_inc(used, RING)
            act.sem_inc(banks_free, 4)
            act.dma_start(colc[:, :], cols).then_inc(small_in, 16)
            act.dma_start(rowc[:, :], rows[0:1, :].to_broadcast([P, ROWS])).then_inc(small_in, 16)
            act.dma_start(pos_i[:, :], pos).then_inc(small_in, 16)
            act.dma_start(blk(10)[:, 0:KC * 64], wdt).then_inc(small_in, 16)

            def hi(n):
                act.wait_ge(raw_in[n % RING], 16 * (n // RING + 1))
                act.wait_ge(used, n + 1)
                act.activation(w_hi[:, n % RING, :], w_raw[:, n % RING, :], ACT.Copy).then_inc(hi_split, 1)

            def square(k, t, src):
                if t:
                    act.wait_ge(own_act, k + 1)
                ins = act.activation(blk(JUNK[k]), src[:, t, :], ACT.Square, accum_out=stat[:, k, 0, t:t + 1])
                ins.then_inc(squares if t else own_act, 1)

            def root(k):
                act.wait_ge(means, k + 1)
                act.activation(stat[:, k, 2, :], stat[:, k, 1, :], ACT.Sqrt).then_inc(roots, 1)

            def gain(k, c):
                at = GA if k == 2 else {0: G1, 1: GS, 4: G2, 5: G3}[k] + c
                return colc[:, at:at + 1]

            def turn(k, m):
                act.wait_ge(turned, 8 * k + m + 1)
                if k == 3:
                    act.activation(act_hi[:, 2 * m:2 * m + 2, :],
                                   bank(4 + m % 4).rearrange("p (c s) -> p c s", c=2), ACT.Copy)\
                        .then_inc(turned_hi, 1)
                    return
                for c in range(2):
                    ins = act.activation(act_hi[:, 2 * m + c, :], bank(4 + m % 4)[:, c * S:(c + 1) * S],
                                         ACT.Copy, scale=gain(k, 2 * m + c))
                ins.then_inc(turned_hi, 1)

            def xbc_rows(b, parity):
                act.wait_ge(pad_zero, 2)
                for m in range(2):
                    act.activation(pad[:, 4 * parity + 2 * m:4 * parity + 2 * m + 2, 2:2 + S],
                                   bank(2 * parity + m).rearrange("p (m s) -> p m s", m=2),
                                   ACT.Copy).then_inc(banks_free, 1)

            def beside_xbc(s):
                if s == 1:
                    act.wait_ge(dt_abs, 1)
                    act.activation(dtt[:, 1, :], dtt[:, 1, :], ACT.Exp, scale=-1.0).then_inc(dt_exp, 1)
                    act.activation(aexp, rowc[:, R_ALOG:R_ALOG + 64], ACT.Exp).then_inc(dt_exp, 1)
                if s == 10:
                    act.wait_ge(dec_sum, 1)
                    act.activation(ex, bank(4)[:, 0:4 * SSD_HEADS].rearrange("p (k h) -> p k h", k=4),
                                   ACT.Exp).then_inc(dec_exp, 1)
                if s == 18:
                    act.wait_ge(lam_sum, 1)
                    act.activation(lam[:, 0:2], lam[:, 0:2], ACT.Exp).then_inc(lam_exp, 1)
                    act.wait_ge(angles, 1)
                    act.activation(ang[:, 0:2], ang[:, 0:2], ACT.Sin).then_inc(sines, 1)
                if s % 8 == 7 and s > 8:
                    b = s // 8 - 1
                    act.wait_ge(conved, b + 1)
                    act.activation(xbc[:, 4 * b:4 * b + 4, :], conv[:, 4 * (b % 2):4 * (b % 2) + 4, :],
                                   ACT.Silu).then_inc(silued, 1)

            def beside_ssd(s):
                for m in (2 * (s - XT_0 - 1), 2 * (s - XT_0 - 1) + 1):
                    if 0 <= m < 10:
                        act.wait_ge(xt_turned, m + 1)
                        t, q = m % 2, m // 2
                        act.activation(xt[:, t, q * NB:(q + 1) * NB] if q < 4 else bt[:, t, :],
                                       bank(4 + m % 4), ACT.Copy).then_inc(xt_out, 1)
                n, at = ssd_step(s)
                if 0 <= n < 8 and at in (1, 5):
                    r = at // 4
                    act.wait_ge(seg_sum, 2 * n + r + 1)
                    if n:
                        act.wait_ge(y_sum, n)
                    for q in range(2):
                        ins = act.activation(em[:, r, 4 * q:4 * q + 4, :],
                                             bank(4 + q).rearrange("p (h l) -> p h l", h=4), ACT.Exp)
                    ins.then_inc(seg_exp, 1)
                if 0 <= n < 8 and at == 6:
                    act.wait_ge(state_sum, n + 1)
                    act.activation(hs, bank(7), ACT.Copy).then_inc(state_out, 1)
                n, at = norm_step(s)
                if 0 <= n < 16:
                    if at == 0:
                        if n:
                            act.wait_ge(head_ms, n)
                        act.activation(sq, head_src(n), ACT.Square).then_inc(head_sq, 1)
                    if at == 2:
                        act.wait_ge(head_ms, n + 1)
                        act.activation(hstat[:, 2, 0:8], hstat[:, 1, 0:8], ACT.Sqrt).then_inc(head_rt, 1)

            def beside_att(s):
                h, at = att_step(s)
                if s == ATT_0 - 2:
                    h, at = -1, 0
                if -1 <= h < 15 and at == 0:
                    act.wait_ge(qk_turned, h + 2)
                    if h >= 1:
                        act.wait_ge(scored, h)
                    act.activation(qkt[:, (h + 1) % 2, :], bank(4), ACT.Copy).then_inc(qk_out, 1)
                if 0 <= h < 16 and at == 2:
                    act.wait_ge(maxed, h + 1)
                    if h >= 2:
                        act.wait_ge(att_ready, h - 1)
                    for k in range(4):
                        ins = act.activation(prob[:, h % 2, k, :],
                                             bank(5 + k // 2)[:, (k % 2) * S:(k % 2 + 1) * S], ACT.Exp,
                                             bias=nmx[:, h % 2, k:k + 1], scale=SCALE,
                                             accum_out=rs[:, h % 2, k:k + 1])
                    ins.then_inc(expd, 1)
                t, at = (s - O_NORM) // 4, (s - O_NORM) % 4
                if 0 <= t < TT and at == 0:
                    act.wait_ge(o_done, ATT_HEADS)
                    if t:
                        act.wait_ge(head_ms, 17)
                    act.activation(o_sq.rearrange("p (b n) -> p b n", b=4), qkv[:, 0:4, t, :],
                                   ACT.Square).then_inc(head_sq, 1)
                if 0 <= t < TT and at == 2:
                    act.wait_ge(head_ms, 17 + t)
                    act.activation(hstat[:, 2, :], hstat[:, 1, :], ACT.Sqrt).then_inc(head_rt, 1)
                if s in (Y_NORM, Y_NORM + 2):
                    act.wait_ge(y_gated, 4)
                    square(1, (s - Y_NORM) // 2, xt)
                if s == Y_NORM + 6:
                    root(1)

            def beside(s):
                if s < 56:
                    beside_xbc(s)
                elif s < ATT_0 - 2:
                    beside_ssd(s)
                elif s < 232:
                    beside_att(s)
                name, b, parity = read_out(s)
                out_banks = [bank(2 * parity + t) for t in range(TT)]
                if name == "xbc":
                    xbc_rows(b, parity)
                if name in ("q", "k", "v"):
                    for t in range(TT):
                        act.activation(qkv[:, 4 * ("q", "k", "v").index(name) + b, t, :], out_banks[t],
                                       ACT.Copy).then_inc(banks_free, 1)
                if name == "z":
                    if b == 0:
                        act.wait_ge(roped, 16)
                    if b >= 2:
                        act.wait_ge(y_gated, b - 1)
                    for t in range(TT):
                        act.activation(z_tmp[:, parity, t, :], out_banks[t], ACT.Silu).then_inc(banks_free, 1)
                if name == "gates":
                    if b == 0:
                        act.wait_ge(y_done, 8)
                    if b == 4:
                        act.wait_ge(qk_turned, ATT_HEADS)
                    for t in range(TT):
                        act.activation(gates_of(b)[:, t, :], out_banks[t], ACT.Sigmoid).then_inc(banks_free, 1)
                due = turn_step(s, 2)
                if due:
                    turn(*due)
                if s in (X_NORM, X_NORM + 2):
                    act.wait_ge(banks_free, 4 + 2 * FIRST["peer_q"])
                    square(2, (s - X_NORM) // 2, x1)
                if s == X_NORM + 6:
                    root(2)
                if name == "peer_q":
                    pq_rows(b, parity)

            def pq_rows(b, parity):
                if b == 0:
                    act.wait_ge(head_ms, 18)
                for m in range(2):
                    act.activation(pq[:, 4 * b + 2 * m:4 * b + 2 * m + 2, :],
                                   bank(2 * parity + m).rearrange("p (m s) -> p m s", m=2), ACT.Copy)\
                        .then_inc(banks_free, 1)

            for n in range(AHEAD):
                hi(n)
            for t in range(TT):
                act.wait_ge(x_in, 32)
                square(0, t, x_sb)
            root(0)
            act.wait_ge(small_in, 64)
            for m in range(8):
                turn(0, m)

            for s in range(8 * FIRST["ple_gate"]):
                hi(s + AHEAD)
                beside(s)
            act.wait_ge(used, RING + 8 * FIRST["ple_gate"])
            pq_rows(3, 1)

            for t in range(TT):
                act.wait_ge(key_sum, t + 1)
                if t == 0:
                    act.wait_ge(h2_ready, 1)
                act.activation(key_scores[t], bank(4 * t, 4).rearrange("p (n k) -> p n k", n=KC), ACT.Copy,
                               scale=stat[:, 2, 3, t:t + 1]).then_inc(key_out, 1)
            for t in range(TT):
                act.wait_ge(top_sub, t + 1)
                act.activation(gate[:, t, :], gate[:, t, :], ACT.Exp).then_inc(top_exp, 1)
            for b in range(D // NB):
                act.wait_ge(ple_sum, b + 1)
                act.activation(up_sb[:, b], tiles(bank(2 * (b % 2), 2)), ACT.Copy).then_inc(ple_out, 1)

            def turn5(t):
                for m in range(4):
                    act.wait_ge(turned, 40 + 4 * t + m + 1)
                    for c in range(4):
                        ins = act.activation(act_hi[:, 4 * m + c, t * P:(t + 1) * P],
                                             bank(4 + m)[:, c * P:(c + 1) * P], ACT.Copy,
                                             scale=gain(5, 4 * m + c))
                    ins.then_inc(turned_hi, 1)

            for t in range(TT):
                act.wait_ge(row_free, SLOTS + (2 * t + 1) * PICKS)
                act.activation(dots[:, t, :], dots[:, t, :], ACT.Gelu).then_inc(gelued, 1)
                if t == 0:
                    act.wait_ge(row_free, SLOTS + 2 * PICKS)
                    turn5(0)
            act.wait_ge(row_free, SLOTS + 4 * PICKS)
            turn5(1)
            square(3, 0, x1)
            square(3, 1, x1)
            for s in range(8 * FIRST["ple_gate"], PIECES + 8):
                if s + AHEAD < PIECES:
                    hi(s + AHEAD)
                if s == 8 * FIRST["ple_gate"] + 3:
                    root(3)
                name, b, parity = read_out(s, 1)
                if name == "ple_gate":
                    act.wait_ge(used, RING + 8 * (s // 8))
                    if b == 0:
                        act.wait_ge(means, 5)
                    if b >= 2:
                        act.wait_ge(out_ready, b - 1)
                    for t in range(TT):
                        act.activation(g_ple[:, parity, t, :], bank(2 * parity + t), ACT.Sigmoid,
                                       scale=stat[:, 3, 3, t:t + 1]).then_inc(banks_free, 1)

        @block.vector
        def _(dve):
            own = Steps(dve, own_dve)
            dve.sem_inc(row_free, SLOTS)

            def step(ins):
                own.mark(ins)
                own.wait()

            def lo(n):
                dve.wait_ge(hi_split, n + 1)
                dve.tensor_tensor(w_lo[:, n % RING, :], w_raw[:, n % RING, :],
                                  w_hi[:, n % RING, :].bitcast(F32), ALU.subtract).then_inc(lo_split, 1)

            def mean(k):
                dve.wait_ge(squares, k + 1)
                dve.tensor_scalar(stat[:, k, 1, :], stat[:, k, 0, :], 1.0 / D, EPS, ALU.mult, ALU.add)\
                    .then_inc(means, 1)

            def inverse(k):
                dve.wait_ge(roots, k + 1)
                step(dve.reciprocal(stat[:, k, 3, :], stat[:, k, 2, :]))

            def gain(k, c):
                at = GA if k == 2 else {0: G1, 1: GS, 4: G2, 5: G3}[k] + c
                return colc[:, at:at + 1]

            def turn(k, m):
                dve.wait_ge(turned_hi, 8 * k + m + 1)
                if k == 3:
                    dve.tensor_tensor(act_lo[:, 2 * m:2 * m + 2, :],
                                      bank(4 + m % 4).rearrange("p (c s) -> p c s", c=2),
                                      act_hi[:, 2 * m:2 * m + 2, :].bitcast(F32), ALU.subtract)\
                        .then_inc(turned_lo, 1)
                    return
                for c in range(2):
                    ins = dve.scalar_tensor_tensor(
                        out=act_lo[:, 2 * m + c, :], in0=bank(4 + m % 4)[:, c * S:(c + 1) * S],
                        scalar=gain(k, 2 * m + c), in1=act_hi[:, 2 * m + c, :].bitcast(F32),
                        op0=ALU.mult, op1=ALU.subtract)
                ins.then_inc(turned_lo, 1)

            def dt_before():
                dve.wait_ge(dt_sum, 1)
                step(dve.tensor_tensor(dtt[:, 0, :].rearrange("p (t h) -> p t h", t=TT),
                                       bank(4)[:, 0:TT * 64].rearrange("p (t h) -> p t h", t=TT),
                                       rowc[:, R_DTB:R_DTB + 64].unsqueeze(1).to_broadcast([P, TT, 64]),
                                       ALU.add))
                dve.scalar_tensor_tensor(out=dtt[:, 1, :], in0=dtt[:, 0, :], scalar=-1.0, in1=dtt[:, 0, :],
                                         op0=ALU.mult, op1=ALU.max).then_inc(dt_abs, 1)

            def dt_and_a():
                dve.wait_ge(dt_exp, 2)
                s_, s2, p_ = dtt[:, 2, :], dtt[:, 3, :], dtt[:, 4, :]
                step(dve.tensor_scalar(s2, dtt[:, 1, :], 2.0, None, ALU.add))
                step(dve.reciprocal(p_, s2))
                step(dve.tensor_tensor(s_, dtt[:, 1, :], p_, ALU.mult))
                step(dve.tensor_tensor(s2, s_, s_, ALU.mult))
                step(dve.tensor_scalar(p_, s2, 1.0 / 17, None, ALU.mult))
                for k in range(7, 0, -1):
                    step(dve.scalar_tensor_tensor(out=p_, in0=p_, scalar=1.0 / (2 * k + 1), in1=s2,
                                                  op0=ALU.add, op1=ALU.mult))
                step(dve.scalar_tensor_tensor(out=p_, in0=p_, scalar=1.0, in1=s_, op0=ALU.add, op1=ALU.mult))
                step(dve.tensor_scalar(s2, dtt[:, 0, :], 0.0, None, ALU.max))
                step(dve.scalar_tensor_tensor(out=dtv.rearrange("p t h -> p (t h)"), in0=p_, scalar=2.0,
                                              in1=s2, op0=ALU.mult, op1=ALU.add))
                for t in range(TT):
                    ins = dve.scalar_tensor_tensor(out=av[:, t, :], in0=dtv[:, t, :], scalar=-1.0,
                                                   in1=aexp, op0=ALU.mult, op1=ALU.mult)
                ins.then_inc(a_ready, 1)

            def rotary_angles(k):
                C1, C2 = 6.28125, 0.0019350051879882812
                C3 = 6.283185307179586 - C1 - C2
                MAGIC, PI = 1.5 * 2.0 ** 23, 3.1415925
                whole, r, turns = ang[:, 4], ang[:, k], ang[:, 2 + k]
                if k == 0:
                    step(dve.tensor_copy(posf, pos_i[:, :]))
                    for t in range(TT):
                        own.mark(dve.tensor_scalar(ang[:, 4, t, :], rowc[:, R_INV:R_INV + 32],
                                                   posf[:, t:t + 1], None, ALU.mult))
                    own.wait()
                step(dve.tensor_scalar(turns, whole, 1.0 / 6.283185307179586, 0.25 * k, ALU.mult, ALU.add))
                step(dve.tensor_scalar(turns, turns, MAGIC, None, ALU.add))
                step(dve.tensor_scalar(turns, turns, -MAGIC, None, ALU.add))
                for c, src in ((C1, whole), (C2, r), (C3, r)):
                    step(dve.scalar_tensor_tensor(out=r, in0=turns, scalar=-c, in1=src, op0=ALU.mult,
                                                  op1=ALU.add))
                if k:
                    step(dve.tensor_scalar(r, r, 1.5707963267948966, None, ALU.add))
                ins = dve.tensor_scalar(r, r, PI, -PI, ALU.min, ALU.max)
                if k:
                    ins.then_inc(angles, 1)
                else:
                    step(ins)

            def lambda_sums():
                step(dve.tensor_tensor(lamp, rowc[:, R_LAM:R_LAM + 128].rearrange("p (k d) -> p k d", k=2),
                                       rowc[:, R_LAM + 128:R_LAM + 256].rearrange("p (k d) -> p k d", k=2),
                                       ALU.mult))
                dve.tensor_reduce(lam[:, 0:2], lamp, AX.X, ALU.add).then_inc(lam_sum, 1)

            def trigonometry():
                dve.wait_ge(sines, 1)
                for w, base in ((0, R_QG), (1, R_KG)):
                    for t in range(TT):
                        for half in range(2):
                            g_ = rowc[:, base + 32 * half:base + 32 * half + 32]
                            own.mark(dve.tensor_tensor(trig[:, w, t, 0, 32 * half:32 * half + 32],
                                                       ang[:, 1, t, :], g_, ALU.mult))
                            own.mark(dve.tensor_tensor(trig[:, w, t, 1, 32 * half:32 * half + 32],
                                                       ang[:, 0, t, :], g_, ALU.mult))
                dve.wait_ge(lam_exp, 1)
                step(dve.tensor_tensor(lam[:, 2:3], lam[:, 1:2], lam[:, 0:1], ALU.subtract))
                step(dve.tensor_scalar(lam[:, 3:4], lam[:, 2:3], -LAM_INIT, None, ALU.add))

            def conv_chunk(b, m):
                dve.wait_ge(banks_free, 4 + 2 * b + 2)
                if b >= 2:
                    dve.wait_ge(silued, b - 1)
                k, ch = 4 * (b % 2) + m, 4 * b + m
                for tap in range(CONV_K):
                    w = colc[:, CW + CONV_K * ch + tap:CW + CONV_K * ch + tap + 1]
                    if tap == 0:
                        ins = dve.tensor_scalar(conv[:, k, :], pad[:, k, 0:S], w,
                                                colc[:, CB + ch:CB + ch + 1], ALU.mult, ALU.add)
                    else:
                        own.wait()
                        ins = dve.scalar_tensor_tensor(out=conv[:, k, :], in0=pad[:, k, tap:tap + S],
                                                       scalar=w, in1=conv[:, k, :],
                                                       op0=ALU.mult, op1=ALU.add)
                    if tap == CONV_K - 1 and m == 3:
                        ins.then_inc(conved, 1)
                    else:
                        own.mark(ins)

            def beside_xbc(s):
                if s == 0:
                    dt_before()
                if s == 3:
                    dt_and_a()
                if s == 8:
                    rotary_angles(0)
                if s == 9:
                    lambda_sums()
                if s == 10:
                    rotary_angles(1)
                if s == 15:
                    dve.wait_ge(dec_exp, 1)
                    for t in range(TT):
                        ins = dve.tensor_tensor(dd[:, t, :], dtv[:, t, 32 * t:32 * t + 32], ex[:, 2 + t, :],
                                                ALU.mult)
                    ins.then_inc(decayed, 1)
                if s == 24:
                    trigonometry()
                if s > 8 and 3 <= s % 8 <= 6:
                    conv_chunk(s // 8 - 1, s % 8 - 3)

            def heads(v):
                return v.rearrange("p (h d) -> p h d", h=HPG)

            def per_head(v):
                return v.unsqueeze(2).to_broadcast([P, HPG, SSD_DIM])

            def outputs(n):
                g, c = n // TT, n % TT
                dve.wait_ge(y_sum, n + 1)
                step(dve.tensor_tensor(heads(ytmp), heads(bank(7)), per_head(ex[:, c, g * HPG:(g + 1) * HPG]),
                                       ALU.mult))
                step(dve.tensor_tensor(ytmp, ytmp, bank(6), ALU.add))
                dve.wait_ge(skip_ready, n + 1)
                dve.tensor_tensor(xt[:, c, g * NB:(g + 1) * NB], ytmp, xsk, ALU.add).then_inc(y_done, 1)

            def decayed_cb(n, r):
                dve.wait_ge(seg_exp, 2 * n + r + 1)
                dve.tensor_tensor(em[:, r], em[:, r], cbm[:, r, :].unsqueeze(1).to_broadcast([P, HPG, P]),
                                  ALU.mult).then_inc(em_ready, 1)

            def eight(v):
                return v.rearrange("p (h d) -> p h d", h=8)

            def head_norm(n):
                dve.wait_ge(head_sq, n + 1)
                step(dve.tensor_reduce(hstat[:, 0, 0:8], eight(sq), AX.X, ALU.add))
                dve.tensor_scalar(hstat[:, 1, 0:8], hstat[:, 0, 0:8], 1.0 / ATT_DIM, EPS,
                                  ALU.mult, ALU.add).then_inc(head_ms, 1)

            def rope(n):
                v = head_src(n)
                dve.wait_ge(head_rt, n + 1)
                step(dve.reciprocal(hstat[:, 3, 0:8], hstat[:, 2, 0:8]))
                step(dve.tensor_tensor(eight(v), eight(v),
                                       hstat[:, 3, 0:8].unsqueeze(2).to_broadcast([P, 8, ATT_DIM]), ALU.mult))
                for k in range(2):
                    tr = trig[:, n // 8, n % 2, k, :]
                    own.mark(dve.tensor_tensor(eight(rot[:, k, :]), eight(v),
                                               tr.unsqueeze(1).to_broadcast([P, 8, ATT_DIM]), ALU.mult))
                own.wait()
                rc, rsn = eight(rot[:, 0, :]), eight(rot[:, 1, :])
                step(dve.tensor_tensor(eight(v)[:, :, 0:32], rc[:, :, 0:32], rsn[:, :, 32:64], ALU.subtract))
                dve.tensor_tensor(eight(v)[:, :, 32:64], rc[:, :, 32:64], rsn[:, :, 0:32],
                                  ALU.add).then_inc(roped, 1)
                dve.wait_ge(roped, n + 1)

            def beside_ssd(s):
                n, at = ssd_step(s)
                if 1 <= n < 9 and at == 0:
                    outputs(n - 1)
                if 0 <= n < 8:
                    if at == 3:
                        dve.wait_ge(cb_sum, n + 1)
                        if n:
                            dve.wait_ge(em_ready, 2 * n)
                        for r, m in ((0, upper), (1, lower)):
                            ins = dve.tensor_tensor(cbm[:, r, :], bank(7)[:, 0:P], m[:, :], ALU.mult)
                        ins.then_inc(cb_out, 1)
                        dve.wait_ge(cb_out, n + 1)
                    if at == 4:
                        decayed_cb(n, 0)
                    if at == 7:
                        decayed_cb(n, 1)
                n, at = norm_step(s)
                if 0 <= n < 16:
                    if at == 1:
                        head_norm(n)
                    if at == 3:
                        rope(n)

            def maxima(h):
                dve.wait_ge(scored, h + 1)
                for j in range(2):
                    own.mark(dve.tensor_reduce(mx[:, h % 2, 2 * j:2 * j + 2], tiles(bank(5 + j)), AX.X,
                                               ALU.max))
                own.wait()
                if h >= 2:
                    dve.wait_ge(expd, h - 1)
                dve.tensor_scalar(nmx[:, h % 2, :], mx[:, h % 2, :], -SCALE, None, ALU.mult).then_inc(maxed, 1)

            def combine(h):
                dve.wait_ge(expd, h + 1)
                step(dve.reciprocal(ri[:, h % 2, :], rs[:, h % 2, :]))
                step(dve.tensor_scalar(ri[:, h % 2, 2:4], ri[:, h % 2, 2:4], lam[:, 3:4], None, ALU.mult))
                if h:
                    dve.wait_ge(att_ready, h)
                for t in range(TT):
                    own.mark(dve.tensor_scalar(att_x[:, t, :], prob[:, h % 2, 2 + t, :],
                                               ri[:, h % 2, 2 + t:3 + t], None, ALU.mult))
                own.wait()
                if h >= 2:
                    dve.wait_ge(att_turned, h - 1)
                for t in range(TT):
                    ins = dve.scalar_tensor_tensor(out=att[:, h % 2, t, :], in0=prob[:, h % 2, t, :],
                                                   scalar=ri[:, h % 2, t:t + 1], in1=att_x[:, t, :],
                                                   op0=ALU.mult, op1=ALU.add)
                ins.then_inc(att_ready, 1)

            def beside_att(s):
                h, at = att_step(s)
                if 2 <= h < 18 and at == 0:
                    dve.wait_ge(o_sum, h - 1)
                    dve.tensor_copy(qkv[:, (h - 2) // 4, :, ((h - 2) % 4) * P:((h - 2) % 4 + 1) * P],
                                    tiles(bank(7)[:, 0:S])).then_inc(o_done, 1)
                if 0 <= h < 16 and at == 1:
                    maxima(h)
                if 1 <= h < 17 and at == 2:
                    dve.wait_ge(att_turned, h)
                    if h >= 3:
                        dve.wait_ge(o_sum, h - 2)
                    dve.tensor_copy(att_t[:, (h - 1) % 2, :], bank(4)).then_inc(att_out, 1)
                if 0 <= h < 16 and at == 3:
                    combine(h)
                t, at = (s - O_NORM) // 4, (s - O_NORM) % 4
                if 0 <= t < TT and at == 1:
                    dve.wait_ge(head_sq, 17 + t)
                    step(dve.tensor_reduce(hstat[:, 0, :], o_sq.rearrange("p (h d) -> p h d", h=ATT_HEADS),
                                           AX.X, ALU.add))
                    dve.tensor_scalar(hstat[:, 1, :], hstat[:, 0, :], 1.0 / P, EPS, ALU.mult, ALU.add)\
                        .then_inc(head_ms, 1)
                if 0 <= t < TT and at == 3:
                    dve.wait_ge(head_rt, 17 + t)
                    step(dve.reciprocal(hstat[:, 3, :], hstat[:, 2, :]))
                    step(dve.tensor_scalar(hstat[:, 3, :], hstat[:, 3, :], 1.0 - LAM_INIT, None, ALU.mult))
                    o = qkv[:, 0:4, t, :].rearrange("p b (h d) -> p b h d", h=4)
                    scales = hstat[:, 3, :].rearrange("p (b h) -> p b h", b=4)
                    for b in range(4):
                        ins = dve.tensor_tensor(o[:, b], o[:, b],
                                                scales[:, b].unsqueeze(2).to_broadcast([P, 4, P]), ALU.mult)
                        if b < 3:
                            own.mark(ins)
                    ins.then_inc(o_ready, 1)
                if s == Y_NORM + 4:
                    mean(1)
                if s == Y_NORM + 7:
                    inverse(1)

            def beside(s):
                if s < 56:
                    beside_xbc(s)
                elif s < ATT_0 - 2:
                    beside_ssd(s)
                elif s < 232:
                    beside_att(s)
                name, b, parity = read_out(s, 2)
                if name == "z":
                    dve.wait_ge(banks_free, 4 + 2 * (FIRST["z"] + b + 1))
                    y = xt[:, :, b * NB:(b + 1) * NB]
                    dve.tensor_tensor(y, y, z_tmp[:, parity], ALU.mult).then_inc(y_gated, 1)
                name, b, parity = read_out(s)
                out_banks = [bank(2 * parity + t) for t in range(TT)]
                if name in ("ssd_out", "att_out", "w_out"):
                    dve.wait_ge(used, RING + 8 * (s // 8))
                if name == "ssd_out":
                    for t in range(TT):
                        dve.scalar_tensor_tensor(out=mixed[:, b, t, :], in0=out_banks[t],
                                                 scalar=stat[:, 1, 3, t:t + 1], in1=mixed[:, b, t, :],
                                                 op0=ALU.mult, op1=ALU.mult).then_inc(banks_free, 1)
                if name == "att_out":
                    for t in range(TT):
                        dve.tensor_tensor(g_att[:, b, t, :], g_att[:, b, t, :], out_banks[t], ALU.mult)\
                            .then_inc(banks_free, 1)
                    dve.wait_ge(banks_free, 4 + 2 * (FIRST["att_out"] + b + 1))
                    dve.tensor_tensor(mixed[:, b], mixed[:, b], g_att[:, b], ALU.add).then_inc(mixed_ready, 1)
                if name == "w_out":
                    if b == 0:
                        dve.wait_ge(x_again, 32)
                    for t in range(TT):
                        xb = x1[:, t, b * NB:(b + 1) * NB]
                        dve.tensor_tensor(xb, xb, out_banks[t], ALU.add).then_inc(banks_free, 1)
                due = turn_step(s, 2)
                if due:
                    turn(*due)
                if s == X_NORM + 4:
                    mean(2)
                if s == X_NORM + 8:
                    inverse(2)
                if s in (X_NORM + 10, X_NORM + 12):
                    t = (s - X_NORM - 10) // 2
                    dve.wait_ge(g2_in, 16)
                    ins = dve.scalar_tensor_tensor(out=h2[:, t, :], in0=x1[:, t, :],
                                                   scalar=stat[:, 2, 3, t:t + 1], in1=g2_sb,
                                                   op0=ALU.mult, op1=ALU.mult)
                    if t:
                        ins.then_inc(h2_ready, 1)

            for b in range(2):
                dve.memset(pad[:, 4 * b:4 * b + 4, :], 0.0).then_inc(pad_zero, 1)
            for n in range(AHEAD):
                lo(n)
            mean(0)
            inverse(0)
            for t in range(TT):
                ins = dve.tensor_scalar(x_sb[:, t, :], x_sb[:, t, :], stat[:, 0, 3, t:t + 1], None, ALU.mult)
            ins.then_inc(h_ready, 1)
            dve.wait_ge(small_in, 64)
            for m in range(8):
                turn(0, m)

            for s in range(8 * FIRST["ple_gate"]):
                lo(s + AHEAD)
                beside(s)

            step(dve.tensor_copy(iota_f[:, :], iota_i[:, :]))

            def top16(n, src, vals, idx):
                for r in range(2):
                    for k in range(n):
                        own.mark(dve.max(vals[:, k, 8 * r:8 * r + 8], src[:, k, :]))
                    own.wait()
                    for k in range(n):
                        own.mark(dve.max_index(idx[:, k, 8 * r:8 * r + 8], vals[:, k, 8 * r:8 * r + 8],
                                               src[:, k, :]))
                    own.wait()
                    if r == 0:
                        for k in range(n):
                            own.mark(dve.match_replace(src[:, k, :], vals[:, k, 0:8], src[:, k, :], LOWEST))
                        own.wait()

            for t in range(TT):
                dve.wait_ge(key_out, t + 1)
                top16(KC, key_scores[t], v16, i16)
                step(dve.tensor_copy(i16f, i16))
                vv = v16.rearrange("p (h k) c -> p h k c", k=2)
                c4 = cand.rearrange("p h (a b) -> p h a b", a=TOPK)
                step(dve.tensor_tensor(c4, vv[:, :, 0, :].unsqueeze(3).to_broadcast([P, EXPERT_HEADS, TOPK, TOPK]),
                                       vv[:, :, 1, :].unsqueeze(2).to_broadcast([P, EXPERT_HEADS, TOPK, TOPK]),
                                       ALU.add))
                top16(EXPERT_HEADS, cand, sc16, ps16)
                g3 = gate[:, t, :].rearrange("p (h k) -> p h k", h=EXPERT_HEADS)
                dve.tensor_tensor(g3, sc16, sc16[:, :, 0:1].to_broadcast([P, EXPERT_HEADS, TOPK]),
                                  ALU.subtract).then_inc(top_sub, 1)
                pos16 = ps16.rearrange("p h k -> p (h k)").bitcast(I32)
                pk = picks[:, t, :]
                for k in range(2):
                    if k == 0:
                        step(dve.tensor_scalar(pk, pos16, 4, None, ALU.logical_shift_right))
                    else:
                        step(dve.tensor_scalar(pk, pos16, TOPK - 1, None, ALU.bitwise_and))
                    step(dve.tensor_copy(psf[:, k, :], pk))
                    step(dve.tensor_tensor(onehot, psf[:, k, :].unsqueeze(2).to_broadcast([P, PICKS, TOPK]),
                                           iota_f[:, :].unsqueeze(1).to_broadcast([P, PICKS, TOPK]),
                                           ALU.is_equal))
                    oh = onehot.rearrange("p (h k) c -> p h k c", h=EXPERT_HEADS)
                    ii = i16f.rearrange("p (h k) c -> p h k c", k=2)[:, :, k, :]
                    step(dve.tensor_tensor(oh, oh, ii.unsqueeze(2).to_broadcast([P, EXPERT_HEADS, TOPK, TOPK]),
                                           ALU.mult))
                    step(dve.tensor_reduce(ef[:, k, :], onehot, AX.X, ALU.add))
                step(dve.scalar_tensor_tensor(out=psf[:, 0, :], in0=ef[:, 0, :], scalar=float(NKEYS),
                                              in1=ef[:, 1, :], op0=ALU.mult, op1=ALU.add))
                dve.tensor_copy(pk, psf[:, 0, :]).then_inc(picked, 1)
                dve.wait_ge(picked, t + 1)
                dve.wait_ge(top_exp, t + 1)
                step(dve.tensor_reduce(esum[:, 0, :], g3, AX.X, ALU.add))
                step(dve.reciprocal(esum[:, 1, :], esum[:, 0, :]))
                step(dve.tensor_tensor(g3, g3, esum[:, 1, :].unsqueeze(2).to_broadcast([P, EXPERT_HEADS, TOPK]),
                                       ALU.mult))

            def turn5(t):
                for m in range(4):
                    dve.wait_ge(turned_hi, 40 + 4 * t + m + 1)
                    for c in range(4):
                        ins = dve.scalar_tensor_tensor(
                            out=act_lo[:, 4 * m + c, t * P:(t + 1) * P], in0=bank(4 + m)[:, c * P:(c + 1) * P],
                            scalar=gain(5, 4 * m + c),
                            in1=act_hi[:, 4 * m + c, t * P:(t + 1) * P].bitcast(F32),
                            op0=ALU.mult, op1=ALU.subtract)
                    ins.then_inc(turned_lo, 1)

            rows_used = 0
            for t in range(TT):
                with dve.Fori(0, PICKS // SLOTS) as i:
                    for s in range(SLOTS):
                        dve.wait_ge(row_in[s], 16 * (rows_used // SLOTS) + 16 * i + 16)
                        dve.scalar_tensor_tensor(out=slot[:, s, :], in0=slot[:, s, :], scalar=1.0,
                                                 in1=h2[:, t, :], op0=ALU.mult, op1=ALU.mult,
                                                 accum_out=dots[:, t, bass.ds(i * SLOTS + s, 1)])\
                            .then_inc(row_free, 1)
                rows_used += PICKS
                dve.wait_ge(gelued, t + 1)
                step(dve.tensor_tensor(dots[:, t, :], dots[:, t, :], gate[:, t, :], ALU.mult))
                with dve.Fori(0, PICKS // SLOTS) as i:
                    for s in range(SLOTS):
                        dve.wait_ge(row_free, SLOTS + rows_used + SLOTS * i + s)
                        dve.wait_ge(row_in[s], 16 * (rows_used // SLOTS) + 16 * i + 16)
                        dve.scalar_tensor_tensor(out=x1[:, t, :], in0=slot[:, s, :],
                                                 scalar=dots[:, t, bass.ds(i * SLOTS + s, 1)],
                                                 in1=x1[:, t, :], op0=ALU.mult, op1=ALU.add)\
                            .then_inc(row_free, 1)
                rows_used += PICKS
                turn5(t)

            for s in range(8 * FIRST["ple_gate"], PIECES + 8):
                if s + AHEAD < PIECES:
                    lo(s + AHEAD)
                if s == 8 * FIRST["ple_gate"] + 2:
                    mean(3)
                if s == 8 * FIRST["ple_gate"] + 5:
                    dve.wait_ge(roots, 4)
                    dve.reciprocal(stat[:, 3, 3, :], stat[:, 3, 2, :]).then_inc(means, 1)
                name, b, parity = read_out(s, 2)
                if name == "ple_gate":
                    dve.wait_ge(banks_free, 4 + 2 * (s // 8))
                    dve.wait_ge(ple_out, b + 1)
                    step(dve.tensor_tensor(g_ple[:, parity], g_ple[:, parity], up_sb[:, b], ALU.mult))
                    xs = x1[:, :, b * NB:(b + 1) * NB]
                    dve.tensor_tensor(xs, xs, g_ple[:, parity], ALU.add).then_inc(out_ready, 1)

        @block.tensor
        def _(pe):
            def mm(out_, lhs, rhs, start, stop, shared=False):
                return nc.tensor.matmul(out_, lhs, rhs, start=start, stop=stop, skip_group_check=shared)

            def source(k, t, c):
                if k == 0:
                    return x_sb[:, t, c * P:(c + 1) * P]
                if k == 1:
                    return xt[:, t, c * P:(c + 1) * P]
                if k == 2:
                    return qkv[:, c // 4, t, (c % 4) * P:(c % 4 + 1) * P]
                if k == 3:
                    return mixed[:, c // 4, t, (c % 4) * P:(c % 4 + 1) * P]
                return x1[:, t, c * P:(c + 1) * P]

            def turn(k, m):
                if k == 0 and m == 0:
                    pe.wait_ge(h_ready, 1)
                if k == 1 and m == 0:
                    pe.wait_ge(y_gated, 4)
                    pe.wait_ge(o_done, ATT_HEADS)
                if k == 2 and m == 0:
                    pe.wait_ge(o_ready, 2)
                if k == 3:
                    pe.wait_ge(mixed_ready, m // 2 + 1)
                if k == 4:
                    pe.wait_ge(banks_free, 4 + 2 * (FIRST["w_out"] + m // 2 + 1))
                if 8 * k + m >= 4:
                    pe.wait_ge(turned_lo, 8 * k + m - 3)
                for c in range(2):
                    for t in range(TT):
                        ins = pe.transpose(bank(4 + m % 4)[:, c * S + t * P:c * S + (t + 1) * P],
                                           source(k, t, 2 * m + c), ident[:, :])
                ins.then_inc(turned, 1)

            def products(s):
                b, j = s // 8, s % 8
                name = [m for m, k in STAGES if FIRST[m] <= b][-1]
                if j == 0:
                    pe.wait_ge(banks_free, 2 * b + 2)
                for k, first in TURNS.items():
                    if b == first:
                        pe.wait_ge(turned_lo, 8 * k + j + 1)
                if name == "ple_gate" and b == FIRST[name]:
                    pe.wait_ge(turned_lo, 44 + j // 2 + 1)
                pe.wait_ge(lo_split, s + 1)
                for cc in range(2):
                    c = 2 * j + cc
                    wh = w_hi[:, s % RING, cc * NB:(cc + 1) * NB]
                    wl = w_lo[:, s % RING, cc * NB:(cc + 1) * NB]
                    if name in ("xbc", "peer_q"):
                        for m in range(4):
                            o = bank(2 * (b % 2) + m // 2)[:, (m % 2) * S:(m % 2 + 1) * S]
                            cut = slice(m * P, (m + 1) * P)
                            mm(o, wh[:, cut], act_hi[:, c, :], c == 0 and m % 2 == 0, False, True)
                            mm(o, wh[:, cut], act_lo[:, c, :], False, False, True)
                            ins = mm(o, wl[:, cut], act_hi[:, c, :], False, c == KC - 1, True)
                    else:
                        for t in range(TT):
                            o, cut = bank(2 * (b % 2) + t), slice(t * P, (t + 1) * P)
                            mm(o, act_hi[:, c, cut], wh, c == 0, False)
                            mm(o, act_hi[:, c, cut], wl, False, False)
                            ins = mm(o, act_lo[:, c, cut], wh, False, c == KC - 1)
                ins.then_inc(used, 1)

            def dt_products():
                pe.wait_ge(turned_lo, 8)
                pe.wait_ge(small_in, 64)
                for t in range(TT):
                    for c in range(KC):
                        for part, a in enumerate((act_hi, act_lo)):
                            ins = mm(bank(4)[:, t * 64:(t + 1) * 64], a[:, c, t * P:(t + 1) * P].bitcast(F32),
                                     wdt_sb[:, c, :], c == 0 and part == 0, c == KC - 1 and part == 1)
                ins.then_inc(dt_sum, 1)

            def beside_ssd(s):
                if s == 8:
                    pe.wait_ge(a_ready, 1)
                    for k, (m, t, r) in enumerate(((lower, 0, 1), (upper, 1, 0), (below, 0, 0), (above, 1, 1))):
                        ins = mm(bank(4)[:, 32 * k:32 * k + 32], m[:, :], av[:, t, 32 * r:32 * r + 32],
                                 True, True)
                    ins.then_inc(dec_sum, 1)
                for m in (2 * (s - XT_0), 2 * (s - XT_0) + 1):
                    if 0 <= m < 10:
                        if m == 0:
                            pe.wait_ge(silued, 6)
                            pe.wait_ge(dec_exp, 1)
                        if m >= 4:
                            pe.wait_ge(xt_out, m - 3)
                        t, q = m % 2, m // 2
                        for c in range(4):
                            ins = pe.transpose(bank(4 + m % 4)[:, c * P:(c + 1) * P],
                                               xbc[:, 4 * q + c, t * P:(t + 1) * P], ident[:, :])
                        ins.then_inc(xt_turned, 1)
                n, at = ssd_step(s)
                if not 0 <= n < 8:
                    return
                g, c = n // TT, n % TT
                if at in (0, 4):
                    r = at // 4
                    pe.wait_ge(rh_ready, 2 * n + r + 1)
                    if n or r:
                        pe.wait_ge(seg_exp, 2 * n + r)
                    else:
                        pe.wait_ge(xt_out, 10)
                    for q in range(2):
                        ins = mm(bank(4 + q), (below, above)[r][:, :],
                                 rh[:, r, 4 * q:4 * q + 4, :].rearrange("p h l -> p (h l)"), True, True)
                    ins.then_inc(seg_sum, 1)
                if at == 2:
                    if n:
                        pe.wait_ge(y_done, n)
                    mm(bank(7)[:, 0:P], xbc[:, 16 + g, c * P:(c + 1) * P],
                       xbc[:, 20 + g, c * P:(c + 1) * P], True, True).then_inc(cb_sum, 1)
                if at == 5:
                    pe.wait_ge(cb_out, n + 1)
                    pe.wait_ge(xd_ready, n + 1)
                    mm(bank(7), bt[:, 1 - c, g * P:(g + 1) * P], xd[:, 1 - c, :], True, True)\
                        .then_inc(state_sum, 1)
                if at == 9:
                    pe.wait_ge(em_ready, 2 * n + 2)
                    pe.wait_ge(xf_ready, 2 * n + 2)
                    for h in range(HPG):
                        for r in range(2):
                            mm(bank(6)[:, h * SSD_DIM:(h + 1) * SSD_DIM], em[:, r, h, :],
                               xf[:, r, h * SSD_DIM:(h + 1) * SSD_DIM], r == 0, r == 1)
                    pe.wait_ge(state_out, n + 1)
                    mm(bank(7), xbc[:, 20 + g, c * P:(c + 1) * P], hs, True, True).then_inc(y_sum, 1)

            def turn_qk(h):
                if h == 0:
                    pe.wait_ge(roped, 16)
                    pe.wait_ge(y_done, 8)
                if h == 1:
                    pe.wait_ge(qk_out, 1)
                if h >= 2:
                    pe.wait_ge(qk_out, h)
                if h >= 3:
                    pe.wait_ge(att_out, h - 2)
                for w in range(2):
                    for t in range(TT):
                        ins = pe.transpose(bank(4)[:, w * S + t * P:w * S + (t + 1) * P],
                                           head_cols(w, t, h), ident[:, :])
                ins.then_inc(qk_turned, 1)

            def scores(h):
                pe.wait_ge(qk_out, h + 1)
                if h:
                    pe.wait_ge(expd, h)
                for j in range(2):
                    rows_j = slice(ATT_DIM * j, ATT_DIM * (j + 1))
                    for t in range(TT):
                        ins = mm(bank(5 + j)[:, t * S:(t + 1) * S],
                                 qkt[rows_j, h % 2, t * P:(t + 1) * P], qkt[rows_j, h % 2, S:2 * S], True, True)
                ins.then_inc(scored, 1)

            def turn_att(h):
                pe.wait_ge(att_ready, h + 1)
                pe.wait_ge(qk_out, min(h + 3, ATT_HEADS))
                for t in range(TT):
                    for kc in range(2):
                        ins = pe.transpose(bank(4)[:, kc * S + t * P:kc * S + (t + 1) * P],
                                           att[:, h % 2, t, kc * P:(kc + 1) * P], ident[:, :])
                ins.then_inc(att_turned, 1)

            def times_v(h):
                pe.wait_ge(att_out, h + 1)
                if h:
                    pe.wait_ge(o_done, h)
                for t in range(TT):
                    for kc in range(2):
                        ins = mm(bank(7)[:, t * P:(t + 1) * P],
                                 att_t[:, h % 2, kc * S + t * P:kc * S + (t + 1) * P],
                                 head_cols(2, kc, h), kc == 0, kc == 1)
                ins.then_inc(o_sum, 1)

            def beside_att(s):
                if s == ATT_0 - 3:
                    turn_qk(0)
                if s == ATT_0 - 1:
                    turn_qk(1)
                h, at = att_step(s)
                if 0 <= h < 16 and at == 0:
                    scores(h)
                if 1 <= h < 17 and at == 1:
                    turn_att(h - 1)
                if 1 <= h < 17 and at == 3:
                    times_v(h - 1)
                if 0 <= h < 14 and at == 3:
                    turn_qk(h + 2)

            pe.wait_ge(masks, 6)
            for m in range(8):
                turn(0, m)
            dt_products()
            for s in range(8 * FIRST["ple_gate"]):
                products(s)
                if s < ATT_0 - 3:
                    beside_ssd(s)
                else:
                    beside_att(s)
                due = turn_step(s, 0)
                if due:
                    turn(*due)

            pe.wait_ge(keys_in, 16)
            pe.wait_ge(banks_free, 4 + 2 * FIRST["ple_gate"])
            for t in range(TT):
                for n in range(KC):
                    ins = mm(bank(4 * t + n // 4)[:, (n % 4) * NKEYS:(n % 4 + 1) * NKEYS],
                             pq[:, n, t * P:(t + 1) * P], keys_sb[:, n, :], True, True)
                ins.then_inc(key_sum, 1)

            pe.wait_ge(ple_in, 32)
            pe.wait_ge(key_out, 2)
            for b in range(D // NB):
                if b >= 2:
                    pe.wait_ge(ple_out, b - 1)
                for t in range(TT):
                    for c in range(2):
                        ins = mm(bank(2 * (b % 2) + t), pt_sb[:, c, t * P:(t + 1) * P],
                                 up_sb[:, b, c, :], c == 0, c == 1)
                ins.then_inc(ple_sum, 1)
            for t in range(TT):
                pe.wait_ge(row_free, SLOTS + 2 * (t + 1) * PICKS)
                for m in range(4):
                    if t:
                        pe.wait_ge(turned_lo, 40 + m + 1)
                    for c in range(4):
                        ins = pe.transpose(bank(4 + m)[:, c * P:(c + 1) * P], source(5, t, 4 * m + c),
                                           ident[:, :])
                    ins.then_inc(turned, 1)
            pe.wait_ge(ple_out, 4)
            for s in range(8 * FIRST["ple_gate"], PIECES):
                products(s)


def _columns(m, nblocks):
    return m.reshape(8, 2, P, nblocks, NB).transpose(3, 0, 2, 1, 4).reshape(nblocks * 8, P, PIECE)


def kernel(**inputs):
    import numpy as np
    import concourse.bacc as bacc
    from concourse.bass_utils import run_bass_kernel_spmd

    a = {k: np.asarray(v) for k, v in inputs.items()}
    w_in = a["w_in"][0]
    at = np.cumsum([0, D, XBC * P, 2 * SSD_HEADS, D, D, D, 2 * D])
    z, xbc, dt, q, k, v, gates = (w_in[:, at[n]:at[n + 1]] for n in range(7))
    parts = {"xbc": xbc, "z": z, "q": q, "k": k, "v": v, "gates": gates,
             "ssd_out": a["w_ssd_br"][0], "att_out": a["w_att_br"][0], "w_out": a["w_out"][0],
             "peer_q": a["peer_wq"][0], "ple_gate": a["ple_gate_w"][0]}
    wall = np.concatenate([_columns(parts[name], n) for name, n in STAGES])

    def chunks(g):
        return g.reshape(-1, P).T

    cols = np.concatenate([
        chunks(a["norm1_g"][0]), chunks(a["ssd_norm_g"][0]), chunks(a["norm2_g"][0]),
        chunks(a["norm3_g"][0]),
        a["subln_g"][0].reshape(P, 1),
        a["conv_w"][0].reshape(CONV_K, XBC, P).transpose(2, 1, 0).reshape(P, XBC * CONV_K),
        chunks(a["conv_b"][0])], axis=1)
    inv = (10000.0 ** (-np.arange(0, ATT_DIM, 2, dtype=np.float64) / ATT_DIM)).astype(np.float32)
    rows = np.concatenate([
        a["dt_bias_f"][0], a["dt_bias_b"][0], a["a_log_f"][0], a["a_log_b"][0], a["d_skip"][0],
        a["q_norm_g"][0], a["k_norm_g"][0], a["lam_q1"][0], a["lam_q2"][0], a["lam_k1"][0],
        a["lam_k2"][0], inv]).reshape(1, ROWS)
    arrays = {
        "x": a["x"].reshape(TT, P, D),
        "wall": wall,
        "wdt": dt.reshape(KC, P, 64).transpose(1, 0, 2).reshape(P, KC * 64),
        "cols": cols,
        "rows": rows,
        "pos": a["positions"].reshape(TT, P).T.astype(np.int32),
        "g2": a["norm2_g"].reshape(1, D),
        "keys_t": a["peer_keys"][0].transpose(3, 0, 1, 2).reshape(P, KC * NKEYS),
        "peer_u": a["peer_u"][0],
        "peer_v": a["peer_v"][0],
        "p_t": a["p"][0, 0].reshape(S, 2, P).transpose(2, 1, 0).reshape(P, 2 * S),
        "ple_up": a["ple_up_w"][0].reshape(2, P, 4, NB).transpose(1, 2, 0, 3).reshape(P, 2 * D),
    }
    arrays = {n: np.ascontiguousarray(v) for n, v in arrays.items()}
    nc = bacc.Bacc("TRN2", target_bir_lowering=False, num_devices=1)
    args = [nc.dram_tensor(n, v.shape, mybir.dt.from_np(v.dtype), kind="ExternalInput").ap()
            for n, v in arrays.items()]
    out = nc.dram_tensor("out", (TT, P, D), F32, kind="ExternalOutput").ap()
    build(nc, *args, out)
    r = run_bass_kernel_spmd(nc, [arrays], core_ids=[0])
    return r.results[0]["out"].reshape(1, S, D)
```

```python
from contextlib import ExitStack

import concourse.bass as bass
import numpy as np
from concourse import mybir

F32 = mybir.dt.float32
F32R = mybir.dt.float32r
I32 = mybir.dt.int32
U32 = mybir.dt.uint32
ALU = mybir.AluOpType
ACT = mybir.ActivationFunctionType
AX = mybir.AxisListType

P = 128
D = 2048
TT = 2
S = TT * P
KC = D // P
SSD_HEADS, SSD_DIM, GROUPS, STATE = 32, 64, 4, 128
HPG = SSD_HEADS // GROUPS
CONV_K = 5
XBC = (D + 2 * GROUPS * STATE) // P
ATT_HEADS, ATT_DIM = 16, 64
EXPERT_HEADS, NKEYS, TOPK = 8, 128, 16
PICKS = EXPERT_HEADS * TOPK
EPS = 1e-6
LAM_INIT = 0.2
SCALE = ATT_DIM ** -0.5
LOWEST = -3.0e38
SLOTS = 8

NB = 512
PIECE = 2 * NB
RING = 4
AHEAD = 2
STAGES = [("xbc", 6), ("q", 4), ("k", 4), ("v", 4), ("z", 4), ("gates", 8),
          ("ssd_out", 4), ("att_out", 4), ("w_out", 4), ("peer_q", 4), ("ple_gate", 4)]
FIRST = {}
_n = 0
for _name, _k in STAGES:
    FIRST[_name] = _n
    _n += _k
BLOCKS = _n
PIECES = 8 * BLOCKS

XT_0 = 57
SSD_0, SSD_STEP = 62, 10
NORM_0, NORM_STEP = 82, 4
ATT_0, ATT_STEP = 150, 4
O_NORM = 219
Y_NORM = 179
X_NORM = 339
KEYS_0 = 350
EARLY = [359, 361, 362, 364, 365, 367]
TURNS = {1: FIRST["ssd_out"], 2: FIRST["att_out"], 3: FIRST["w_out"], 4: FIRST["peer_q"]}

G1, GS, G2, G3, GA, CW = 0, 16, 32, 48, 64, 65
CB = CW + XBC * CONV_K
COLS = CB + XBC
R_DTB, R_ALOG, R_DSKIP, R_QG, R_KG, R_LAM, R_INV = 0, 64, 128, 160, 224, 288, 544
ROWS = 576


class Steps:

    def __init__(self, eng, sem):
        self.eng, self.sem, self.n = eng, sem, 0

    def mark(self, ins):
        ins.then_inc(self.sem, 1)
        self.n += 1

    def wait(self):
        self.eng.wait_ge(self.sem, self.n)


def turn_step(s, late):
    for k, first in TURNS.items():
        m = s - late - 8 * first
        if -8 <= m < -2:
            return k, m + 8
        if 2 <= m < 4:
            return k, m + 4
    return None


def build(nc, x, wall, wdt_in, cols, rows, pos, g2, keys_t, peer_u, peer_v, p_t, ple_up, out):
    ctx = ExitStack()
    with ctx:
        def sb(name, shape, dt=F32):
            return ctx.enter_context(nc.sbuf_tensor(name, shape, dt))

        def sem(name):
            return ctx.enter_context(nc.semaphore(name))

        act_hi = sb("act_hi", [P, KC, S], F32R)
        act_lo = sb("act_lo", [P, KC, S], F32R)
        w_hi = sb("w_hi", [P, RING, PIECE], F32R)
        w_lo = sb("w_lo", [P, RING, PIECE], F32R)
        w_raw = sb("w_raw", [P, RING, PIECE])
        work = sb("work", [P, 14 * D])
        ident = sb("ident", [P, P])
        upper = sb("upper", [P, P])
        lower = sb("lower", [P, P])
        below = sb("below", [P, P])
        above = sb("above", [P, P])
        colc = sb("colc", [P, COLS])
        rowc = sb("rowc", [P, ROWS])
        pos_i = sb("pos_i", [P, TT], I32)
        stat = sb("stat", [P, 4, 4, TT])
        iota_i = sb("iota_i", [P, TOPK], I32)
        iota_f = sb("iota_f", [P, TOPK])
        staged = sb("staged", [P, 2 * SLOTS], I32)
        small = sb("small", [P, 2320])

        def carve(at, *shapes):
            views = []
            for shape in shapes:
                n = int(np.prod(shape))
                v = small[:, at:at + n]
                if len(shape) > 1:
                    names = "abcd"[:len(shape)]
                    v = v.rearrange("p (" + " ".join(names) + ") -> p " + " ".join(names),
                                    **dict(zip(names, shape)))
                views.append(v)
                at += n
            return views

        dtv, av, aexp, ex, dd, dtt = carve(
            0, (TT, 64), (TT, 64), (64,), (4, SSD_HEADS), (TT, SSD_HEADS), (5, TT * 64))
        cbm, = carve(512, (2, P))
        dt_rows, = carve(768, (S,))
        trig, hstat, lam, mx, nmx, rs, ri, posf, ang, lamp = carve(
            1152, (2, TT, 2, ATT_DIM), (4, ATT_HEADS), (4,), (2, 4), (2, 4), (2, 4), (2, 4), (TT,),
            (5, TT, 32), (2, ATT_DIM))
        v16, i16, i16f, sc16, ps16, psf, ef, esum, picks, gate, dots = carve(
            0, (KC, TOPK), (KC, TOPK), (KC, TOPK), (EXPERT_HEADS, TOPK), (EXPERT_HEADS, TOPK),
            (2, PICKS), (2, PICKS), (2, EXPERT_HEADS), (TT, PICKS), (TT, PICKS), (TT, PICKS))
        i16, ps16, picks = i16.bitcast(U32), ps16.bitcast(U32), picks.bitcast(I32)

        PS = ctx.enter_context(nc.psum_tensor("PS", [P, 8 * NB], F32))

        def blk(first, n=1):
            return work[:, first * D:(first + n) * D]

        def bank(b, n=1):
            return PS[:, b * NB:(b + n) * NB]

        def tiles(v):
            return v.rearrange("p (t d) -> p t d", t=TT)

        def by_block(v):
            return v.rearrange("p (b t n) -> p b t n", t=TT, n=NB)

        small_in = sem("small_in")
        x_in = [sem(f"x_in{t}") for t in range(TT)]
        masks = sem("masks")
        raw_in = [sem(f"raw_in{k}") for k in range(RING)]
        hi_split = sem("hi_split")
        lo_split = sem("lo_split")
        used = sem("used")
        banks_free = sem("banks_free")
        own_act = sem("own_act")
        own_dve = sem("own_dve")
        own_pool = sem("own_pool")
        squares = sem("squares")
        means = sem("means")
        roots = sem("roots")
        inverses = sem("inverses")
        h_ready = sem("h_ready")
        turned = sem("turned")
        turned_hi = sem("turned_hi")
        turned_lo = sem("turned_lo")
        dt_hi = sem("dt_hi")
        dt_lo = sem("dt_lo")
        dt_sum = sem("dt_sum")
        dt_out = sem("dt_out")
        dt_turned = sem("dt_turned")
        dt_abs = sem("dt_abs")
        dt_exp = sem("dt_exp")
        pad_zero = sem("pad_zero")
        conved = sem("conved")
        silued = sem("silued")
        xt_turned = sem("xt_turned")
        xt_out = sem("xt_out")
        a_ready = sem("a_ready")
        dec_sum = sem("dec_sum")
        dec_exp = sem("dec_exp")
        decayed = sem("decayed")
        xd_ready = sem("xd_ready")
        xf_ready = sem("xf_ready")
        state_sum = sem("state_sum")
        state_out = sem("state_out")
        rh_ready = sem("rh_ready")
        seg_sum = sem("seg_sum")
        seg_exp = sem("seg_exp")
        cb_sum = sem("cb_sum")
        cb_out = sem("cb_out")
        em_ready = sem("em_ready")
        skip_ready = sem("skip_ready")
        y_sum = sem("y_sum")
        y_done = sem("y_done")
        y_gated = sem("y_gated")
        head_sq = sem("head_sq")
        head_ms = sem("head_ms")
        head_rt = sem("head_rt")
        angles = sem("angles")
        sines = sem("sines")
        lam_sum = sem("lam_sum")
        lam_exp = sem("lam_exp")
        roped = sem("roped")
        qk_turned = sem("qk_turned")
        qk_out = sem("qk_out")
        scored = sem("scored")
        maxed = sem("maxed")
        expd = sem("expd")
        att_ready = sem("att_ready")
        att_turned = sem("att_turned")
        att_out = sem("att_out")
        o_sum = sem("o_sum")
        o_done = sem("o_done")
        o_ready = sem("o_ready")
        mixed_ready = sem("mixed_ready")
        x_again = sem("x_again")
        g2_in = sem("g2_in")
        keys_in = sem("keys_in")
        x_scaled = sem("x_scaled")
        h2_ready = sem("h2_ready")
        key_sum = sem("key_sum")
        key_out = sem("key_out")
        top_sub = sem("top_sub")
        top_exp = sem("top_exp")
        picked = sem("picked")
        indices_staged = sem("indices_staged")
        gathers_due = sem("gathers_due")
        row_in = [sem(f"row_in{k}") for k in range(SLOTS)]
        row_free = sem("row_free")
        gelued = sem("gelued")
        ple_in = sem("ple_in")
        ple_sum = sem("ple_sum")
        ple_out = sem("ple_out")
        out_ready = sem("out_ready")
        stored = sem("stored")

        x_sb = tiles(blk(0, 2))
        wdt = blk(10)[:, 0:PIECE]
        xbc = blk(2, 3).rearrange("p (c s) -> p c s", c=XBC)
        conv = blk(11).rearrange("p (m s) -> p m s", m=8)
        pad = blk(12, 2)[:, 0:8 * (S + 4)].rearrange("p (m s) -> p m s", m=8)
        qkv = by_block(blk(8, 6))
        xt = tiles(blk(0, 2))
        rh = blk(2).rearrange("p (r h l) -> p r h l", r=2, h=HPG)
        em = blk(3).rearrange("p (r h l) -> p r h l", r=2, h=HPG)
        bt = tiles(blk(5)[:, 0:TT * NB])
        hs = blk(5)[:, TT * NB:TT * NB + NB]
        sq = blk(5)[:, 3 * NB:4 * NB]
        xf = blk(6)[:, 0:2 * NB].rearrange("p (r d) -> p r d", r=2)
        xd = tiles(blk(6)[:, 2 * NB:4 * NB])
        xsk = blk(7)[:, 0:NB]
        ytmp = blk(7)[:, NB:2 * NB]
        rot = blk(7)[:, 2 * NB:4 * NB].rearrange("p (k d) -> p k d", k=2)
        qkt = blk(4)[:, 0:2 * NB].rearrange("p (b s) -> p b s", b=2)
        att_t = blk(4)[:, 2 * NB:4 * NB].rearrange("p (b s) -> p b s", b=2)
        prob = blk(5).rearrange("p (b j s) -> p b j s", b=2, j=4)
        att = blk(6)[:, 0:2 * NB].rearrange("p (b t s) -> p b t s", b=2, t=TT)
        att_x = tiles(blk(6)[:, 2 * NB:3 * NB])
        z_tmp = by_block(blk(7))
        o_sq = blk(7)
        mixed, g_att = by_block(blk(2, 2)), by_block(blk(10, 2))
        x1 = tiles(blk(12, 2))
        h2 = tiles(blk(8, 2))
        g2_sb = blk(5)
        keys_sb = blk(6).rearrange("p (n k) -> p n k", n=KC)
        pq = blk(7).rearrange("p (b n s) -> p b n s", b=2, n=4)
        scores_0 = blk(10)[:, 0:2 * NB].rearrange("p (b n k) -> p b n k", b=2, n=4)
        cand = blk(10)[:, 2 * NB:2 * NB + TOPK * TOPK]
        onehot = blk(10)[:, 3 * NB:4 * NB].rearrange("p (k c) -> p k c", c=TOPK)
        scores_1 = blk(11).rearrange("p (b n k) -> p b n k", b=4, n=4)
        slot = blk(0, SLOTS).rearrange("p (n d) -> p n d", n=SLOTS)
        pt_sb, = carve(0, (2, S))
        up_sb = by_block(blk(10, 2))
        g_ple = by_block(blk(6))

        JUNK = [7, 3, 0, 0]

        def head_src(n):
            return qkv[:, 4 * (n // 8) + (n % 8) // 2, n % 2, :]

        def head_cols(w, t, h):
            return qkv[:, 4 * w + h // 4, t, (h % 4) * P:(h % 4 + 1) * P]

        def gates_of(b):
            return mixed[:, b] if b < 4 else g_att[:, b - 4]

        def ssd_step(s):
            return (s - SSD_0) // SSD_STEP, (s - SSD_0) % SSD_STEP

        def att_step(s):
            return (s - ATT_0) // ATT_STEP, (s - ATT_0) % ATT_STEP

        def norm_step(s):
            return (s - NORM_0) // NORM_STEP, (s - NORM_0) % NORM_STEP

        def read_out(s, j=1):
            if s % 8 != j or s < 8:
                return None, 0, 0
            n = s // 8 - 1
            name = [m for m, k in STAGES if FIRST[m] <= n][-1]
            return name, n - FIRST[name], n % 2

        block = ctx.enter_context(nc.Block())

        @block.sync
        def _(sp):
            for t in range(TT):
                sp.dma_start(x_sb[:, t, :], x[t]).then_inc(x_in[t], 16)
            for k in range(RING):
                sp.dma_start(w_raw[:, k, :], wall[k]).then_inc(raw_in[k], 16)
            with sp.Fori(1, PIECES // RING) as g:
                for k in range(RING):
                    sp.wait_ge(lo_split, RING * g - RING + k + 1)
                    sp.dma_start(w_raw[:, k, :], wall[bass.ds(RING * g + k, 1)]
                                 .rearrange("o p n -> (o p) n")).then_inc(raw_in[k], 16)
            with sp.Fori(0, D // NB) as b:
                sp.wait_ge(out_ready, b + 1)
                sp.dma_start(out[:, :, bass.ds(b * NB, NB)].rearrange("t p n -> p t n"),
                             x1[:, :, bass.ds(b * NB, NB)]).then_inc(stored, 16)
            sp.wait_ge(stored, 16 * (D // NB))

        @block.gpsimd
        def _(pool):
            own = Steps(pool, own_pool)
            for m in (upper, lower, below, above):
                own.mark(pool.memset(m[:, :], 1.0))
            own.mark(pool.memset(ident[:, :], 0.0))
            own.wait()
            for m, op, sign in ((upper, ALU.is_ge, -1), (lower, ALU.is_ge, 1),
                                (below, ALU.is_gt, 1), (above, ALU.is_gt, -1)):
                pool.affine_select(out=m[:, :], in_=m[:, :], compare_op=op, fill=0.0, base=0,
                                   pattern=[[-sign, P]], channel_multiplier=sign).then_inc(masks, 1)
            pool.affine_select(out=ident[:, :], in_=ident[:, :], compare_op=ALU.not_equal, fill=1.0,
                               base=0, pattern=[[-1, P]], channel_multiplier=1).then_inc(masks, 1)
            pool.iota(iota_i[:, :], pattern=[[1, TOPK]], base=0, channel_multiplier=0).then_inc(masks, 1)

            pool.wait_ge(masks, 6)
            pool.wait_ge(small_in, 64)
            pool.wait_ge(xt_out, 10)
            pool.wait_ge(decayed, 1)

            def heads(v):
                return v.rearrange("p (h d) -> p h d", h=HPG)

            def per_head(v, n):
                return v.unsqueeze(2).to_broadcast([P, HPG, n])

            for n in range(TT * GROUPS):
                g, c = n // TT, n % TT
                hg = slice(g * HPG, (g + 1) * HPG)
                xg = [heads(xt[:, t, g * NB:(g + 1) * NB]) for t in range(TT)]

                def steps_of_a(r, m):
                    if n:
                        pool.wait_ge(seg_sum, 2 * n - 1 + r)
                    pool.tensor_tensor(rh[:, r], m[:, :].unsqueeze(1).to_broadcast([P, HPG, P]),
                                       per_head(av[:, c, 32 * r + g * HPG:32 * r + (g + 1) * HPG], P),
                                       ALU.mult).then_inc(rh_ready, 1)

                steps_of_a(0, upper)
                if c == 0:
                    if g:
                        pool.wait_ge(state_sum, n)
                    for t in (1, 0):
                        pool.tensor_tensor(heads(xd[:, t, :]), xg[t], per_head(dd[:, t, hg], SSD_DIM),
                                           ALU.mult).then_inc(xd_ready, 1)
                steps_of_a(1, lower)
                if n:
                    pool.wait_ge(y_sum, n)
                for r in range(2):
                    pool.tensor_tensor(heads(xf[:, r, :]), xg[c],
                                       per_head(dtv[:, c, 32 * r + g * HPG:32 * r + (g + 1) * HPG], SSD_DIM),
                                       ALU.mult).then_inc(xf_ready, 1)
                if n:
                    pool.wait_ge(y_done, n)
                pool.tensor_tensor(heads(xsk), xg[c],
                                   per_head(rowc[:, R_DSKIP + g * HPG:R_DSKIP + (g + 1) * HPG], SSD_DIM),
                                   ALU.mult).then_inc(skip_ready, 1)

            pool.wait_ge(o_done, ATT_HEADS)
            for t in range(TT):
                pool.dma_start(x1[:, t, :], x[t]).then_inc(x_again, 16)
            pool.dma_start(g2_sb, g2[0:1, :].to_broadcast([P, D])).then_inc(g2_in, 16)
            pool.dma_start(blk(6), keys_t).then_inc(keys_in, 16)

            pool.wait_ge(g2_in, 16)
            for t in range(TT):
                pool.wait_ge(x_scaled, t + 1)
                pool.tensor_tensor(h2[:, t, :], h2[:, t, :], g2_sb, ALU.mult).then_inc(h2_ready, 1)
            done = 0
            for t in range(TT):
                for table in (peer_u, peer_v):
                    with pool.Fori(0, PICKS // (2 * SLOTS)) as i:
                        for half in range(2):
                            first = done + half * SLOTS + 2 * SLOTS * i
                            pool.wait_ge(row_free, first + 1)
                            if table is peer_u and half == 0:
                                pool.wait_ge(picked, EXPERT_HEADS * t + i + 1)
                            pool.tensor_copy(staged[:, half * SLOTS:(half + 1) * SLOTS],
                                             picks[:, t, bass.ds(i * 2 * SLOTS + half * SLOTS, SLOTS)])\
                                .then_inc(indices_staged, 1)
                            pool.wait_ge(indices_staged, done // SLOTS + 2 * i + half + 1)
                            for s in range(SLOTS):
                                pool.wait_ge(row_free, first + s + 1)
                                if done == 0 and half == 0 and s == 5:
                                    pool.wait_ge(h2_ready, TT)
                                if done == 0 and half == 0 and s == 6:
                                    pool.wait_ge(key_sum, 4)
                                pool.sem_inc(gathers_due, 1)
                                k = half * SLOTS + s
                                pool.indirect_dma_start(
                                    slot[:, s, :], None, table[:, :],
                                    bass.IndirectOffsetOnAxis(ap=staged[:, k:k + 1], axis=0),
                                ).then_inc(row_in[s], 16)
                    done += PICKS
                    if done == 2 * PICKS:
                        pool.wait_ge(picked, TT * EXPERT_HEADS)
                        pool.dma_start(blk(10, 2), ple_up).then_inc(ple_in, 16)
                        pool.dma_start(small[:, 0:2 * S], p_t).then_inc(ple_in, 16)

        @block.scalar
        def _(act):
            act.sem_inc(used, RING)
            act.sem_inc(banks_free, 4)
            act.dma_start(colc[:, :], cols).then_inc(small_in, 16)
            act.dma_start(rowc[:, :], rows[0:1, :].to_broadcast([P, ROWS])).then_inc(small_in, 16)
            act.dma_start(pos_i[:, :], pos).then_inc(small_in, 16)
            act.dma_start(wdt, wdt_in).then_inc(small_in, 16)

            def hi(n):
                act.wait_ge(raw_in[n % RING], 16 * (n // RING + 1))
                act.wait_ge(used, n + 1)
                if n == RING - 1:
                    act.wait_ge(dt_sum, 1)
                act.activation(w_hi[:, n % RING, :], w_raw[:, n % RING, :], ACT.Copy).then_inc(hi_split, 1)

            def square(k, t, src):
                if t:
                    act.wait_ge(own_act, k + 1)
                ins = act.activation(bank(4, 4) if (k, t) == (3, 0) else blk(JUNK[k]), src[:, t, :],
                                     ACT.Square, accum_out=stat[:, k, 0, t:t + 1])
                ins.then_inc(squares if t else own_act, 1)

            def root(k):
                act.wait_ge(means, k + 1)
                act.activation(stat[:, k, 2, :], stat[:, k, 1, :], ACT.Sqrt).then_inc(roots, 1)

            def gain(k, c):
                at = GA if k == 2 else {0: G1, 1: GS, 4: G2, 5: G3}[k] + c
                return colc[:, at:at + 1]

            def turn(k, m):
                act.wait_ge(turned, 8 * k + m + 1)
                if k == 3:
                    act.activation(act_hi[:, 2 * m:2 * m + 2, :],
                                   bank(4 + m % 4).rearrange("p (c s) -> p c s", c=2), ACT.Copy)\
                        .then_inc(turned_hi, 1)
                    return
                for c in range(2):
                    ins = act.activation(act_hi[:, 2 * m + c, :], bank(4 + m % 4)[:, c * S:(c + 1) * S],
                                         ACT.Copy, scale=gain(k, 2 * m + c))
                ins.then_inc(turned_hi, 1)

            def xbc_rows(b, parity):
                act.wait_ge(pad_zero, 2)
                for m in range(2):
                    act.activation(pad[:, 4 * parity + 2 * m:4 * parity + 2 * m + 2, 2:2 + S],
                                   bank(2 * parity + m).rearrange("p (m s) -> p m s", m=2),
                                   ACT.Copy).then_inc(banks_free, 1)

            def beside_xbc(s):
                if s == 4:
                    act.wait_ge(dt_abs, 1)
                    act.activation(dtt[:, 1, :], dtt[:, 1, :], ACT.Exp, scale=-1.0).then_inc(dt_exp, 1)
                    act.activation(aexp, rowc[:, R_ALOG:R_ALOG + 64], ACT.Exp).then_inc(dt_exp, 1)
                if s == 10:
                    act.wait_ge(dec_sum, 1)
                    act.activation(ex, bank(4)[:, 0:4 * SSD_HEADS].rearrange("p (k h) -> p k h", k=4),
                                   ACT.Exp).then_inc(dec_exp, 1)
                if s == 18:
                    act.wait_ge(lam_sum, 1)
                    act.activation(lam[:, 0:2], lam[:, 0:2], ACT.Exp).then_inc(lam_exp, 1)
                    act.wait_ge(angles, 1)
                    act.activation(ang[:, 0:2], ang[:, 0:2], ACT.Sin).then_inc(sines, 1)
                if s % 8 == 7 and s > 8:
                    b = s // 8 - 1
                    act.wait_ge(conved, b + 1)
                    act.activation(xbc[:, 4 * b:4 * b + 4, :], conv[:, 4 * (b % 2):4 * (b % 2) + 4, :],
                                   ACT.Silu).then_inc(silued, 1)

            def beside_ssd(s):
                for m in (2 * (s - XT_0 - 1), 2 * (s - XT_0 - 1) + 1):
                    if 0 <= m < 10:
                        act.wait_ge(xt_turned, m + 1)
                        t, q = m % 2, m // 2
                        act.activation(xt[:, t, q * NB:(q + 1) * NB] if q < 4 else bt[:, t, :],
                                       bank(4 + m % 4), ACT.Copy).then_inc(xt_out, 1)
                n, at = ssd_step(s)
                if 0 <= n < 8 and at in (1, 5):
                    r = at // 4
                    act.wait_ge(seg_sum, 2 * n + r + 1)
                    if n:
                        act.wait_ge(y_sum, n)
                    for q in range(2):
                        ins = act.activation(em[:, r, 4 * q:4 * q + 4, :],
                                             bank(4 + q).rearrange("p (h l) -> p h l", h=4), ACT.Exp)
                    ins.then_inc(seg_exp, 1)
                if 0 <= n < 8 and at == 6:
                    act.wait_ge(state_sum, n + 1)
                    act.activation(hs, bank(7), ACT.Copy).then_inc(state_out, 1)
                n, at = norm_step(s)
                if 0 <= n < 16:
                    if at == 0:
                        if n:
                            act.wait_ge(head_ms, n)
                        act.activation(sq, head_src(n), ACT.Square).then_inc(head_sq, 1)
                    if at == 2:
                        act.wait_ge(head_ms, n + 1)
                        act.activation(hstat[:, 2, 0:8], hstat[:, 1, 0:8], ACT.Sqrt).then_inc(head_rt, 1)

            def beside_att(s):
                h, at = att_step(s)
                if s == ATT_0 - 2:
                    h, at = -1, 0
                if -1 <= h < 15 and at == 0:
                    act.wait_ge(qk_turned, h + 2)
                    if h >= 1:
                        act.wait_ge(scored, h)
                    act.activation(qkt[:, (h + 1) % 2, :], bank(4), ACT.Copy).then_inc(qk_out, 1)
                if 0 <= h < 16 and at == 2:
                    act.wait_ge(maxed, h + 1)
                    if h >= 2:
                        act.wait_ge(att_ready, h - 1)
                    for k in range(4):
                        ins = act.activation(prob[:, h % 2, k, :],
                                             bank(5 + k // 2)[:, (k % 2) * S:(k % 2 + 1) * S], ACT.Exp,
                                             bias=nmx[:, h % 2, k:k + 1], scale=SCALE,
                                             accum_out=rs[:, h % 2, k:k + 1])
                    ins.then_inc(expd, 1)
                t, at = (s - O_NORM) // 4, (s - O_NORM) % 4
                if 0 <= t < TT and at == 0:
                    act.wait_ge(o_done, ATT_HEADS)
                    if t:
                        act.wait_ge(head_ms, 17)
                    act.activation(o_sq.rearrange("p (b n) -> p b n", b=4), qkv[:, 0:4, t, :],
                                   ACT.Square).then_inc(head_sq, 1)
                if 0 <= t < TT and at == 2:
                    act.wait_ge(head_ms, 17 + t)
                    act.activation(hstat[:, 2, :], hstat[:, 1, :], ACT.Sqrt).then_inc(head_rt, 1)
                if s in (Y_NORM, Y_NORM + 2):
                    act.wait_ge(y_gated, 4)
                    square(1, (s - Y_NORM) // 2, xt)
                if s == Y_NORM + 6:
                    root(1)

            def beside(s):
                if s < 56:
                    beside_xbc(s)
                elif s < ATT_0 - 2:
                    beside_ssd(s)
                elif s < 232:
                    beside_att(s)
                name, b, parity = read_out(s)
                out_banks = [bank(2 * parity + t) for t in range(TT)]
                if name == "xbc":
                    xbc_rows(b, parity)
                if name in ("q", "k", "v"):
                    for t in range(TT):
                        act.activation(qkv[:, 4 * ("q", "k", "v").index(name) + b, t, :], out_banks[t],
                                       ACT.Copy).then_inc(banks_free, 1)
                if name == "z":
                    if b == 0:
                        act.wait_ge(roped, 16)
                    if b >= 2:
                        act.wait_ge(y_gated, b - 1)
                    for t in range(TT):
                        act.activation(z_tmp[:, parity, t, :], out_banks[t], ACT.Silu).then_inc(banks_free, 1)
                if name == "gates":
                    if b == 0:
                        act.wait_ge(y_done, 8)
                    if b == 4:
                        act.wait_ge(qk_turned, ATT_HEADS)
                    for t in range(TT):
                        act.activation(gates_of(b)[:, t, :], out_banks[t], ACT.Sigmoid).then_inc(banks_free, 1)
                due = turn_step(s, 2)
                if due:
                    turn(*due)
                if s in (X_NORM, X_NORM + 2):
                    act.wait_ge(banks_free, 4 + 2 * FIRST["peer_q"])
                    square(2, (s - X_NORM) // 2, x1)
                if s == X_NORM + 6:
                    root(2)
                if s in (X_NORM + 11, X_NORM + 13):
                    t = (s - X_NORM - 11) // 2
                    act.wait_ge(inverses, 3)
                    act.wait_ge(turned_lo, 32)
                    act.activation(h2[:, t, :], x1[:, t, :], ACT.Copy, scale=stat[:, 2, 3, t:t + 1])\
                        .then_inc(x_scaled, 1)
                if name == "peer_q":
                    pq_rows(b, parity)
                name, b, parity = read_out(s, 5)
                if name == "peer_q":
                    key_rows(b)

            def key_rows(b):
                act.wait_ge(key_sum, b + 1)
                if b == 0:
                    act.wait_ge(inverses, 3)
                if b >= 2:
                    act.wait_ge(picked, 2 * b - 2)
                for t, dst in ((0, scores_0[:, b % 2]), (1, scores_1[:, b])):
                    act.activation(dst, bank(4 + 2 * (b % 2) + t).rearrange("p (n k) -> p n k", n=4),
                                   ACT.Copy, scale=stat[:, 2, 3, t:t + 1]).then_inc(key_out, 1)

            def pq_rows(b, parity):
                if b == 0:
                    act.wait_ge(head_ms, 18)
                if b >= 2:
                    act.wait_ge(key_sum, b - 1)
                for m in range(2):
                    act.activation(pq[:, b % 2, 2 * m:2 * m + 2, :],
                                   bank(2 * parity + m).rearrange("p (m s) -> p m s", m=2), ACT.Copy)\
                        .then_inc(banks_free, 1)

            act.wait_ge(x_in[0], 16)
            square(0, 0, x_sb)
            root(0)
            for n in range(AHEAD):
                hi(n)
            act.wait_ge(inverses, 1)
            act.activation(x_sb[:, 0, :], x_sb[:, 0, :], ACT.Copy, scale=stat[:, 0, 3, 0:1]).then_inc(h_ready, 1)
            act.wait_ge(small_in, 64)
            for m in range(8):
                turn(0, m)
            act.activation(w_hi[:, RING - 1, :], wdt, ACT.Copy).then_inc(dt_hi, 1)

            for s in range(8 * FIRST["ple_gate"]):
                hi(s + AHEAD)
                beside(s)
            act.wait_ge(used, RING + 8 * FIRST["ple_gate"])
            pq_rows(3, 1)
            hi(8 * FIRST["ple_gate"] + 2)
            hi(8 * FIRST["ple_gate"] + 3)

            key_rows(3)

            def turn5(t):
                for m in range(4):
                    act.wait_ge(turned, 40 + 4 * t + m + 1)
                    for c in range(4):
                        ins = act.activation(act_hi[:, 4 * m + c, t * P:(t + 1) * P],
                                             bank(4 + m)[:, c * P:(c + 1) * P], ACT.Copy,
                                             scale=gain(5, 4 * m + c))
                    ins.then_inc(turned_hi, 1)

            for t in range(TT):
                act.wait_ge(top_sub, (t + 1) * EXPERT_HEADS)
                act.activation(gate[:, t, :], gate[:, t, :], ACT.Exp).then_inc(top_exp, 1)
                act.wait_ge(row_free, SLOTS + (2 * t + 1) * PICKS)
                act.activation(dots[:, t, :], dots[:, t, :], ACT.Gelu).then_inc(gelued, 1)
                if t == 0:
                    act.wait_ge(row_free, SLOTS + 2 * PICKS)
                    turn5(0)
                    for b in range(D // NB):
                        act.wait_ge(ple_sum, b + 1)
                        act.activation(up_sb[:, b], tiles(bank(2 * (b % 2), 2)), ACT.Copy).then_inc(ple_out, 1)
                    act.wait_ge(turned_lo, 44)
                    square(3, 0, x1)
            act.wait_ge(row_free, SLOTS + 4 * PICKS)
            turn5(1)
            square(3, 1, x1)
            for s in range(8 * FIRST["ple_gate"], PIECES + 8):
                if 8 * FIRST["ple_gate"] + RING <= s + AHEAD < PIECES:
                    hi(s + AHEAD)
                if s == 8 * FIRST["ple_gate"] + 3:
                    root(3)
                name, b, parity = read_out(s, 1)
                if name == "ple_gate":
                    act.wait_ge(used, RING + 8 * (s // 8))
                    if b == 0:
                        act.wait_ge(inverses, 4)
                    if b >= 2:
                        act.wait_ge(out_ready, b - 1)
                    for t in range(TT):
                        act.activation(g_ple[:, parity, t, :], bank(2 * parity + t), ACT.Sigmoid,
                                       scale=stat[:, 3, 3, t:t + 1]).then_inc(banks_free, 1)

        @block.vector
        def _(dve):
            own = Steps(dve, own_dve)
            dve.sem_inc(row_free, SLOTS)

            def step(ins):
                own.mark(ins)
                own.wait()

            def lo(n):
                dve.wait_ge(hi_split, n + 1)
                dve.tensor_tensor(w_lo[:, n % RING, :], w_raw[:, n % RING, :],
                                  w_hi[:, n % RING, :].bitcast(F32), ALU.subtract).then_inc(lo_split, 1)

            def mean(k):
                if k == 0:
                    dve.wait_ge(own_act, 1)
                else:
                    dve.wait_ge(squares, k)
                dve.tensor_scalar(stat[:, k, 1, :], stat[:, k, 0, :], 1.0 / D, EPS, ALU.mult, ALU.add)\
                    .then_inc(means, 1)

            def inverse(k):
                dve.wait_ge(roots, k + 1)
                dve.reciprocal(stat[:, k, 3, :], stat[:, k, 2, :]).then_inc(inverses, 1)
                dve.wait_ge(inverses, k + 1)

            def gain(k, c):
                at = GA if k == 2 else {0: G1, 1: GS, 4: G2, 5: G3}[k] + c
                return colc[:, at:at + 1]

            def turn(k, m):
                dve.wait_ge(turned_hi, 8 * k + m + 1)
                if k == 3:
                    dve.tensor_tensor(act_lo[:, 2 * m:2 * m + 2, :],
                                      bank(4 + m % 4).rearrange("p (c s) -> p c s", c=2),
                                      act_hi[:, 2 * m:2 * m + 2, :].bitcast(F32), ALU.subtract)\
                        .then_inc(turned_lo, 1)
                    return
                for c in range(2):
                    ins = dve.scalar_tensor_tensor(
                        out=act_lo[:, 2 * m + c, :], in0=bank(4 + m % 4)[:, c * S:(c + 1) * S],
                        scalar=gain(k, 2 * m + c), in1=act_hi[:, 2 * m + c, :].bitcast(F32),
                        op0=ALU.mult, op1=ALU.subtract)
                ins.then_inc(turned_lo, 1)

            def dt_before():
                dve.wait_ge(dt_turned, 1)
                step(dve.tensor_tensor(dtt[:, 0, :].rearrange("p (t h) -> p t h", t=TT),
                                       bank(5)[:, 0:TT * 64].rearrange("p (t h) -> p t h", t=TT),
                                       rowc[:, R_DTB:R_DTB + 64].unsqueeze(1).to_broadcast([P, TT, 64]),
                                       ALU.add))
                dve.scalar_tensor_tensor(out=dtt[:, 1, :], in0=dtt[:, 0, :], scalar=-1.0, in1=dtt[:, 0, :],
                                         op0=ALU.mult, op1=ALU.max).then_inc(dt_abs, 1)

            def dt_and_a():
                dve.wait_ge(dt_exp, 2)
                s_, s2, p_ = dtt[:, 2, :], dtt[:, 3, :], dtt[:, 4, :]
                step(dve.tensor_scalar(s2, dtt[:, 1, :], 2.0, None, ALU.add))
                step(dve.reciprocal(p_, s2))
                step(dve.tensor_tensor(s_, dtt[:, 1, :], p_, ALU.mult))
                step(dve.tensor_tensor(s2, s_, s_, ALU.mult))
                step(dve.tensor_scalar(p_, s2, 1.0 / 17, None, ALU.mult))
                for k in range(7, 0, -1):
                    step(dve.scalar_tensor_tensor(out=p_, in0=p_, scalar=1.0 / (2 * k + 1), in1=s2,
                                                  op0=ALU.add, op1=ALU.mult))
                step(dve.scalar_tensor_tensor(out=p_, in0=p_, scalar=1.0, in1=s_, op0=ALU.add, op1=ALU.mult))
                step(dve.tensor_scalar(s2, dtt[:, 0, :], 0.0, None, ALU.max))
                step(dve.scalar_tensor_tensor(out=dtv.rearrange("p t h -> p (t h)"), in0=p_, scalar=2.0,
                                              in1=s2, op0=ALU.mult, op1=ALU.add))
                for t in range(TT):
                    ins = dve.scalar_tensor_tensor(out=av[:, t, :], in0=dtv[:, t, :], scalar=-1.0,
                                                   in1=aexp, op0=ALU.mult, op1=ALU.mult)
                ins.then_inc(a_ready, 1)

            def rotary_angles(k):
                C1, C2 = 6.28125, 0.0019350051879882812
                C3 = 6.283185307179586 - C1 - C2
                MAGIC, PI = 1.5 * 2.0 ** 23, 3.1415925
                whole, r, turns = ang[:, 4], ang[:, k], ang[:, 2 + k]
                if k == 0:
                    step(dve.tensor_copy(posf, pos_i[:, :]))
                    for t in range(TT):
                        own.mark(dve.tensor_scalar(ang[:, 4, t, :], rowc[:, R_INV:R_INV + 32],
                                                   posf[:, t:t + 1], None, ALU.mult))
                    own.wait()
                step(dve.tensor_scalar(turns, whole, 1.0 / 6.283185307179586, 0.25 * k, ALU.mult, ALU.add))
                step(dve.tensor_scalar(turns, turns, MAGIC, None, ALU.add))
                step(dve.tensor_scalar(turns, turns, -MAGIC, None, ALU.add))
                for c, src in ((C1, whole), (C2, r), (C3, r)):
                    step(dve.scalar_tensor_tensor(out=r, in0=turns, scalar=-c, in1=src, op0=ALU.mult,
                                                  op1=ALU.add))
                if k:
                    step(dve.tensor_scalar(r, r, 1.5707963267948966, None, ALU.add))
                ins = dve.tensor_scalar(r, r, PI, -PI, ALU.min, ALU.max)
                if k:
                    ins.then_inc(angles, 1)
                else:
                    step(ins)

            def lambda_sums():
                step(dve.tensor_tensor(lamp, rowc[:, R_LAM:R_LAM + 128].rearrange("p (k d) -> p k d", k=2),
                                       rowc[:, R_LAM + 128:R_LAM + 256].rearrange("p (k d) -> p k d", k=2),
                                       ALU.mult))
                dve.tensor_reduce(lam[:, 0:2], lamp, AX.X, ALU.add).then_inc(lam_sum, 1)

            def trigonometry():
                dve.wait_ge(sines, 1)
                for w, base in ((0, R_QG), (1, R_KG)):
                    for t in range(TT):
                        for half in range(2):
                            g_ = rowc[:, base + 32 * half:base + 32 * half + 32]
                            own.mark(dve.tensor_tensor(trig[:, w, t, 0, 32 * half:32 * half + 32],
                                                       ang[:, 1, t, :], g_, ALU.mult))
                            own.mark(dve.tensor_tensor(trig[:, w, t, 1, 32 * half:32 * half + 32],
                                                       ang[:, 0, t, :], g_, ALU.mult))
                dve.wait_ge(lam_exp, 1)
                step(dve.tensor_tensor(lam[:, 2:3], lam[:, 1:2], lam[:, 0:1], ALU.subtract))
                step(dve.tensor_scalar(lam[:, 3:4], lam[:, 2:3], -LAM_INIT, None, ALU.add))

            def conv_chunk(b, m):
                dve.wait_ge(banks_free, 4 + 2 * b + 2)
                if b >= 2:
                    dve.wait_ge(silued, b - 1)
                k, ch = 4 * (b % 2) + m, 4 * b + m
                for tap in range(CONV_K):
                    w = colc[:, CW + CONV_K * ch + tap:CW + CONV_K * ch + tap + 1]
                    if tap == 0:
                        ins = dve.tensor_scalar(conv[:, k, :], pad[:, k, 0:S], w,
                                                colc[:, CB + ch:CB + ch + 1], ALU.mult, ALU.add)
                    else:
                        own.wait()
                        ins = dve.scalar_tensor_tensor(out=conv[:, k, :], in0=pad[:, k, tap:tap + S],
                                                       scalar=w, in1=conv[:, k, :],
                                                       op0=ALU.mult, op1=ALU.add)
                    if tap == CONV_K - 1 and m == 3:
                        ins.then_inc(conved, 1)
                    else:
                        own.mark(ins)

            def beside_xbc(s):
                if s == 1:
                    dve.wait_ge(dt_sum, 1)
                    dve.tensor_copy(dt_rows[0:64, :], bank(4)[0:64, 0:S]).then_inc(dt_out, 1)
                if s == 3:
                    dt_before()
                if s == 5:
                    dt_and_a()
                if s == 8:
                    rotary_angles(0)
                if s == 9:
                    lambda_sums()
                if s == 10:
                    rotary_angles(1)
                if s == 15:
                    dve.wait_ge(dec_exp, 1)
                    for t in range(TT):
                        ins = dve.tensor_tensor(dd[:, t, :], dtv[:, t, 32 * t:32 * t + 32], ex[:, 2 + t, :],
                                                ALU.mult)
                    ins.then_inc(decayed, 1)
                if s == 24:
                    trigonometry()
                if s > 8 and 3 <= s % 8 <= 6:
                    conv_chunk(s // 8 - 1, s % 8 - 3)

            def heads(v):
                return v.rearrange("p (h d) -> p h d", h=HPG)

            def per_head(v):
                return v.unsqueeze(2).to_broadcast([P, HPG, SSD_DIM])

            def outputs(n):
                g, c = n // TT, n % TT
                dve.wait_ge(y_sum, n + 1)
                step(dve.tensor_tensor(heads(ytmp), heads(bank(7)), per_head(ex[:, c, g * HPG:(g + 1) * HPG]),
                                       ALU.mult))
                step(dve.tensor_tensor(ytmp, ytmp, bank(6), ALU.add))
                dve.wait_ge(skip_ready, n + 1)
                dve.tensor_tensor(xt[:, c, g * NB:(g + 1) * NB], ytmp, xsk, ALU.add).then_inc(y_done, 1)

            def decayed_cb(n, r):
                dve.wait_ge(seg_exp, 2 * n + r + 1)
                dve.tensor_tensor(em[:, r], em[:, r], cbm[:, r, :].unsqueeze(1).to_broadcast([P, HPG, P]),
                                  ALU.mult).then_inc(em_ready, 1)

            def eight(v):
                return v.rearrange("p (h d) -> p h d", h=8)

            def head_norm(n):
                dve.wait_ge(head_sq, n + 1)
                step(dve.tensor_reduce(hstat[:, 0, 0:8], eight(sq), AX.X, ALU.add))
                dve.tensor_scalar(hstat[:, 1, 0:8], hstat[:, 0, 0:8], 1.0 / ATT_DIM, EPS,
                                  ALU.mult, ALU.add).then_inc(head_ms, 1)

            def rope(n):
                v = head_src(n)
                dve.wait_ge(head_rt, n + 1)
                step(dve.reciprocal(hstat[:, 3, 0:8], hstat[:, 2, 0:8]))
                step(dve.tensor_tensor(eight(v), eight(v),
                                       hstat[:, 3, 0:8].unsqueeze(2).to_broadcast([P, 8, ATT_DIM]), ALU.mult))
                for k in range(2):
                    tr = trig[:, n // 8, n % 2, k, :]
                    own.mark(dve.tensor_tensor(eight(rot[:, k, :]), eight(v),
                                               tr.unsqueeze(1).to_broadcast([P, 8, ATT_DIM]), ALU.mult))
                own.wait()
                rc, rsn = eight(rot[:, 0, :]), eight(rot[:, 1, :])
                step(dve.tensor_tensor(eight(v)[:, :, 0:32], rc[:, :, 0:32], rsn[:, :, 32:64], ALU.subtract))
                dve.tensor_tensor(eight(v)[:, :, 32:64], rc[:, :, 32:64], rsn[:, :, 0:32],
                                  ALU.add).then_inc(roped, 1)
                dve.wait_ge(roped, n + 1)

            def beside_ssd(s):
                n, at = ssd_step(s)
                if 1 <= n < 9 and at == 0:
                    outputs(n - 1)
                if 0 <= n < 8:
                    if at == 3:
                        dve.wait_ge(cb_sum, n + 1)
                        if n:
                            dve.wait_ge(em_ready, 2 * n)
                        for r, m in ((0, upper), (1, lower)):
                            ins = dve.tensor_tensor(cbm[:, r, :], bank(7)[:, 0:P], m[:, :], ALU.mult)
                        ins.then_inc(cb_out, 1)
                        dve.wait_ge(cb_out, n + 1)
                    if at == 4:
                        decayed_cb(n, 0)
                    if at == 7:
                        decayed_cb(n, 1)
                n, at = norm_step(s)
                if 0 <= n < 16:
                    if at == 1:
                        head_norm(n)
                    if at == 3:
                        rope(n)

            def maxima(h):
                dve.wait_ge(scored, h + 1)
                for j in range(2):
                    own.mark(dve.tensor_reduce(mx[:, h % 2, 2 * j:2 * j + 2], tiles(bank(5 + j)), AX.X,
                                               ALU.max))
                own.wait()
                if h >= 2:
                    dve.wait_ge(expd, h - 1)
                dve.tensor_scalar(nmx[:, h % 2, :], mx[:, h % 2, :], -SCALE, None, ALU.mult).then_inc(maxed, 1)

            def combine(h):
                dve.wait_ge(expd, h + 1)
                step(dve.reciprocal(ri[:, h % 2, :], rs[:, h % 2, :]))
                step(dve.tensor_scalar(ri[:, h % 2, 2:4], ri[:, h % 2, 2:4], lam[:, 3:4], None, ALU.mult))
                if h:
                    dve.wait_ge(att_ready, h)
                for t in range(TT):
                    own.mark(dve.tensor_scalar(att_x[:, t, :], prob[:, h % 2, 2 + t, :],
                                               ri[:, h % 2, 2 + t:3 + t], None, ALU.mult))
                own.wait()
                if h >= 2:
                    dve.wait_ge(att_turned, h - 1)
                for t in range(TT):
                    ins = dve.scalar_tensor_tensor(out=att[:, h % 2, t, :], in0=prob[:, h % 2, t, :],
                                                   scalar=ri[:, h % 2, t:t + 1], in1=att_x[:, t, :],
                                                   op0=ALU.mult, op1=ALU.add)
                ins.then_inc(att_ready, 1)

            def beside_att(s):
                h, at = att_step(s)
                if 2 <= h < 18 and at == 0:
                    dve.wait_ge(o_sum, h - 1)
                    dve.tensor_copy(qkv[:, (h - 2) // 4, :, ((h - 2) % 4) * P:((h - 2) % 4 + 1) * P],
                                    tiles(bank(7)[:, 0:S])).then_inc(o_done, 1)
                if 0 <= h < 16 and at == 1:
                    maxima(h)
                if 1 <= h < 17 and at == 2:
                    dve.wait_ge(att_turned, h)
                    if h >= 3:
                        dve.wait_ge(o_sum, h - 2)
                    dve.tensor_copy(att_t[:, (h - 1) % 2, :], bank(4)).then_inc(att_out, 1)
                if 0 <= h < 16 and at == 3:
                    combine(h)
                t, at = (s - O_NORM) // 4, (s - O_NORM) % 4
                if 0 <= t < TT and at == 1:
                    dve.wait_ge(head_sq, 17 + t)
                    step(dve.tensor_reduce(hstat[:, 0, :], o_sq.rearrange("p (h d) -> p h d", h=ATT_HEADS),
                                           AX.X, ALU.add))
                    dve.tensor_scalar(hstat[:, 1, :], hstat[:, 0, :], 1.0 / P, EPS, ALU.mult, ALU.add)\
                        .then_inc(head_ms, 1)
                if 0 <= t < TT and at == 3:
                    dve.wait_ge(head_rt, 17 + t)
                    step(dve.reciprocal(hstat[:, 3, :], hstat[:, 2, :]))
                    step(dve.tensor_scalar(hstat[:, 3, :], hstat[:, 3, :], 1.0 - LAM_INIT, None, ALU.mult))
                    o = qkv[:, 0:4, t, :].rearrange("p b (h d) -> p b h d", h=4)
                    scales = hstat[:, 3, :].rearrange("p (b h) -> p b h", b=4)
                    for b in range(4):
                        ins = dve.tensor_tensor(o[:, b], o[:, b],
                                                scales[:, b].unsqueeze(2).to_broadcast([P, 4, P]), ALU.mult)
                        if b < 3:
                            own.mark(ins)
                    ins.then_inc(o_ready, 1)
                if s == Y_NORM + 4:
                    mean(1)
                if s == Y_NORM + 7:
                    inverse(1)

            def beside(s):
                if s < 56:
                    beside_xbc(s)
                elif s < ATT_0 - 2:
                    beside_ssd(s)
                elif s < 232:
                    beside_att(s)
                name, b, parity = read_out(s, 2)
                if name == "z":
                    dve.wait_ge(banks_free, 4 + 2 * (FIRST["z"] + b + 1))
                    y = xt[:, :, b * NB:(b + 1) * NB]
                    dve.tensor_tensor(y, y, z_tmp[:, parity], ALU.mult).then_inc(y_gated, 1)
                name, b, parity = read_out(s)
                out_banks = [bank(2 * parity + t) for t in range(TT)]
                if name in ("ssd_out", "att_out", "w_out"):
                    dve.wait_ge(used, RING + 8 * (s // 8))
                if name == "ssd_out":
                    for t in range(TT):
                        dve.scalar_tensor_tensor(out=mixed[:, b, t, :], in0=out_banks[t],
                                                 scalar=stat[:, 1, 3, t:t + 1], in1=mixed[:, b, t, :],
                                                 op0=ALU.mult, op1=ALU.mult).then_inc(banks_free, 1)
                if name == "att_out":
                    for t in range(TT):
                        dve.tensor_tensor(g_att[:, b, t, :], g_att[:, b, t, :], out_banks[t], ALU.mult)\
                            .then_inc(banks_free, 1)
                    dve.wait_ge(banks_free, 4 + 2 * (FIRST["att_out"] + b + 1))
                    dve.tensor_tensor(mixed[:, b], mixed[:, b], g_att[:, b], ALU.add).then_inc(mixed_ready, 1)
                if name == "w_out":
                    if b == 0:
                        dve.wait_ge(x_again, 32)
                    for t in range(TT):
                        xb = x1[:, t, b * NB:(b + 1) * NB]
                        dve.tensor_tensor(xb, xb, out_banks[t], ALU.add).then_inc(banks_free, 1)
                due = turn_step(s, 2)
                if due:
                    turn(*due)
                if s == X_NORM + 4:
                    mean(2)
                if s == X_NORM + 8:
                    inverse(2)
                b, at = (s - KEYS_0) // 8, (s - KEYS_0) % 8
                if b == 0 and at == 0:
                    step(dve.tensor_copy(iota_f[:, :], iota_i[:, :]))
                if b == 0:
                    key_steps(b, at)
                if s in EARLY:
                    n = EARLY.index(s)
                    if n == 0:
                        dve.wait_ge(h2_ready, TT)
                    dot(0, 0, 0, n, slice(n, n + 1))

            def top16(rows):
                for r in range(2):
                    eight_at = slice(8 * r, 8 * r + 8)
                    for src, vals, idx in rows:
                        own.mark(dve.max(vals[:, eight_at], src))
                    own.wait()
                    for src, vals, idx in rows:
                        own.mark(dve.max_index(idx[:, eight_at], vals[:, eight_at], src))
                    own.wait()
                    if r == 0:
                        for src, vals, idx in rows:
                            own.mark(dve.match_replace(src, vals[:, 0:8], src, LOWEST))
                        own.wait()

            def best_keys(t, h):
                dve.wait_ge(key_out, 2 * (h // 2) + t + 1)
                src = (scores_0[:, (h // 2) % 2], scores_1[:, h // 2])[t]
                top16([(src[:, 2 * (h % 2) + k, :], v16[:, 2 * h + k, :], i16[:, 2 * h + k, :])
                       for k in range(2)])

            def best_sums(t, h):
                a0, a1 = v16[:, 2 * h, :], v16[:, 2 * h + 1, :]
                step(dve.tensor_tensor(cand.rearrange("p (a b) -> p a b", a=TOPK),
                                       a0.unsqueeze(2).to_broadcast([P, TOPK, TOPK]),
                                       a1.unsqueeze(1).to_broadcast([P, TOPK, TOPK]), ALU.add))
                top16([(cand, sc16[:, h, :], ps16[:, h, :])])
                dve.tensor_scalar(gate[:, t, h * TOPK:(h + 1) * TOPK], sc16[:, h, :], sc16[:, h, 0:1], None,
                                  ALU.subtract).then_inc(top_sub, 1)

            def experts(t, h):
                n = 2 * TOPK
                at = slice(h * TOPK, h * TOPK + n)
                pk = picks[:, t, at]
                pos16 = ps16.rearrange("p h k -> p (h k)")[:, at].bitcast(I32)
                step(dve.tensor_copy(i16f[:, 2 * h:2 * h + 4, :], i16[:, 2 * h:2 * h + 4, :]))
                for k in range(2):
                    if k == 0:
                        step(dve.tensor_scalar(pk, pos16, 4, None, ALU.logical_shift_right))
                    else:
                        step(dve.tensor_scalar(pk, pos16, TOPK - 1, None, ALU.bitwise_and))
                    step(dve.tensor_copy(psf[:, k, at], pk))
                    step(dve.tensor_tensor(onehot, psf[:, k, at].unsqueeze(2).to_broadcast([P, n, TOPK]),
                                           iota_f[:, :].unsqueeze(1).to_broadcast([P, n, TOPK]), ALU.is_equal))
                    oh = onehot.rearrange("p (h k) c -> p h k c", h=2)
                    ii = i16f.rearrange("p (h k) c -> p h k c", k=2)[:, h:h + 2, k, :]
                    step(dve.tensor_tensor(oh, oh, ii.unsqueeze(2).to_broadcast([P, 2, TOPK, TOPK]), ALU.mult))
                    step(dve.tensor_reduce(ef[:, k, at], onehot, AX.X, ALU.add))
                step(dve.scalar_tensor_tensor(out=psf[:, 0, at], in0=ef[:, 0, at], scalar=float(NKEYS),
                                              in1=ef[:, 1, at], op0=ALU.mult, op1=ALU.add))
                dve.tensor_copy(pk, psf[:, 0, at]).then_inc(picked, 2)

            def softmax(t):
                dve.wait_ge(top_exp, t + 1)
                g3 = gate[:, t, :].rearrange("p (h k) -> p h k", h=EXPERT_HEADS)
                step(dve.tensor_reduce(esum[:, 0, :], g3, AX.X, ALU.add))
                step(dve.reciprocal(esum[:, 1, :], esum[:, 0, :]))
                step(dve.tensor_tensor(g3, g3, esum[:, 1, :].unsqueeze(2).to_broadcast([P, EXPERT_HEADS, TOPK]),
                                       ALU.mult))

            def key_steps(b, at):
                if at in (1, 3):
                    best_keys(0, 2 * b + at // 2)
                if at in (2, 4):
                    best_sums(0, 2 * b + at // 2 - 1)
                if at == 5:
                    experts(0, 2 * b)

            def dot(t, before, i, s, at):
                dve.wait_ge(row_in[s], 16 * (before // SLOTS) + 16 * i + 16)
                dve.scalar_tensor_tensor(out=slot[:, s, :], in0=slot[:, s, :], scalar=1.0,
                                         in1=h2[:, t, :], op0=ALU.mult, op1=ALU.mult,
                                         accum_out=dots[:, t, at]).then_inc(row_free, 1)

            def between_rows(n):
                rest = [(b, at) for b in range(1, 4) for at in range(1, 6)]
                if n < len(rest):
                    key_steps(*rest[n])
                    return
                h, at = 2 * ((n - len(rest)) // 5), (n - len(rest)) % 5
                if h >= EXPERT_HEADS:
                    return
                if at in (0, 2):
                    best_keys(1, h + at // 2)
                if at in (1, 3):
                    best_sums(1, h + at // 2)
                if at == 4:
                    experts(1, h)

            for b in range(2):
                dve.memset(pad[:, 4 * b:4 * b + 4, :], 0.0).then_inc(pad_zero, 1)
            dve.wait_ge(x_in[1], 16)
            step(dve.scalar_tensor_tensor(out=blk(6), in0=x_sb[:, 1, :], scalar=1.0, in1=x_sb[:, 1, :],
                                          op0=ALU.mult, op1=ALU.mult, accum_out=stat[:, 0, 0, 1:2]))
            mean(0)
            inverse(0)
            dve.tensor_scalar(x_sb[:, 1, :], x_sb[:, 1, :], stat[:, 0, 3, 1:2], None, ALU.mult)\
                .then_inc(h_ready, 1)
            for n in range(AHEAD):
                lo(n)
            dve.wait_ge(small_in, 64)
            for m in range(8):
                turn(0, m)
            dve.wait_ge(dt_hi, 1)
            dve.tensor_tensor(w_lo[:, RING - 1, :], wdt, w_hi[:, RING - 1, :].bitcast(F32), ALU.subtract)\
                .then_inc(dt_lo, 1)

            for s in range(8 * FIRST["ple_gate"]):
                lo(s + AHEAD)
                beside(s)

            def turn5(t):
                for m in range(4):
                    dve.wait_ge(turned_hi, 40 + 4 * t + m + 1)
                    for c in range(4):
                        ins = dve.scalar_tensor_tensor(
                            out=act_lo[:, 4 * m + c, t * P:(t + 1) * P], in0=bank(4 + m)[:, c * P:(c + 1) * P],
                            scalar=gain(5, 4 * m + c),
                            in1=act_hi[:, 4 * m + c, t * P:(t + 1) * P].bitcast(F32),
                            op0=ALU.mult, op1=ALU.subtract)
                    ins.then_inc(turned_lo, 1)

            lo(8 * FIRST["ple_gate"] + 2)
            lo(8 * FIRST["ple_gate"] + 3)
            rows_used = 0
            for t in range(TT):
                if t == 0:
                    for i in range(PICKS // SLOTS):
                        for s in range(SLOTS):
                            if i or s >= len(EARLY):
                                dot(0, 0, i, s, slice(i * SLOTS + s, i * SLOTS + s + 1))
                            if s % 4 == 1:
                                between_rows(2 * i + s // 4)
                else:
                    with dve.Fori(0, PICKS // SLOTS) as i:
                        for s in range(SLOTS):
                            dot(t, rows_used, i, s, bass.ds(i * SLOTS + s, 1))
                rows_used += PICKS
                softmax(t)
                dve.wait_ge(gelued, t + 1)
                step(dve.tensor_tensor(dots[:, t, :], dots[:, t, :], gate[:, t, :], ALU.mult))

                def add(i, s, at):
                    dve.wait_ge(row_free, SLOTS + rows_used + SLOTS * i + s)
                    dve.wait_ge(row_in[s], 16 * (rows_used // SLOTS) + 16 * i + 16)
                    dve.scalar_tensor_tensor(out=x1[:, t, :], in0=slot[:, s, :], scalar=dots[:, t, at],
                                             in1=x1[:, t, :], op0=ALU.mult, op1=ALU.add)\
                        .then_inc(row_free, 1)

                for i in range(2 * (1 - t)):
                    for s in range(SLOTS):
                        add(i, s, slice(i * SLOTS + s, i * SLOTS + s + 1))
                        if s % 4 == 1:
                            between_rows(2 * (PICKS // SLOTS + i) + s // 4)
                with dve.Fori(2 * (1 - t), PICKS // SLOTS) as i:
                    for s in range(SLOTS):
                        add(i, s, bass.ds(i * SLOTS + s, 1))
                rows_used += PICKS
                turn5(t)

            for s in range(8 * FIRST["ple_gate"], PIECES + 8):
                if 8 * FIRST["ple_gate"] + RING <= s + AHEAD < PIECES:
                    lo(s + AHEAD)
                if s == 8 * FIRST["ple_gate"] + 2:
                    mean(3)
                if s == 8 * FIRST["ple_gate"] + 5:
                    inverse(3)
                name, b, parity = read_out(s, 2)
                if name == "ple_gate":
                    dve.wait_ge(banks_free, 4 + 2 * (s // 8))
                    dve.wait_ge(ple_out, b + 1)
                    step(dve.tensor_tensor(g_ple[:, parity], g_ple[:, parity], up_sb[:, b], ALU.mult))
                    xs = x1[:, :, b * NB:(b + 1) * NB]
                    dve.tensor_tensor(xs, xs, g_ple[:, parity], ALU.add).then_inc(out_ready, 1)

        @block.tensor
        def _(pe):
            def mm(out_, lhs, rhs, start, stop, shared=False):
                return nc.tensor.matmul(out_, lhs, rhs, start=start, stop=stop, skip_group_check=shared)

            def source(k, t, c):
                if k == 0:
                    return x_sb[:, t, c * P:(c + 1) * P]
                if k == 1:
                    return xt[:, t, c * P:(c + 1) * P]
                if k == 2:
                    return qkv[:, c // 4, t, (c % 4) * P:(c % 4 + 1) * P]
                if k == 3:
                    return mixed[:, c // 4, t, (c % 4) * P:(c % 4 + 1) * P]
                return x1[:, t, c * P:(c + 1) * P]

            def turn(k, m):
                if k == 0 and m == 0:
                    pe.wait_ge(h_ready, TT)
                if k == 1 and m == 0:
                    pe.wait_ge(y_gated, 4)
                    pe.wait_ge(o_done, ATT_HEADS)
                if k == 2 and m == 0:
                    pe.wait_ge(o_ready, 2)
                if k == 3:
                    pe.wait_ge(mixed_ready, m // 2 + 1)
                if k == 4:
                    pe.wait_ge(banks_free, 4 + 2 * (FIRST["w_out"] + m // 2 + 1))
                if 8 * k + m >= 4:
                    pe.wait_ge(turned_lo, 8 * k + m - 3)
                for c in range(2):
                    for t in range(TT):
                        ins = pe.transpose(bank(4 + m % 4)[:, c * S + t * P:c * S + (t + 1) * P],
                                           source(k, t, 2 * m + c), ident[:, :])
                ins.then_inc(turned, 1)

            def products(s, only=None):
                b, j = s // 8, s % 8
                name = [m for m, k in STAGES if FIRST[m] <= b][-1]
                if j == 0:
                    pe.wait_ge(banks_free, 2 * b + 2)
                for k, first in TURNS.items():
                    if b == first:
                        pe.wait_ge(turned_lo, 8 * k + j + 1)
                if b == 0:
                    pe.wait_ge(turned_lo, j + 1)
                if name == "ple_gate" and b == FIRST[name]:
                    pe.wait_ge(turned_lo, (40 if only == 0 else 44) + j // 2 + 1)
                pe.wait_ge(lo_split, s + 1)
                for cc in range(2):
                    c = 2 * j + cc
                    wh = w_hi[:, s % RING, cc * NB:(cc + 1) * NB]
                    wl = w_lo[:, s % RING, cc * NB:(cc + 1) * NB]
                    if name in ("xbc", "peer_q"):
                        for m in range(4):
                            o = bank(2 * (b % 2) + m // 2)[:, (m % 2) * S:(m % 2 + 1) * S]
                            cut = slice(m * P, (m + 1) * P)
                            mm(o, wh[:, cut], act_hi[:, c, :], c == 0 and m % 2 == 0, False, True)
                            mm(o, wh[:, cut], act_lo[:, c, :], False, False, True)
                            ins = mm(o, wl[:, cut], act_hi[:, c, :], False, c == KC - 1, True)
                    else:
                        for t in range(TT) if only is None else (only,):
                            o, cut = bank(2 * (b % 2) + t), slice(t * P, (t + 1) * P)
                            mm(o, act_hi[:, c, cut], wh, c == 0, False)
                            mm(o, act_hi[:, c, cut], wl, False, False)
                            ins = mm(o, act_lo[:, c, cut], wh, False, c == KC - 1)
                if only != 0:
                    ins.then_inc(used, 1)

            def dt_products():
                pe.wait_ge(turned_lo, 8)
                pe.wait_ge(dt_lo, 1)
                o = bank(4)[0:64, 0:S]
                for c in range(KC):
                    w = slice(c * 64, (c + 1) * 64)
                    mm(o, w_hi[:, RING - 1, w], act_hi[:, c, :], c == 0, False)
                    mm(o, w_hi[:, RING - 1, w], act_lo[:, c, :], False, False)
                    ins = mm(o, w_lo[:, RING - 1, w], act_hi[:, c, :], False, c == KC - 1)
                ins.then_inc(dt_sum, 1)

            def turn_dt():
                pe.wait_ge(dt_out, 1)
                for t in range(TT):
                    ins = pe.transpose(bank(5)[:, t * 64:(t + 1) * 64], dt_rows[0:64, t * P:(t + 1) * P],
                                       ident[0:64, 0:64])
                ins.then_inc(dt_turned, 1)

            def beside_ssd(s):
                if s == 8:
                    pe.wait_ge(a_ready, 1)
                    for k, (m, t, r) in enumerate(((lower, 0, 1), (upper, 1, 0), (below, 0, 0), (above, 1, 1))):
                        ins = mm(bank(4)[:, 32 * k:32 * k + 32], m[:, :], av[:, t, 32 * r:32 * r + 32],
                                 True, True)
                    ins.then_inc(dec_sum, 1)
                for m in (2 * (s - XT_0), 2 * (s - XT_0) + 1):
                    if 0 <= m < 10:
                        if m == 0:
                            pe.wait_ge(silued, 6)
                            pe.wait_ge(dec_exp, 1)
                        if m >= 4:
                            pe.wait_ge(xt_out, m - 3)
                        t, q = m % 2, m // 2
                        for c in range(4):
                            ins = pe.transpose(bank(4 + m % 4)[:, c * P:(c + 1) * P],
                                               xbc[:, 4 * q + c, t * P:(t + 1) * P], ident[:, :])
                        ins.then_inc(xt_turned, 1)
                n, at = ssd_step(s)
                if not 0 <= n < 8:
                    return
                g, c = n // TT, n % TT
                if at in (0, 4):
                    r = at // 4
                    pe.wait_ge(rh_ready, 2 * n + r + 1)
                    if n or r:
                        pe.wait_ge(seg_exp, 2 * n + r)
                    else:
                        pe.wait_ge(xt_out, 10)
                    for q in range(2):
                        ins = mm(bank(4 + q), (below, above)[r][:, :],
                                 rh[:, r, 4 * q:4 * q + 4, :].rearrange("p h l -> p (h l)"), True, True)
                    ins.then_inc(seg_sum, 1)
                if at == 2:
                    if n:
                        pe.wait_ge(y_done, n)
                    mm(bank(7)[:, 0:P], xbc[:, 16 + g, c * P:(c + 1) * P],
                       xbc[:, 20 + g, c * P:(c + 1) * P], True, True).then_inc(cb_sum, 1)
                if at == 5:
                    pe.wait_ge(cb_out, n + 1)
                    pe.wait_ge(xd_ready, n + 1)
                    mm(bank(7), bt[:, 1 - c, g * P:(g + 1) * P], xd[:, 1 - c, :], True, True)\
                        .then_inc(state_sum, 1)
                if at == 9:
                    pe.wait_ge(em_ready, 2 * n + 2)
                    pe.wait_ge(xf_ready, 2 * n + 2)
                    for h in range(HPG):
                        for r in range(2):
                            mm(bank(6)[:, h * SSD_DIM:(h + 1) * SSD_DIM], em[:, r, h, :],
                               xf[:, r, h * SSD_DIM:(h + 1) * SSD_DIM], r == 0, r == 1)
                    pe.wait_ge(state_out, n + 1)
                    mm(bank(7), xbc[:, 20 + g, c * P:(c + 1) * P], hs, True, True).then_inc(y_sum, 1)

            def turn_qk(h):
                if h == 0:
                    pe.wait_ge(roped, 16)
                    pe.wait_ge(y_done, 8)
                if h == 1:
                    pe.wait_ge(qk_out, 1)
                if h >= 2:
                    pe.wait_ge(qk_out, h)
                if h >= 3:
                    pe.wait_ge(att_out, h - 2)
                for w in range(2):
                    for t in range(TT):
                        ins = pe.transpose(bank(4)[:, w * S + t * P:w * S + (t + 1) * P],
                                           head_cols(w, t, h), ident[:, :])
                ins.then_inc(qk_turned, 1)

            def scores(h):
                pe.wait_ge(qk_out, h + 1)
                if h:
                    pe.wait_ge(expd, h)
                for j in range(2):
                    rows_j = slice(ATT_DIM * j, ATT_DIM * (j + 1))
                    for t in range(TT):
                        ins = mm(bank(5 + j)[:, t * S:(t + 1) * S],
                                 qkt[rows_j, h % 2, t * P:(t + 1) * P], qkt[rows_j, h % 2, S:2 * S], True, True)
                ins.then_inc(scored, 1)

            def turn_att(h):
                pe.wait_ge(att_ready, h + 1)
                pe.wait_ge(qk_out, min(h + 3, ATT_HEADS))
                for t in range(TT):
                    for kc in range(2):
                        ins = pe.transpose(bank(4)[:, kc * S + t * P:kc * S + (t + 1) * P],
                                           att[:, h % 2, t, kc * P:(kc + 1) * P], ident[:, :])
                ins.then_inc(att_turned, 1)

            def times_v(h):
                pe.wait_ge(att_out, h + 1)
                if h:
                    pe.wait_ge(o_done, h)
                for t in range(TT):
                    for kc in range(2):
                        ins = mm(bank(7)[:, t * P:(t + 1) * P],
                                 att_t[:, h % 2, kc * S + t * P:kc * S + (t + 1) * P],
                                 head_cols(2, kc, h), kc == 0, kc == 1)
                ins.then_inc(o_sum, 1)

            def beside_att(s):
                if s == ATT_0 - 3:
                    turn_qk(0)
                if s == ATT_0 - 1:
                    turn_qk(1)
                h, at = att_step(s)
                if 0 <= h < 16 and at == 0:
                    scores(h)
                if 1 <= h < 17 and at == 1:
                    turn_att(h - 1)
                if 1 <= h < 17 and at == 3:
                    times_v(h - 1)
                if 0 <= h < 14 and at == 3:
                    turn_qk(h + 2)

            def key_products(b):
                pe.wait_ge(keys_in, 16)
                pe.wait_ge(banks_free, 4 + 2 * (FIRST["peer_q"] + b + 1))
                if b == 0:
                    pe.wait_ge(turned_lo, 40)
                if b >= 2:
                    pe.wait_ge(key_out, 2 * b - 2)
                for t in range(TT):
                    for n in range(4):
                        ins = mm(bank(4 + 2 * (b % 2) + t)[:, n * NKEYS:(n + 1) * NKEYS],
                                 pq[:, b % 2, n, t * P:(t + 1) * P], keys_sb[:, 4 * b + n, :], True, True)
                ins.then_inc(key_sum, 1)

            pe.wait_ge(masks, 6)
            for m in range(4):
                turn(0, m)
            for s in range(8 * FIRST["ple_gate"]):
                products(s)
                if s < 2:
                    turn(0, 4 + 2 * s)
                    turn(0, 5 + 2 * s)
                if s == 1:
                    dt_products()
                if s == 2:
                    turn_dt()
                if s < ATT_0 - 3:
                    beside_ssd(s)
                else:
                    beside_att(s)
                due = turn_step(s, 0)
                if due:
                    turn(*due)
                name, b, parity = read_out(s, 3)
                if name == "peer_q":
                    key_products(b)

            key_products(3)

            def ple_products():
                pe.wait_ge(ple_in, 32)
                pe.wait_ge(key_out, 8)
                for b in range(D // NB):
                    if b >= 2:
                        pe.wait_ge(ple_out, b - 1)
                    for t in range(TT):
                        for c in range(2):
                            ins = mm(bank(2 * (b % 2) + t), pt_sb[:, c, t * P:(t + 1) * P],
                                     up_sb[:, b, c, :], c == 0, c == 1)
                    ins.then_inc(ple_sum, 1)

            for t in range(TT):
                pe.wait_ge(row_free, SLOTS + 2 * (t + 1) * PICKS)
                for m in range(4):
                    if t and m == 0:
                        pe.wait_ge(own_act, 4)
                    elif m == 0:
                        pe.wait_ge(key_out, 8)
                    for c in range(4):
                        ins = pe.transpose(bank(4 + m)[:, c * P:(c + 1) * P], source(5, t, 4 * m + c),
                                           ident[:, :])
                    ins.then_inc(turned, 1)
                if t == 0:
                    ple_products()
                    pe.wait_ge(ple_out, 4)
                for s in range(8 * FIRST["ple_gate"], 8 * FIRST["ple_gate"] + RING):
                    products(s, t)
            for s in range(8 * FIRST["ple_gate"] + RING, PIECES):
                products(s)


def _columns(m, nblocks):
    return m.reshape(8, 2, P, nblocks, NB).transpose(3, 0, 2, 1, 4).reshape(nblocks * 8, P, PIECE)


def kernel(**inputs):
    import concourse.bacc as bacc
    from concourse.bass_utils import run_bass_kernel_spmd

    a = {k: np.asarray(v) for k, v in inputs.items()}
    w_in = a["w_in"][0]
    at = np.cumsum([0, D, XBC * P, 2 * SSD_HEADS, D, D, D, 2 * D])
    z, xbc, dt, q, k, v, gates = (w_in[:, at[n]:at[n + 1]] for n in range(7))
    parts = {"xbc": xbc, "z": z, "q": q, "k": k, "v": v, "gates": gates,
             "ssd_out": a["w_ssd_br"][0], "att_out": a["w_att_br"][0], "w_out": a["w_out"][0],
             "peer_q": a["peer_wq"][0], "ple_gate": a["ple_gate_w"][0]}
    wall = np.concatenate([_columns(parts[name], n) for name, n in STAGES])

    def chunks(g):
        return g.reshape(-1, P).T

    cols = np.concatenate([
        chunks(a["norm1_g"][0]), chunks(a["ssd_norm_g"][0]), chunks(a["norm2_g"][0]),
        chunks(a["norm3_g"][0]),
        a["subln_g"][0].reshape(P, 1),
        a["conv_w"][0].reshape(CONV_K, XBC, P).transpose(2, 1, 0).reshape(P, XBC * CONV_K),
        chunks(a["conv_b"][0])], axis=1)
    inv = (10000.0 ** (-np.arange(0, ATT_DIM, 2, dtype=np.float64) / ATT_DIM)).astype(np.float32)
    rows = np.concatenate([
        a["dt_bias_f"][0], a["dt_bias_b"][0], a["a_log_f"][0], a["a_log_b"][0], a["d_skip"][0],
        a["q_norm_g"][0], a["k_norm_g"][0], a["lam_q1"][0], a["lam_q2"][0], a["lam_k1"][0],
        a["lam_k2"][0], inv]).reshape(1, ROWS)
    arrays = {
        "x": a["x"].reshape(TT, P, D),
        "wall": wall,
        "wdt": dt.reshape(KC, P, 64).transpose(1, 0, 2).reshape(P, KC * 64),
        "cols": cols,
        "rows": rows,
        "pos": a["positions"].reshape(TT, P).T,
        "g2": a["norm2_g"].reshape(1, D),
        "keys_t": a["peer_keys"][0].transpose(3, 0, 1, 2).reshape(P, KC * NKEYS),
        "peer_u": a["peer_u"][0],
        "peer_v": a["peer_v"][0],
        "p_t": a["p"][0, 0].reshape(S, 2, P).transpose(2, 1, 0).reshape(P, 2 * S),
        "ple_up": a["ple_up_w"][0].reshape(2, P, 4, NB).transpose(1, 2, 0, 3).reshape(P, 2 * D),
    }
    arrays = {n: np.ascontiguousarray(v) for n, v in arrays.items()}
    nc = bacc.Bacc("TRN2", target_bir_lowering=False, num_devices=1)
    args = [nc.dram_tensor(n, v.shape, mybir.dt.from_np(v.dtype), kind="ExternalInput").ap()
            for n, v in arrays.items()]
    out = nc.dram_tensor("out", (TT, P, D), F32, kind="ExternalOutput").ap()
    build(nc, *args, out)
    r = run_bass_kernel_spmd(nc, [arrays], core_ids=[0])
    return r.results[0]["out"].reshape(1, S, D)
```
